# Optimizing a Trainium2 kernel written in Bass

```python
import jax, jax.numpy as jnp
from jax import lax
import numpy as np
import math

D_MODEL = 2048
BATCH = 1
SEQ = 256
DEPTH = 1

POOL_WIDTH = D_MODEL // 2
POOL_WINDOWS = (2, 4, 8, 16)
POOL_GROUP = POOL_WIDTH // len(POOL_WINDOWS)
LRU_WIDTH = D_MODEL // 2
LRU_HEADS = 8
LRU_HEAD_DIM = LRU_WIDTH // LRU_HEADS
CONV_WIDTH = 4
LRU_C = 8.0
MIX_WIDTH = POOL_WIDTH + LRU_WIDTH
IN_PROJ_WIDTH = POOL_WIDTH + 2 * LRU_WIDTH
PEER_HEADS = 8
PEER_N_KEYS = 128
PEER_N_EXPERTS = PEER_N_KEYS * PEER_N_KEYS
PEER_D_KEY = 256
PEER_HALF = PEER_D_KEY // 2
PEER_TOPK = 16
PEER_CHUNK = 128
EPS = 1e-6


def rmsnorm(x, g):
    xf = x.astype(jnp.float32)
    y = xf * lax.rsqrt(jnp.mean(xf * xf, axis=-1, keepdims=True) + EPS)
    return (y * g.astype(jnp.float32)).astype(x.dtype)

def pool_mixer(u, pool_w, pool_b, pool_scale):
    B, S, _ = u.shape
    uf = u.astype(jnp.float32).reshape(B, S, len(POOL_WINDOWS), POOL_GROUP)
    csum = jnp.cumsum(uf, axis=1)
    pos = jnp.arange(1, S + 1, dtype=jnp.float32)[None, :, None]
    outs = []
    for g, w in enumerate(POOL_WINDOWS):
        c = csum[:, :, g]
        c_prev = jnp.pad(c, ((0, 0), (w, 0), (0, 0)))[:, :S]
        mean = (c - c_prev) / jnp.minimum(pos, float(w))
        outs.append(mean - uf[:, :, g])
    d = jnp.stack(outs, axis=2).astype(u.dtype)
    y = jnp.einsum('bsgi,gij->bsgj', d, pool_w) + pool_b
    return y.reshape(B, S, POOL_WIDTH) * pool_scale

def _lru_combine(left, right):
    a1, b1 = left
    a2, b2 = right
    return a1 * a2, a2 * b1 + b2

def rg_lru_mixer(xb, gate, conv_w, conv_b, gate_a_w, gate_a_b, gate_x_w, gate_x_b, lru_lambda):
    B, S, _ = xb.shape
    xp = jnp.pad(xb, ((0, 0), (CONV_WIDTH - 1, 0), (0, 0)))
    xc = conv_b + xp[:, 0:S] * conv_w[0]
    for k in range(1, CONV_WIDTH):
        xc = xc + xp[:, k:k + S] * conv_w[k]
    xh = xc.reshape(B, S, LRU_HEADS, LRU_HEAD_DIM)
    r = jax.nn.sigmoid(jnp.einsum('bshi,hij->bshj', xh, gate_a_w) + gate_a_b).reshape(B, S, LRU_WIDTH)
    i = jax.nn.sigmoid(jnp.einsum('bshi,hij->bshj', xh, gate_x_w) + gate_x_b).reshape(B, S, LRU_WIDTH)
    log_a = (LRU_C * r.astype(jnp.float32)) * jax.nn.log_sigmoid(lru_lambda.astype(jnp.float32))
    a = jnp.exp(log_a)
    mult = jnp.sqrt(-jnp.expm1(2.0 * log_a))
    b = mult * (i * xc).astype(jnp.float32)
    _, h = lax.associative_scan(_lru_combine, (a, b), axis=1)
    return h.astype(xb.dtype) * jax.nn.gelu(gate)

def peer_ffn(z, peer_wq, keys1, keys2, peer_u, peer_v):
    B, S, D = z.shape
    zt = z.reshape(-1, PEER_CHUNK, D)
    k1 = keys1.astype(jnp.float32)
    k2 = keys2.astype(jnp.float32)

    def chunk(zc):
        q = (zc @ peer_wq).astype(jnp.float32).reshape(PEER_CHUNK, PEER_HEADS, 2, PEER_HALF)
        s1 = jnp.einsum('chd,hkd->chk', q[:, :, 0], k1)
        s2 = jnp.einsum('chd,hkd->chk', q[:, :, 1], k2)
        v1, i1 = lax.top_k(s1, PEER_TOPK)
        v2, i2 = lax.top_k(s2, PEER_TOPK)
        cand = (v1[..., :, None] + v2[..., None, :]).reshape(PEER_CHUNK, PEER_HEADS, PEER_TOPK * PEER_TOPK)
        cand_idx = (i1[..., :, None] * PEER_N_KEYS + i2[..., None, :]).reshape(PEER_CHUNK, PEER_HEADS, PEER_TOPK * PEER_TOPK)
        top_s, top_pos = lax.top_k(cand, PEER_TOPK)
        expert = jnp.take_along_axis(cand_idx, top_pos, axis=-1)
        gate = jax.nn.softmax(top_s, axis=-1)
        u = jnp.take(peer_u, expert, axis=0)
        act = jax.nn.gelu(jnp.einsum('chkd,cd->chk', u, zc))
        v = jnp.take(peer_v, expert, axis=0)
        w = (gate * act.astype(jnp.float32)).astype(zc.dtype)
        return jnp.einsum('chk,chkd->cd', w, v).astype(zc.dtype)

    return lax.map(chunk, zt).reshape(B, S, D)

def first_inputs(seed: int = 0) -> dict:
    key = jax.random.key(seed)
    ks = jax.random.split(key, 24)
    L = DEPTH
    f32 = jnp.float32

    def nrm(k, shape, scale):
        return jax.random.normal(k, shape, f32) * scale

    a0 = jax.random.uniform(ks[12], (L, LRU_WIDTH), f32, 0.9, 0.999) ** (1.0 / LRU_C)
    lru_lambda = jnp.log(a0) - jnp.log1p(-a0)
    return {
        "x": nrm(ks[0], (BATCH, SEQ, D_MODEL), 1.0),
        "norm1_g": 1.0 + nrm(ks[1], (L, D_MODEL), 0.02),
        "w_in": nrm(ks[2], (L, D_MODEL, IN_PROJ_WIDTH), D_MODEL ** -0.5),
        "pool_w": nrm(ks[3], (L, len(POOL_WINDOWS), POOL_GROUP, POOL_GROUP), POOL_GROUP ** -0.5),
        "pool_b": nrm(ks[4], (L, len(POOL_WINDOWS), POOL_GROUP), 0.01),
        "pool_scale": 1.0 + nrm(ks[5], (L, POOL_WIDTH), 0.02),
        "conv_w": nrm(ks[6], (L, CONV_WIDTH, LRU_WIDTH), CONV_WIDTH ** -0.5),
        "conv_b": nrm(ks[7], (L, LRU_WIDTH), 0.01),
        "gate_a_w": nrm(ks[8], (L, LRU_HEADS, LRU_HEAD_DIM, LRU_HEAD_DIM), LRU_HEAD_DIM ** -0.5),
        "gate_a_b": nrm(ks[9], (L, LRU_HEADS, LRU_HEAD_DIM), 0.01),
        "gate_x_w": nrm(ks[10], (L, LRU_HEADS, LRU_HEAD_DIM, LRU_HEAD_DIM), LRU_HEAD_DIM ** -0.5),
        "gate_x_b": nrm(ks[11], (L, LRU_HEADS, LRU_HEAD_DIM), 0.01),
        "lru_lambda": lru_lambda,
        "w_out": nrm(ks[13], (L, MIX_WIDTH, D_MODEL), MIX_WIDTH ** -0.5),
        "norm2_g": 1.0 + nrm(ks[14], (L, D_MODEL), 0.02),
        "peer_wq": nrm(ks[15], (L, D_MODEL, PEER_HEADS * PEER_D_KEY), D_MODEL ** -0.5),
        "peer_keys1": nrm(ks[16], (L, PEER_HEADS, PEER_N_KEYS, PEER_HALF), PEER_HALF ** -0.5),
        "peer_keys2": nrm(ks[17], (L, PEER_HEADS, PEER_N_KEYS, PEER_HALF), PEER_HALF ** -0.5),
        "peer_u": nrm(ks[18], (L, PEER_N_EXPERTS, D_MODEL), D_MODEL ** -0.5),
        "peer_v": nrm(ks[19], (L, PEER_N_EXPERTS, D_MODEL), PEER_HEADS ** -0.5),
        "norm_f_g": 1.0 + nrm(ks[20], (D_MODEL,), 0.02),
    }

def first_block(x, norm1_g, w_in, pool_w, pool_b, pool_scale, conv_w, conv_b, gate_a_w, gate_a_b,
              gate_x_w, gate_x_b, lru_lambda, w_out, norm2_g, peer_wq, peer_keys1, peer_keys2,
              peer_u, peer_v, norm_f_g):
    h = x
    for l in range(DEPTH):
        z = rmsnorm(h, norm1_g[l])
        proj = z @ w_in[l]
        u_pool = proj[..., :POOL_WIDTH]
        x_lru = proj[..., POOL_WIDTH:POOL_WIDTH + LRU_WIDTH]
        g_lru = proj[..., POOL_WIDTH + LRU_WIDTH:]
        y_pool = pool_mixer(u_pool, pool_w[l], pool_b[l], pool_scale[l])
        y_lru = rg_lru_mixer(x_lru, g_lru, conv_w[l], conv_b[l], gate_a_w[l], gate_a_b[l],
                             gate_x_w[l], gate_x_b[l], lru_lambda[l])
        y = jnp.concatenate([y_pool, y_lru], axis=-1)
        h = h + y @ w_out[l]
        h = h + peer_ffn(rmsnorm(h, norm2_g[l]), peer_wq[l], peer_keys1[l], peer_keys2[l],
                         peer_u[l], peer_v[l])
    return rmsnorm(h, norm_f_g)


CHUNK = 64
Q_BLOCK = 128
SB_HEADS = 8
SB_HEAD_DIM = 128
D_SB = SB_HEADS * SB_HEAD_DIM
D_CONV = D_MODEL // 2
CONV_WIDTH_2 = 31
D_FF = 4 * D_MODEL
IN_SPLITS = (D_SB, D_SB, D_SB, D_CONV, D_CONV, D_MODEL, D_MODEL)
D_IN = sum(IN_SPLITS)


def rmsnorm_2(x, g):
    xf = x.astype(jnp.float32)
    y = xf * lax.rsqrt(jnp.mean(xf * xf, axis=-1, keepdims=True) + EPS)
    return (y * g.astype(jnp.float32)).astype(x.dtype)

def layernorm(x, g, b):
    xf = x.astype(jnp.float32)
    mu = jnp.mean(xf, axis=-1, keepdims=True)
    var = jnp.mean(jnp.square(xf - mu), axis=-1, keepdims=True)
    y = (xf - mu) * lax.rsqrt(var + EPS)
    return (y * g.astype(jnp.float32) + b.astype(jnp.float32)).astype(x.dtype)

def stick_breaking_attention(q, k, v):
    b, s, h, dh = q.shape
    scale = 1.0 / math.sqrt(dh)
    outs = []
    for i in range(s // Q_BLOCK):
        t0, t1 = i * Q_BLOCK, (i + 1) * Q_BLOCK
        qb = q[:, t0:t1]
        kb = k[:, :t1]
        vb = v[:, :t1]
        z = jnp.einsum('bqhd,bkhd->bhqk', qb, kb).astype(jnp.float32) * scale
        tq = t0 + jnp.arange(Q_BLOCK)[:, None]
        sk = jnp.arange(t1)[None, :]
        mask = sk < tq
        log_1m = jnp.where(mask, jax.nn.log_sigmoid(-z), 0.0)
        suffix = lax.cumsum(log_1m, axis=3, reverse=True) - log_1m
        a = jnp.where(mask, jnp.exp(jax.nn.log_sigmoid(z) + suffix), 0.0)
        outs.append(jnp.einsum('bhqk,bkhd->bqhd', a.astype(vb.dtype), vb))
    return jnp.concatenate(outs, axis=1)

def causal_depthwise_conv(u, w, bias):
    c = u.shape[-1]
    y = lax.conv_general_dilated(
        u, w.reshape(CONV_WIDTH_2, 1, c).astype(u.dtype),
        window_strides=(1,), padding=[(CONV_WIDTH_2 - 1, 0)],
        dimension_numbers=('NWC', 'WIO', 'NWC'), feature_group_count=c)
    return y + bias

def second_inputs(seed: int = 0) -> dict:
    key = jax.random.key(seed)
    ks = jax.random.split(key, 17)
    L = DEPTH
    nrm = lambda k, shape, fan_in: jax.random.normal(k, shape, jnp.float32) * (fan_in ** -0.5)
    gain = lambda k, shape: 1.0 + 0.02 * jax.random.normal(k, shape, jnp.float32)
    small = lambda k, shape: 0.02 * jax.random.normal(k, shape, jnp.float32)
    return {
        "x": jax.random.normal(ks[0], (BATCH, SEQ, D_MODEL), jnp.float32),
        "g_pre_mix": gain(ks[1], (L, D_MODEL)),
        "w_in": nrm(ks[2], (L, D_MODEL, D_IN), D_MODEL),
        "b_in": small(ks[3], (L, D_IN)),
        "w_dw": nrm(ks[4], (L, CONV_WIDTH_2, D_CONV), CONV_WIDTH_2),
        "b_dw": small(ks[5], (L, D_CONV)),
        "g_conv_ln": gain(ks[6], (L, D_CONV)),
        "b_conv_ln": small(ks[7], (L, D_CONV)),
        "w_sb_out": nrm(ks[8], (L, D_SB, D_MODEL), D_SB),
        "w_conv_out": nrm(ks[9], (L, D_CONV, D_MODEL), D_CONV),
        "w_o": nrm(ks[10], (L, D_MODEL, D_MODEL), D_MODEL),
        "g_post_mix": gain(ks[11], (L, D_MODEL)),
        "g_pre_mlp": gain(ks[12], (L, D_MODEL)),
        "w_up": nrm(ks[13], (L, D_MODEL, D_FF), D_MODEL),
        "w_down": nrm(ks[14], (L, D_FF, D_MODEL), D_FF),
        "g_post_mlp": gain(ks[15], (L, D_MODEL)),
    }

def second_block(x, g_pre_mix, w_in, b_in, w_dw, b_dw, g_conv_ln, b_conv_ln,
              w_sb_out, w_conv_out, w_o, g_post_mix, g_pre_mlp, w_up, w_down,
              g_post_mlp):
    b, s, _ = x.shape
    offs = np.cumsum(IN_SPLITS)[:-1].tolist()
    for l in range(DEPTH):
        h = rmsnorm_2(x, g_pre_mix[l])
        proj = jnp.einsum('bsd,de->bse', h, w_in[l]) + b_in[l]
        q, k, v, glu_a, glu_b, gate_sb, gate_cv = jnp.split(proj, offs, axis=-1)
        hd = (b, s, SB_HEADS, SB_HEAD_DIM)
        o_sb = stick_breaking_attention(q.reshape(hd), k.reshape(hd), v.reshape(hd))
        o_sb = jnp.einsum('bse,ed->bsd', o_sb.reshape(b, s, D_SB), w_sb_out[l])
        u = glu_a * jax.nn.sigmoid(glu_b)
        u = causal_depthwise_conv(u, w_dw[l], b_dw[l])
        u = jax.nn.silu(layernorm(u, g_conv_ln[l], b_conv_ln[l]))
        o_cv = jnp.einsum('bsc,cd->bsd', u, w_conv_out[l])
        merged = jax.nn.sigmoid(gate_sb) * o_sb + jax.nn.sigmoid(gate_cv) * o_cv
        y = jnp.einsum('bsd,de->bse', merged, w_o[l])
        x = x + rmsnorm_2(y, g_post_mix[l])
        h = rmsnorm_2(x, g_pre_mlp[l])
        f = jnp.square(jax.nn.relu(jnp.einsum('bsd,df->bsf', h, w_up[l])))
        f = jnp.einsum('bsf,fd->bsd', f, w_down[l])
        x = x + rmsnorm_2(f, g_post_mlp[l])
    return x


def setup_inputs(seed=0):
    out = dict(first_inputs(seed))
    for name, value in second_inputs(seed + 1).items():
        if name != "x":
            out[name + "_2"] = value
    return out


def reference(
    x, norm1_g, w_in, pool_w, pool_b, pool_scale, conv_w, conv_b, gate_a_w, gate_a_b, gate_x_w,
    gate_x_b, lru_lambda, w_out, norm2_g, peer_wq, peer_keys1, peer_keys2, peer_u, peer_v,
    norm_f_g, g_pre_mix_2, w_in_2, b_in_2, w_dw_2, b_dw_2, g_conv_ln_2, b_conv_ln_2, w_sb_out_2,
    w_conv_out_2, w_o_2, g_post_mix_2, g_pre_mlp_2, w_up_2, w_down_2, g_post_mlp_2,
):
    x = first_block(
        x, norm1_g, w_in, pool_w, pool_b, pool_scale, conv_w, conv_b, gate_a_w, gate_a_b,
        gate_x_w, gate_x_b, lru_lambda, w_out, norm2_g, peer_wq, peer_keys1, peer_keys2, peer_u,
        peer_v, norm_f_g,
    )
    return second_block(
        x, g_pre_mix_2, w_in_2, b_in_2, w_dw_2, b_dw_2, g_conv_ln_2, b_conv_ln_2, w_sb_out_2,
        w_conv_out_2, w_o_2, g_post_mix_2, g_pre_mlp_2, w_up_2, w_down_2, g_post_mlp_2,
    )


_drawn_inputs = setup_inputs


def setup_inputs(seed=0):
    import zlib

    import numpy as np

    out = dict(_drawn_inputs(seed))
    spreads = {}
    factors = {'pool_b': 3.428,
     'gate_a_b': 22.026,
     'gate_x_b': 21.4,
     'g_pre_mix_2': 3.081,
     'g_conv_ln_2': 46.533,
     'b_conv_ln_2': 44.447,
     'g_post_mix_2': 10.321,
     'g_pre_mlp_2': 32.573,
     'g_post_mlp_2': 62.31,
     'b_in_2': 4.02,
     'b_dw_2': 5.443}
    for name, (base, spread) in spreads.items():
        noise = np.random.default_rng([zlib.crc32(name.encode()), seed]).standard_normal(out[name].shape)
        drawn = base * np.exp(spread * noise) if base else spread * noise
        out[name] = __import__('jax').numpy.asarray(drawn.astype(out[name].dtype))
    for name, factor in factors.items():
        out[name] = (out[name] * factor).astype(out[name].dtype)
    return out
```

```python
from contextlib import ExitStack

import concourse.bass as bass
from concourse import mybir
from concourse.alu_op_type import AluOpType as ALU

F32 = mybir.dt.float32
F32R = mybir.dt.float32r
U32 = mybir.dt.uint32
ACT = mybir.ActivationFunctionType
AX = mybir.AxisListType

T = 256
NRAW = 3
NW = 5
HALF = 8 * 128
TAPS = 31

COLS = [("g1", 16), ("pool_b", 8), ("pool_scale", 8), ("conv_w", 32), ("conv_b", 8), ("gab", 8), ("gxb", 8),
        ("lam", 8), ("g2", 16), ("gf", 16), ("gpm", 16), ("b_in", 72), ("w_dw", 8 * TAPS), ("b_dw", 8),
        ("gcl", 8), ("bcl", 8), ("gpost", 16), ("gpmlp", 16), ("gpostmlp", 16), ("eps", 1)]
COL0 = {}
NCOL = 0
for _n, _c in COLS:
    COL0[_n] = NCOL
    NCOL += _c

CI, CTRI, CONE, CIOTA, CRC, CEND = 0, 128, 256, 384, 512, 576


class Engine:

    def __init__(self, sem):
        self.sem, self.n, self.ops, self.waited = sem, 0, [], {}

    def wait(self, *tokens):
        for sem, value in tokens:
            if self.waited.get(sem.name, 0) < value:
                self.waited[sem.name] = value
                self.ops.append(lambda e, sem=sem, value=value: e.wait_ge(sem, value))

    def __call__(self, fn, *tokens):
        self.wait(*tokens)
        self.n += 1
        sem = self.sem
        self.ops.append(lambda e: fn(e).then_inc(sem, 1))
        return (self.sem, self.n)

    def dma(self, fn, sem, count, *tokens):
        self.wait(*tokens)
        self.ops.append(lambda e: fn(e).then_inc(sem, 16))
        return (sem, 16 * count)

    def run(self, e):
        for op in self.ops:
            op(e)


class Ring:

    def __init__(self, bufs):
        self.bufs, self.free, self.at = bufs, [[] for _ in bufs], -1

    def next(self):
        self.at = (self.at + 1) % len(self.bufs)
        return self.at


def build(nc, ins, out):
    ctx = ExitStack()
    with ctx:
        def sb(name, shape, dt=F32):
            return ctx.enter_context(nc.sbuf_tensor(name, shape, dt))

        def sem(name):
            return ctx.enter_context(nc.semaphore(name))

        def region(nbytes, name, *layouts):
            out = {}
            for layout in layouts:
                with ExitStack() as c:
                    for n, shape, dt in layout:
                        out[n] = c.enter_context(nc.sbuf_tensor(n, shape, dt))
            sb(name, [128, nbytes // 4])
            return out

        raw = [sb(f"raw{i}", [128, HALF]) for i in range(NRAW)]
        hi = [sb(f"hi{i}", [128, 8, 128], F32R) for i in range(NW)]
        lo = [sb(f"lo{i}", [128, 8, 128], F32R) for i in range(NW)]
        ZA = sb("ZA", [128, 16, 512], F32R)
        X = sb("X", [128, 16, T])
        zb = region(32768, "zb_mem",
                    [("ZB", [128, 16, 512], F32R)],
                    [("zb_pad0", [128, 16, T], F32), ("S1", [128, 8, T], F32), ("W1", [128, 8, T], F32)],
                    [("stage0", [128, 8, 16, 16], F32), ("stage1", [128, 8, 16, 16], F32),
                     ("oneA", [128, 4, 128], F32), ("oneB", [128, 4, 128], F32),
                     ("IJG", [128, 3, T], F32), ("TS", [128, 2, 128], F32), ("TP", [128, 2, 128], U32),
                     ("sel", [128, 3, 2, 128], F32), ("sm", [128, 4, 16], F32)],
                    [("qkv", [128, 4, 3, T], F32), ("VT", [128, 4, T], F32), ("zs0", [128, 2, 384], F32),
                     ("zs1", [128, 2, 384], F32), ("sp0", [128, 2, 384], F32), ("sp1", [128, 2, 384], F32),
                     ("mask", [128, 384], F32), ("neg", [128, 384], F32)])
        ry = region(16384, "y_mem",
                    [("Y", [128, 16, T], F32)],
                    [("poolw", [128, 4, 2, 256], F32), ("gaw", [128, 8, 128], F32), ("gxw", [128, 8, 128], F32)],
                    [("y_pad1", [128, 8, T], F32), ("upa", [128, 2, 272], F32), ("upb", [128, 2, 272], F32)],
                    [("y_pad0", [128, 8, T], F32), ("keys", [128, 16, 128], F32)],
                    [("O", [128, 8, T], F32), ("CV", [128, 8, T], F32)])
        rr = region(39 * 1024, "rr_mem",
                    [("XC", [128, 8, T], F32), ("rg", [128, 8, T], F32), ("ig", [128, 8, T], F32),
                     ("gl", [128, 8, T], F32), ("XL0", [128, 260], F32), ("XL1", [128, 260], F32),
                     ("UP0", [128, 2, 272], F32), ("UP1", [128, 2, 272], F32)],
                    [("rr_pad0", [128, 8, T], F32), ("sqx", [128, 16, T], F32)],
                    [("A1", [128, 16, T], F32), ("Gc", [128, T, 16], F32)],
                    [("rr_pad1", [128, 16, T], F32), ("eq", [128, 8, 16, 16], F32), ("Vk", [128, 2, 8, 2, 16], F32),
                     ("Ik", [128, 2, 8, 2, 16], U32), ("If", [128, 2, 8, 2, 16], F32),
                     ("mr0", [128, 256], F32), ("mr1", [128, 256], F32)],
                    [("rr_pad2", [128, 16, T], F32), ("rr_pad3", [128, 16, T], F32),
                     ("cd0", [128, 16, 16], F32), ("cd1", [128, 16, 16], F32), ("tpa", [128, 2, 128], U32),
                     ("tpf", [128, 2, 128], F32)],
                    [("SGS", [128, 16, T], F32), ("SGC", [128, 16, T], F32),
                     ("UC0", [128, 288], F32), ("UC1", [128, 288], F32), ("UC2", [128, 288], F32),
                     ("UC3", [128, 288], F32), ("UC4", [128, 288], F32)])
        con = sb("con", [128, CEND])
        col = sb("col", [128, NCOL])
        UP = [rr["UP0"], rr["UP1"]]
        upa, upb = ry["upa"], ry["upb"]
        sp4 = sb("sp4", [128, 3, 8])
        gfm = sb("gfm", [128, 16])
        Rn = [sb(f"R{i}", [128, T]) for i in range(3)]
        acc = [sb(f"acc{i}", [128, T]) for i in range(2)]
        tA = Ring([sb(f"tA{i}", [128, T]) for i in range(3)])
        tS = Ring([sb(f"tS{i}", [128, T]) for i in range(4)])
        tQ = Ring([sb(f"tQ{i}", [128, T]) for i in range(2)])
        GB = Ring([ctx.enter_context(nc.psum_tensor(f"G{i}", [128, 512], F32)) for i in range(4)])
        MB = Ring([ctx.enter_context(nc.psum_tensor(f"M{i}", [128, 512], F32)) for i in range(4)])
        scr = nc.dram_tensor("g_scratch", [8, 128, T * 16], F32, kind="Internal").ap()
        ident, tri, ones, iota = (con[:, c:c + 128] for c in (CI, CTRI, CONE, CIOTA))
        iota16 = con[:, CIOTA:CIOTA + 16]
        ZB, Y = zb["ZB"], ry["Y"]

        def C(name, i=0):
            return col[:, COL0[name] + i:COL0[name] + i + 1]

        PE, A, D, P = (Engine(sem(n)) for n in ("s_pe", "s_act", "s_dve", "s_pool"))
        SP = Engine(sem("s_sp"))
        s_raw = [sem(f"s_raw{i}") for i in range(NRAW)]
        s_in = {n: sem(f"s_{n}") for n in ("con", "col", "mask", "poolw", "gaw", "gxw", "keys")}
        s_x = [sem(f"s_x{i}") for i in range(4)]
        s_st = [sem("s_st0"), sem("s_st1")]
        s_gc, s_out = sem("s_gc"), sem("s_out")

        def tt(o, a, b, op):
            return lambda e: e.tensor_tensor(o, a, b, op)

        def ts(o, a, s1, op0, s2=None, op1=None):
            if op1 is None:
                return lambda e: e.tensor_scalar(o, a, s1, None, op0)
            return lambda e: e.tensor_scalar(o, a, s1, s2, op0, op1)

        def stt(o, a, s, b, op0, op1):
            return lambda e: e.scalar_tensor_tensor(out=o, in0=a, scalar=s, in1=b, op0=op0, op1=op1)

        def act(o, i, f, **k):
            return lambda e: e.activation(o, i, f, **k)

        def mm(o, l, r, start, stop):
            return lambda e: e.matmul(o, l, r, start=start, stop=stop, skip_group_check=True)

        def many(*fns):
            def run(e):
                for f in fns:
                    last = f(e)
                return last
            return run

        ld = {}
        ld["con"] = A.dma(lambda e: e.dma_start(con[:, :], ins["con"][:, 0:CEND]), s_in["con"], 1)
        ld["col"] = A.dma(lambda e: e.dma_start(col[:, :], ins["cols"]), s_in["col"], 1)
        ldx = [A.dma(lambda e, i=i: e.dma_start(X[:, 4 * i:4 * i + 4, :], ins["xT"][:, 4 * i:4 * i + 4, :]), s_x[i], 1)
               for i in range(4)]
        ld["gaw"] = A.dma(lambda e: e.dma_start(ry["gaw"][:, :, :], ins["gaw"]), s_in["gaw"], 1)
        ld["gxw"] = A.dma(lambda e: e.dma_start(ry["gxw"][:, :, :], ins["gxw"]), s_in["gxw"], 1)
        ld["poolw"] = A.dma(lambda e: e.dma_start(ry["poolw"][:, :, :, :], ins["poolw"]), s_in["poolw"], 1)

        halves = []
        units = []

        def unit(hs, evac):
            a = len(halves)
            halves.extend(hs)
            units.append((a, len(halves), evac))

        def unit2(w, m, Z, evac, order=((0, range(8)), (1, range(8))), kbase=0):
            hs = []
            for n, (kh, kks) in enumerate(order):
                hs.append((w[m, kbase + kh], Z, kh, list(kks), 0, n == 0, n == 1))
            unit(hs, evac)

        ready_a, ready_b = [[] for _ in range(16)], [[] for _ in range(16)]
        mm_half = {}
        w_tok = {}

        def prep(h):
            if h >= len(halves):
                return
            r, w = h % NRAW, h % NW
            src = halves[h][0]
            ld_tok = SP.dma(lambda e: e.dma_start(raw[r][:, :], src), s_raw[r], h // NRAW + 1,
                            *(w_tok[h - NRAW] if h >= NRAW else []))
            free = [mm_half[h - NW]] if h >= NW else []
            rw = raw[r][:, :].rearrange("p (k n) -> p k n", k=8)
            a = A(act(hi[w][:, :, :], rw, ACT.Copy), ld_tok, *free)
            c = POOL_K
            toks = [a]
            if c < 8:
                toks.append(D(tt(lo[w][:, 0:8 - c, :], rw[:, 0:8 - c, :], hi[w][:, 0:8 - c, :].bitcast(F32), ALU.subtract), a))
            if c:
                toks.append(P(tt(lo[w][:, 8 - c:8, :], rw[:, 8 - c:8, :], hi[w][:, 8 - c:8, :].bitcast(F32), ALU.subtract), a))
            w_tok[h] = toks

        POOL_K = 2

        def products(u):
            a, b, _ = units[u]
            banks = {}
            for h in range(a, b):
                _, Z, kh, kks, bk, start, stop = halves[h]
                if bk not in banks:
                    banks[bk] = GB.next()
                g = banks[bk]
                G = GB.bufs[g]
                PE.wait(*w_tok[h])
                if start:
                    PE.wait(*GB.free[g])
                ready = ready_a if Z is ZA else ready_b
                w = h % NW
                for n, kk in enumerate(kks):
                    k = 8 * kh + kk
                    PE.wait(*ready[k])
                    f = many(mm(G[:, 0:512], hi[w][:, kk, :], Z[:, k, :], start and n == 0, False),
                             mm(G[:, 0:256], lo[w][:, kk, :], Z[:, k, 0:256], False, stop and n == 7))
                    if n < 7:
                        PE.ops.append(f)
                    else:
                        mm_half[h] = PE(f)
            return [(GB.bufs[banks[k]], banks[k], mm_half[b - 1]) for k in sorted(banks)]

        def low(bank, scale=None):
            G, g, tok = bank
            i = tA.next()
            k = {} if scale is None else {"scale": scale}
            return i, A(act(tA.bufs[i][:, :], G[:, 256:512], ACT.Copy, **k), tok, *tA.free[i])

        def join(bank, i, a, dst, *tokens):
            G, g, tok = bank
            d = D(tt(dst, G[:, 0:256], tA.bufs[i][:, :], ALU.add), a, *tokens)
            GB.free[g] = [d]
            tA.free[i] = [d]
            return d

        def join_s(bank, i, a):
            j = tS.next()
            return j, join(bank, i, a, tS.bufs[j][:, :], *tS.free[j])

        def split(Z, ready, k, src, scale, *tokens):
            if scale is None:
                a = A(act(Z[:, k, 0:256], src, ACT.Copy), *tokens)
                d = D(tt(Z[:, k, 256:512], src, Z[:, k, 0:256].bitcast(F32), ALU.subtract), a)
            else:
                a = A(act(Z[:, k, 0:256], src, ACT.Copy, scale=scale), *tokens)
                d = D(stt(Z[:, k, 256:512], src, scale, Z[:, k, 0:256].bitcast(F32), ALU.mult, ALU.subtract), a)
            ready[k] = [a, d]
            return d

        acc_free = [[], []]
        acc_tok = [None, None]

        def add_square(n, first, src, *tokens):
            if first:
                acc_tok[n] = P(tt(acc[n][:, :], src, src, ALU.mult), *tokens, *acc_free[n])
                return acc_tok[n]
            q = tQ.next()
            t = P(tt(tQ.bufs[q][:, :], src, src, ALU.mult), *tokens, *tQ.free[q])
            acc_tok[n] = P(tt(acc[n][:, :], acc[n][:, :], tQ.bufs[q][:, :], ALU.add), t, acc_tok[n])
            tQ.free[q] = [acc_tok[n]]
            return t

        def mean_of(src, *tokens):
            m = MB.next()
            t = PE(mm(MB.bufs[m][:, 0:256], ones, src, True, True), *tokens, *MB.free[m], ld["con"])
            return m, t

        def rstd(n, dst, count, *tokens):
            m, t = mean_of(acc[n][:, :], acc_tok[n])
            acc_free[n] = [t]
            a = A(act(dst, MB.bufs[m][:, 0:256], ACT.Sqrt, scale=1.0 / count, bias=C("eps")), t, *tokens)
            MB.free[m] = [a]
            return D(lambda e: e.reciprocal(dst, dst), a)

        pre, post = {}, {}

        def at(where, step, fn):
            where.setdefault(step, []).append(fn)

        R1, R2, R3 = Rn
        rtok = {}
        XC, rg, ig, gl, S1, W1 = (rr[n] if n in rr else zb[n] for n in ("XC", "rg", "ig", "gl", "S1", "W1"))
        XL = Ring([rr["XL0"], rr["XL1"]])
        UPr = Ring(UP)
        pad_tok = [P(lambda e, b=b: e.memset(b[:, 0:3], 0.0)) for b in (rr["XL0"], rr["XL1"])]
        upad = [P(lambda e, b=b: e.memset(b[:, :, 0:16], 0.0)) for b in UP]

        def start_x():
            for i in range(4):
                for k in range(4 * i, 4 * i + 4):
                    split(ZA, ready_a, k, X[:, k, :], C("g1", k), ldx[i], ld["col"])
                if i == 0:
                    prep(0)
                if i == 1:
                    prep(1)
                if i == 3:
                    prep(2)

        ini = {}

        def first_norm():
            rtok["R1"] = rstd(0, R1[:, :], 2048)
        at(post, 0, first_norm)

        sg_tok, xc_tok, gl_tok = {}, {}, {}

        def evac_lru_x(j):
            def ev(u, banks):
                i, a = low(banks[0])
                x = XL.next()
                b = XL.bufs[x]
                d = join(banks[0], i, a, b[:, 3:259], pad_tok[x], *XL.free[x])
                p = P(tt(b[:, 3:259], b[:, 3:259], R1[:, :], ALU.mult), d, rtok["R1"])
                yield
                c = D(ts(XC[:, j, :], b[:, 0:256], C("conv_w", j), ALU.mult, C("conv_b", j), ALU.add), p)
                for k in range(1, 4):
                    c = D(stt(XC[:, j, :], b[:, k:k + 256], C("conv_w", 8 * k + j), XC[:, j, :], ALU.mult, ALU.add), c)
                XL.free[x] = [c]
                xc_tok[j] = c

                def gates():
                    m = MB.next()
                    M = MB.bufs[m]
                    t = PE(many(mm(M[:, 0:256], ry["gaw"][:, j, :], XC[:, j, :], True, True),
                                mm(M[:, 256:512], ry["gxw"][:, j, :], XC[:, j, :], True, True)),
                           xc_tok[j], ld["gaw"], ld["gxw"], *MB.free[m])
                    a = A(act(rg[:, j, :], M[:, 0:256], ACT.Sigmoid, bias=C("gab", j)), t, ini['sqx'])
                    b = A(act(ig[:, j, :], M[:, 256:512], ACT.Sigmoid, bias=C("gxb", j)), t)
                    MB.free[m] = [b]
                    sg_tok[j] = b
                at(post, u + 1, gates)
            return ev

        def evac_gate(j):
            def ev(u, banks):
                i, a = low(banks[0])
                s, d = join_s(banks[0], i, a)
                b = tS.bufs[s]
                p = P(tt(b[:, :], b[:, :], R1[:, :], ALU.mult), d)
                yield
                yield
                gl_tok[j] = A(act(gl[:, j, :], b[:, :], ACT.Gelu_apprx_tanh), p)
                tS.free[s] = [gl_tok[j]]
            return ev

        def evac_pool(g, mi):
            def ev(u, banks):
                i, a = low(banks[0])
                if mi == 0:
                    UPr.next()
                x = UPr.at
                b = UPr.bufs[x]
                d = join(banks[0], i, a, b[:, mi, 16:272], *upad, *UPr.free[x])
                p = P(tt(b[:, mi, 16:272], b[:, mi, 16:272], R1[:, :], ALU.mult), d)
                up_tok.setdefault(g, []).append(p)
                yield
                if mi == 1:
                    pool_tail(g, x, b, up_tok[g], u)
            return ev

        up_tok = {}
        yw_free = [[], []]
        up_busy = [sg_tok]

        def pool_tail(g, x, b, toks, u):
            nonlocal up_busy
            src, t, w, n, bufs = b, toks, 1, 0, [upa, upb]
            while w < (2, 4, 8, 16)[g]:
                dst = bufs[n % 2]
                t = [D(tt(dst[:, :, 2 * w:272], src[:, :, 2 * w:272], src[:, :, w:272 - w], ALU.add), *t, *([sg_tok[7]] if up_busy == [sg_tok] else up_busy))]
                up_busy = []
                src, w, n = dst, 2 * w, n + 1
            dst = bufs[n % 2]
            rcg = con[:, CRC + 16 * g:CRC + 16 * g + 16].unsqueeze(1).broadcast_to([128, 2, 16])
            t1 = D(tt(dst[:, :, 16:32], src[:, :, 16:32], rcg, ALU.mult), *t, ld["con"])
            D(stt(dst[:, :, 32:272], src[:, :, 32:272], 1.0 / w, b[:, :, 32:272], ALU.mult, ALU.subtract), *t)
            t = [D(tt(dst[:, :, 16:32], dst[:, :, 16:32], b[:, :, 16:32], ALU.subtract), t1)]
            UPr.free[x] = t
            d_tok = t

            def dense():
                nonlocal up_busy
                m = MB.next()
                M = MB.bufs[m]
                fns = []
                for mi in range(2):
                    for ki in range(2):
                        fns.append(mm(M[:, 256 * mi:256 * mi + 256], ry["poolw"][:, g, ki, 128 * mi:128 * mi + 128],
                                      dst[:, ki, 16:272], ki == 0, ki == 1))
                t = PE(many(*fns), *d_tok, ld["poolw"], *MB.free[m])
                up_busy = [t]
                for mi in range(2):
                    k = 2 * g + mi
                    s = tS.next()
                    S = tS.bufs[s]
                    d = D(ts(S[:, :], M[:, 256 * mi:256 * mi + 256], C("pool_b", k), ALU.add, C("pool_scale", k), ALU.mult),
                          t, *tS.free[s])
                    MB.free[m] = [d]
                    tS.free[s] = [split(ZB, ready_b, k, S[:, :], None, d)]
            if g == 0:
                at(pre, u, dense)
            else:
                at(post, u + 1, dense)

        nU = 0
        for j in range(8):
            unit2(ins["w_in"], 8 + j, ZA, evac_lru_x(j))
        for j in range(8):
            unit2(ins["w_in"], 16 + j, ZA, evac_gate(j))
        for g in (3, 2, 1, 0):
            for mi in range(2):
                unit2(ins["w_in"], 2 * g + mi, ZA, evac_pool(g, mi))

        lru = {}

        def lru_decay(j0):
            for j in range(j0, j0 + 4):
                lru[f"v{j}"] = A(act(rg[:, j, :], rg[:, j, :], ACT.Tanh, scale=sp4[:, 2, j:j + 1]), sg_tok[j], ini['sp'])
        at(post, 10, lambda: lru_decay(0))
        at(post, 11, lambda: lru_decay(4))

        def lru_a(h):
            j = slice(4 * h, 4 * h + 4)
            v, w, s = rg[:, j, :], W1[:, j, :], S1[:, j, :]
            vt = lru[f"v{4 * h + 3}"]
            a = A(act(s, v, ACT.Sqrt, scale=4.0), vt)
            d = D(ts(w, v, 1.0, ALU.add), vt)
            d = D(lambda e: e.reciprocal(w, w), d)
            p = P(tt(s, s, w, ALU.mult), a, d)
            p = P(tt(s, s, ig[:, j, :], ALU.mult), p)
            lru[f"b{h}"] = P(tt(s, s, XC[:, j, :], ALU.mult), p, xc_tok[4 * h + 3])
            d = D(ts(v, v, -1.0, ALU.mult, 1.0, ALU.add), a)
            lru[f"a{h}"] = D(tt(v, v, w, ALU.mult), d)
        at(post, 12, lambda: lru_a(0))
        at(post, 14, lambda: lru_a(1))

        def lru_scan(h):
            for j in range(4 * h, 4 * h + 4):
                d = D(lambda e, j=j: e.tensor_tensor_scan(XC[:, j, :], rg[:, j, :], S1[:, j, :], 0.0, ALU.mult, ALU.add),
                      lru[f"a{h}"], lru[f"b{h}"])
                lru[f"h{j}"] = P(tt(gl[:, j, :], gl[:, j, :], XC[:, j, :], ALU.mult), d, gl_tok[j])
        at(post, 17, lambda: lru_scan(0))
        at(post, 18, lambda: lru_scan(1))

        def lru_out(j):
            split(ZB, ready_b, 8 + j, gl[:, j, :], None, lru[f"h{j}"], lru["h7"], lru["a1"])
        for j in range(8):
            at(post, 19 + j // 2, lambda j=j: lru_out(j))

        x_tok = {k: ldx[k // 4] for k in range(16)}

        def evac_wout(m):
            def ev(u, banks):
                i, a = low(banks[0])
                s, d = join_s(banks[0], i, a)
                b = tS.bufs[s]
                p = P(tt(X[:, m, :], b[:, :], X[:, m, :], ALU.add), d)
                tS.free[s] = [p]
                x_tok[m] = p
                add_square(0, m == 0, X[:, m, :], p)
                yield
                yield
                split(ZA, ready_a, m, X[:, m, :], C("g2", m), p, mm_half[2 * 24 - 1])
            return ev

        order = ((1, range(8)), (0, (6, 7, 4, 5, 2, 3, 0, 1)))
        for m in range(16):
            unit2(ins["w_out"], m, ZB, evac_wout(m), order)

        def norm2():
            rtok["R2"] = rstd(0, R2[:, :], 2048)
        at(post, 40, norm2)

        ld_keys = {}

        def load_keys():
            ld_keys[0] = A.dma(lambda e: e.dma_start(ry["keys"][:, :, :], ins["keys"]), s_in["keys"], 1, up_busy[0], sg_tok[7])
        at(post, 30, load_keys)

        Vk, Ik, If, eq = rr["Vk"], rr["Ik"], rr["If"], rr["eq"]
        TS, TP, sel, sm, IJG = zb["TS"], zb["TP"], zb["sel"], zb["sm"], zb["IJG"]
        mr = Ring([rr["mr0"], rr["mr1"]])
        cd = Ring([rr["cd0"], rr["cd1"]])
        QT = Ring([tS.bufs[0]])
        q_tok, q_buf, key_bank, key_tok = {}, {}, {}, {}
        NEG = -3.0e38
        zb_old = []

        def top16(src, vals, idx, width, *tokens):
            r = mr.next()
            R = mr.bufs[r][:, 0:width]
            d = D(lambda e: e.max(vals[:, 0:8], src), *tokens)
            f = D(lambda e: e.match_replace(R, vals[:, 0:8], src, NEG), d, *mr.free[r])
            D(lambda e: e.max_index(idx[:, 0:8], vals[:, 0:8], src), d)
            g = D(lambda e: e.max(vals[:, 8:16], R), f)
            g = D(lambda e: e.max_index(idx[:, 8:16], vals[:, 8:16], R), g)
            mr.free[r] = [g]
            return g

        def evac_wq(h, half):
            def ev(u, banks):
                i, a = low(banks[0])
                s, d = join_s(banks[0], i, a)
                b = tS.bufs[s]
                p = P(tt(b[:, :], b[:, :], R2[:, :], ALU.mult), d, rtok["R2"])
                q_tok[h, half], q_buf[h, half] = p, s
                tS.free[s] = [p]

                def scores():
                    m = key_bank[h, half] = MB.next()
                    M = MB.bufs[m]
                    s = q_buf[h, half]
                    fns = [mm(M[:, 128 * t:128 * t + 128], tS.bufs[s][:, 128 * t:128 * t + 128],
                              ry["keys"][:, 2 * h + half, :], True, True) for t in range(2)]
                    key_tok[h, half] = PE(many(*fns), q_tok[h, half], ld_keys[0], *MB.free[m])
                    tS.free[s] = [key_tok[h, half]]
                at(post, u + 1, scores)

                def route(t):
                    m = key_bank[h, half]
                    M = MB.bufs[m]
                    g = top16(M[:, 128 * t:128 * t + 128], Vk[:, t, h, half, :], Ik[:, t, h, half, :],
                              128, key_tok[h, half], *zb_old)
                    rk[t, h, half] = g
                    if t == 1:
                        MB.free[m] = [g]
                at(post, u + 2, lambda: route(0))
                at(post, u + 2, lambda: route(1))
                if half == 1:
                    at(post, u + 3, lambda: cand(0, h))
                    at(post, u + 4, lambda: cand(1, h))
                yield
            return ev

        rk, ck = {}, {}

        def cand(t, h):
            c = cd.next()
            b = cd.bufs[c]
            v1 = Vk[:, t, h, 0, :].unsqueeze(2).broadcast_to([128, 16, 16])
            v2 = Vk[:, t, h, 1, :].unsqueeze(1).broadcast_to([128, 16, 16])
            p = P(tt(b[:, :, :], v1, v2, ALU.add), rk[t, h, 0], rk[t, h, 1], *cd.free[c])
            g = top16(b[:, :, :].rearrange("p a b -> p (a b)"), TS[:, t, 16 * h:16 * h + 16], TP[:, t, 16 * h:16 * h + 16],
                      256, p)
            cd.free[c] = [g]
            ck[t, h] = g

        for h in range(8):
            for half in range(2):
                unit2(ins["wq"], 2 * h + half, ZA, evac_wq(h, half))
        U0 = len(units)

        dec = {}

        def decode_a(t):
            for h in range(8):
                dec["c", t] = ck[t, h]
            a = P(lambda e: e.tensor_copy(If[:, t, :, :, :], Ik[:, t, :, :, :]), rk[t, 7, 1])
            d = D(ts(rr["tpa"][:, t, :], TP[:, t, :], 4, ALU.logical_shift_right), ck[t, 7])
            dec["pa", t] = D(lambda e: e.tensor_copy(sel[:, 0, t, :], rr["tpa"][:, t, :]), d)
            d = D(ts(rr["tpa"][:, t, :], TP[:, t, :], 15, ALU.bitwise_and), dec["pa", t])
            dec["pb", t] = D(lambda e: e.tensor_copy(sel[:, 1, t, :], rr["tpa"][:, t, :]), d)
            dec["if", t] = a

        def decode_b(t, half):
            digit = sel[:, half, t, :].rearrange("p (h k) -> p h k", h=8)
            io = iota16.unsqueeze(1).broadcast_to([128, 128, 16])
            e3 = eq[:, :, :, :].rearrange("p h k a -> p (h k) a")
            p = D(tt(e3, sel[:, half, t, :].unsqueeze(2).broadcast_to([128, 128, 16]), io, ALU.is_equal),
                  dec["pb", t], *dec.get("eq", []))
            for h in range(8):
                p2 = P(tt(eq[:, h, :, :], eq[:, h, :, :],
                          If[:, t, h, half, :].unsqueeze(1).broadcast_to([128, 16, 16]), ALU.mult), p, dec["if", t])
            d = D(lambda e: e.tensor_reduce(rr["tpf"][:, half, :], e3, AX.X, ALU.add), p2)
            dec["eq"] = [d]
            dec["sel", t, half] = d

            def turn():
                m = MB.next()
                M = MB.bufs[m]
                t1 = PE(lambda e: e.transpose(M[:, 0:128], rr["tpf"][:, half, :], ident), d, *MB.free[m])
                a = A(act(IJG[:, half, 128 * t:128 * t + 128], M[:, 0:128], ACT.Copy), t1)
                MB.free[m] = [a]
                dec["eq"] = [d, t1]
                dec["ijg", t, half] = a
            return turn

        def softmax(t):
            s3 = TS[:, t, :].rearrange("p (h k) -> p h k", h=8)
            g = sel[:, 2, t, :]
            g3 = g.rearrange("p (h k) -> p h k", h=8)
            d = D(tt(g3, s3, s3[:, :, 0:1].broadcast_to([128, 8, 16]), ALU.subtract), ck[t, 7])
            a = A(act(g, g, ACT.Exp), d)
            d = D(lambda e: e.tensor_reduce(sm[:, t, 0:8], g3, AX.X, ALU.add), a)
            d = D(lambda e: e.reciprocal(sm[:, t, 0:8], sm[:, t, 0:8]), d)
            d = D(tt(g3, g3, sm[:, t, 0:8].unsqueeze(2).broadcast_to([128, 8, 16]), ALU.mult), d)
            dec["g", t] = d

            def turn():
                m = MB.next()
                M = MB.bufs[m]
                t1 = PE(lambda e: e.transpose(M[:, 0:128], g, ident), d, *MB.free[m])
                a = A(act(IJG[:, 2, 128 * t:128 * t + 128], M[:, 0:128], ACT.Copy), t1)
                MB.free[m] = [a]
                dec["ijg", t, 2] = a
            return turn

        def sched_decode(t, u):
            at(post, u, lambda: decode_a(t))

            def b(half):
                turn = decode_b(t, half)
                at(post, u + 2 + half, turn)
            at(post, u + 1, lambda: b(0))
            at(post, u + 2, lambda: b(1))

            def s():
                turn = softmax(t)
                at(post, u + 2, turn)
            at(post, u + 1, s)
        sched_decode(0, U0 + 4)
        sched_decode(1, U0 + 6)

        stage = Ring([zb["stage0"], zb["stage1"]])
        oA, oB = Ring([zb["oneA"][:, i, :] for i in range(4)]), Ring([zb["oneB"][:, i, :] for i in range(4)])
        st_w = []
        st_count = [0, 0]

        def spread(c0):
            s = stage.next()
            S = stage.bufs[s]
            for q in range(4):
                m = MB.next()
                M = MB.bufs[m]
                for n in range(4):
                    c = c0 + 4 * q + n
                    need = [dec["ijg", c // 128, k] for k in range(3)]
                    a, b = oA.next(), oB.next()
                    p = D(ts(oA.bufs[a], iota, IJG[:, 0, c:c + 1], ALU.is_equal), *need, *oA.free[a])
                    d = D(ts(oB.bufs[b], iota, IJG[:, 1, c:c + 1], ALU.is_equal, IJG[:, 2, c:c + 1], ALU.mult),
                          *need, *oB.free[b])
                    t = PE(mm(M[:, 128 * n:128 * n + 128], oA.bufs[a], oB.bufs[b], True, True), p, d,
                           *(MB.free[m] if n == 0 else []))
                    oA.free[a], oB.free[b] = [t], [t]
                src = M[:, :].rearrange("p (c k j) -> p k c j", c=4, k=8)
                a = A(act(S[:, :, 4 * q:4 * q + 4, :], src, ACT.Copy), t, *stage.free[s])
                MB.free[m] = [a]
            st_count[s] += 1
            dst = scr[:, :, 16 * c0:16 * c0 + 256].rearrange("k p n -> p k n")
            w = A.dma(lambda e: e.dma_start(dst, S[:, :, :, :].rearrange("p k c j -> p k (c j)")), s_st[s], st_count[s], a)
            stage.free[s] = [w]
            st_w.append(w)

        for n in range(16):
            at(post, U0 + 10 + n, lambda n=n: spread(16 * n))

        Gc = rr["Gc"]
        gc = {"n": 0, "free": []}

        def load_g(jc):
            gc["n"] += 1
            gc[jc] = SP_G.dma(lambda e: e.dma_start(Gc[:, :, :].rearrange("p c j -> p (c j)"), scr[jc]), s_gc, gc["n"],
                              *st_w[-2:], *gc["free"], *dec["eq"])
        SP_G = A
        A1 = rr["A1"]
        a_tok = {}

        def evac_u(jc, j):
            def ev(u, banks):
                i, a = low(banks[0])
                s, d = join_s(banks[0], i, a)
                b = tS.bufs[s]
                p = P(tt(b[:, :], b[:, :], R2[:, :], ALU.mult), d)
                yield
                if jc < 2:
                    dst = (Y if jc == 0 else A1)[:, j, :]
                    old = list(key_tok.values()) if jc == 0 else [dec["g", 1], ck[1, 7]]
                    a_tok[jc, j] = A(act(dst, b[:, :], ACT.Gelu_apprx_tanh), p, *old)
                    tS.free[s] = [a_tok[jc, j]]
                else:
                    a = A(act(b[:, :], b[:, :], ACT.Gelu_apprx_tanh), p)
                    p = P(tt(b[:, :], b[:, :], Gc[:, :, j], ALU.mult), a, gc[jc])
                    gc["free"] = [p]
                    yield
                    tS.free[s] = [split(ZB, ready_b, j, b[:, :], None, p, v_last[jc - 1])]
            return ev

        def gate_a(jc, j):
            B = Y if jc == 0 else A1
            p = P(tt(B[:, j, :], B[:, j, :], Gc[:, :, j], ALU.mult), a_tok[jc, j], gc[jc])
            a_tok[jc, j] = p
            gc["free"] = [p]

        def split_a(jc):
            B = Y if jc == 0 else A1
            for j in range(16):
                split(ZB, ready_b, j, B[:, j, :], None, a_tok[jc, j],
                      *([v_last[jc - 1]] if jc else [st_w[-1], st_w[-2], PE_last[0]]))

        v_last = {}
        PE_last = [None]
        gf_tok = D(tt(gfm[:, :], col[:, COL0["gf"]:COL0["gf"] + 16], col[:, COL0["gpm"]:COL0["gpm"] + 16], ALU.mult), ld["col"])

        def evac_v(jc, m):
            def ev(u, banks):
                i, a = low(banks[0])
                b = tA.bufs[i]
                p = P(tt(b[:, :], b[:, :], X[:, m, :], ALU.add), a)
                d = join(banks[0], i, p, X[:, m, :])
                x_tok[m] = d
                yield
                if jc == 7:
                    add_square(0, m == 0, X[:, m, :], d)
                    p = P(ts(X[:, m, :], X[:, m, :], C("gf", m), ALU.mult), d)
                    add_square(1, m == 0, X[:, m, :], p)
                    x_tok[m] = p
                    yield
                    split(ZA, ready_a, m, X[:, m, :], C("gpm", m), p, last_zA[0])
            return ev

        last_zA = [None]

        def chunk_u(jc):
            s = len(units)
            for j in range(16):
                unit2(ins["pu"], 16 * jc + j, ZA, evac_u(jc, j))
            if jc == 7:
                at(pre, len(units), lambda: last_zA.__setitem__(0, mm_half[units[s + 15][1] - 1]))
            return s

        def chunk_v(jc):
            s = len(units)
            for m in range(16):
                unit2(ins["pv"], m, ZB, evac_v(jc, m), kbase=2 * jc)
            at(pre, len(units), lambda: v_last.__setitem__(jc, mm_half[units[s + 15][1] - 1]))
            if jc >= 1 and jc < 7:
                at(post, s + 1, lambda: load_g(jc + 1))
            return s

        chunk_u(0)
        u1 = chunk_u(1)
        at(post, U0 + 26, lambda: load_g(0))
        for j in range(16):
            at(post, U0 + 28 + j // 5, lambda j=j: gate_a(0, j))
        v0 = len(units)

        def before_v0():
            PE_last[0] = oA.free[oA.at][0]
            split_a(0)
        at(pre, v0, before_v0)
        chunk_v(0)
        at(post, v0, lambda: load_g(1))
        for j in range(16):
            at(post, v0 + 4 + j // 2, lambda j=j: gate_a(1, j))
        at(pre, v0 + 16, lambda: split_a(1))
        chunk_v(1)
        for jc in range(2, 8):
            chunk_u(jc)
            chunk_v(jc)

        F0 = len(units)

        def norm_f():
            t = rstd(0, R3[:, :], 2048)
            rtok["RF"] = t
            m, t2 = mean_of(acc[1][:, :], acc_tok[1])
            acc_free[1] = [t2]
            j = tS.next()
            b = tS.bufs[j]
            p = P(tt(b[:, :], R3[:, :], R3[:, :], ALU.mult), t, *tS.free[j])
            d = D(tt(b[:, :], MB.bufs[m][:, 0:256], b[:, :], ALU.mult), p, t2)
            MB.free[m] = [d]
            a = A(act(b[:, :], b[:, :], ACT.Sqrt, scale=1.0 / 2048, bias=C("eps")), d)
            d = D(lambda e: e.reciprocal(b[:, :], b[:, :]), a)
            rtok["RC"] = P(tt(R2[:, :], b[:, :], R3[:, :], ALU.mult), d)
            tS.free[j] = [rtok["RC"]]
        at(post, F0, norm_f)

        def scale_x(m):
            x_tok[m] = P(tt(X[:, m, :], X[:, m, :], R3[:, :], ALU.mult), x_tok[m], *ready_a[m])
        for m in range(16):
            at(post, F0 + 2 + m, lambda m=m: scale_x(m))

        qkv, VT, O, CV = zb["qkv"], zb["VT"], ry["O"], ry["CV"]
        zsr, spr = Ring([zb["zs0"], zb["zs1"]]), Ring([zb["sp0"], zb["sp1"]])
        UC = Ring([rr[f"UC{i}"] for i in range(5)])
        zb_dead = {}

        def open_f():
            last = mm_half[units[F0 - 1][1] - 1]
            zb_dead[0] = last
            zb_dead["mask"] = A.dma(lambda e: e.dma_start(zb["mask"][:, :], ins["con"][:, CEND:CEND + 384]),
                                    s_in["mask"], 1, last)
            zb_dead["mask"] = A.dma(lambda e: e.dma_start(zb["neg"][:, :], ins["con"][:, CEND + 384:CEND + 768]),
                                    s_in["mask"], 2, last)
            for i in range(5):
                ucpad.append(P(lambda e, i=i: e.memset(rr[f"UC{i}"][:, 0:30], 0.0), gc["free"][0]))
        ucpad = []
        at(pre, F0, open_f)

        sgl = {}
        conv_q = []
        conv_tok = {}

        def evac_glu_b(j):
            def ev(u, banks):
                i, a = low(banks[0])
                s, d = join_s(banks[0], i, a)
                b = tS.bufs[s]
                p = P(tt(b[:, :], b[:, :], R2[:, :], ALU.mult), d, rtok["RC"])
                yield
                yield
                q = sg.next()
                sgl[j] = (q, A(act(sg.bufs[q][:, :], b[:, :], ACT.Sigmoid, bias=C("b_in", 32 + j)), p, *sg.free[q]))
                tS.free[s] = [sgl[j][1]]
            return ev
        sg = Ring([acc[0], acc[1]])

        def evac_glu_a(j):
            def ev(u, banks):
                i, a = low(banks[0])
                s, d = join_s(banks[0], i, a)
                b = tS.bufs[s]
                p = P(tt(b[:, :], b[:, :], R2[:, :], ALU.mult), d, rtok["RC"])
                yield
                c = UC.next()
                q, st = sgl[j]
                d = D(stt(UC.bufs[c][:, 30:286], b[:, :], C("b_in", 24 + j), sg.bufs[q][:, :], ALU.add, ALU.mult), p, st,
                      ucpad[c], *UC.free[c])
                tS.free[s] = [d]
                sg.free[q] = [d]
                for k in range(TAPS):
                    conv_q.append((j, k, c, d))
            return ev

        def conv_step(n):
            for _ in range(min(n, len(conv_q))):
                j, k, c, d = conv_q.pop(0)
                b = UC.bufs[c]
                w = C("w_dw", 8 * k + j)
                if k == 0:
                    t = D(ts(CV[:, j, :], b[:, 0:256], w, ALU.mult, C("b_dw", j), ALU.add), d)
                else:
                    t = D(stt(CV[:, j, :], b[:, k:k + 256], w, CV[:, j, :], ALU.mult, ALU.add), conv_tok[j])
                conv_tok[j] = t
                if k == TAPS - 1:
                    UC.free[c] = [t]

        qkv_free = [[] for _ in range(4)]
        vt_free = [[] for _ in range(4)]
        qkv_tok = {}

        def evac_qkv(h, w):
            def ev(u, banks):
                i, a = low(banks[0])
                s, d = join_s(banks[0], i, a)
                b = tS.bufs[s]
                p = P(tt(b[:, :], b[:, :], R2[:, :], ALU.mult), d, rtok["RC"])
                yield
                yield
                a = A(act(qkv[:, h % 4, w, :], b[:, :], ACT.Identity, bias=C("b_in", 8 * w + h)), p,
                      zb_dead[0], *qkv_free[h % 4])
                tS.free[s] = [a]
                qkv_tok[h, w] = a
                if w == 2 and h % 2:
                    g = attention(h - 1)
                    for n in range(4):
                        at(post, u + 1 + n, lambda: next(g, None))
            return ev

        av_last = [None]

        def attention(h0):
            mV = MB.next()
            tv = PE(many(*[(lambda e, h=h, b=b: e.transpose(MB.bufs[mV][:, 256 * (h - h0) + 128 * b:256 * (h - h0) + 128 * b + 128],
                                                           qkv[:, h % 4, 2, 128 * b:128 * b + 128], ident))
                           for h in (h0, h0 + 1) for b in range(2)]), qkv_tok[h0 + 1, 2], *MB.free[mV])
            av = D(lambda e: e.tensor_copy(VT[:, h0 % 4:h0 % 4 + 2, :].rearrange("p h n -> p (h n)"), MB.bufs[mV][:, :]),
                   tv, *vt_free[h0 % 4])
            MB.free[mV] = [av]
            z = zsr.next()
            s = spr.next()
            ZS, SPb = zsr.bufs[z], spr.bufs[s]
            for h in (h0, h0 + 1):
                m = MB.next()
                M = MB.bufs[m]
                q, k = qkv[:, h % 4, 0, :], qkv[:, h % 4, 1, :]
                t = PE(many(mm(M[:, 0:256], k[:, 0:128], q, True, True),
                            mm(M[:, 256:384], k[:, 128:256], q[:, 128:256], True, True)),
                       qkv_tok[h, 1], *MB.free[m])
                zt = A(act(ZS[:, h - h0, :], M[:, 0:384], ACT.Copy, scale=128 ** -0.5), t, *zsr.free[z])
                MB.free[m] = [zt]
            qkv_free[h0 % 4] = qkv_free[h0 % 4 + 1] = [t, tv]
            yield
            a = A(act(SPb[:, :, :], ZS[:, :, :], ACT.Abs), zt, *spr.free[s])
            a = A(act(SPb[:, :, :], SPb[:, :, :], ACT.Exp, scale=-1.0), a)
            a = A(act(SPb[:, :, :], SPb[:, :, :], ACT.Ln, bias=1.0), a)
            d = D(stt(SPb[:, :, :], ZS[:, :, :], 0.0, SPb[:, :, :], ALU.max, ALU.add), a)
            p = P(tt(SPb[:, :, :], SPb[:, :, :], zb["mask"][:, :].unsqueeze(1).broadcast_to([128, 2, 384]), ALU.mult),
                  d, zb_dead["mask"])
            yield
            for h in (h0, h0 + 1):
                n = h - h0
                m = MB.next()
                M = MB.bufs[m]
                t = PE(many(mm(M[:, 0:256], tri, SPb[:, n, 0:256], True, False),
                            mm(M[:, 128:256], ones, SPb[:, n, 256:384], False, True),
                            mm(M[:, 256:384], tri, SPb[:, n, 256:384], True, True)), p, *MB.free[m])
                d = D(tt(ZS[:, n, :], ZS[:, n, :], M[:, 0:384], ALU.subtract), t)
                MB.free[m] = [d]
            spr.free[s] = [t]
            p = P(tt(ZS[:, :, :], ZS[:, :, :], zb["neg"][:, :].unsqueeze(1).broadcast_to([128, 2, 384]), ALU.add), d)
            a = A(act(ZS[:, :, :], ZS[:, :, :], ACT.Exp), p)
            yield
            m = MB.next()
            M = MB.bufs[m]
            fns = []
            for h in (h0, h0 + 1):
                n = h - h0
                fns += [mm(M[:, 256 * n:256 * n + 256], VT[:, h % 4, 0:128], ZS[:, n, 0:256], True, False),
                        mm(M[:, 256 * n + 128:256 * n + 256], VT[:, h % 4, 128:256], ZS[:, n, 256:384], False, True)]
            t = PE(many(*fns), a, av, *MB.free[m])
            zsr.free[z] = [t]
            vt_free[h0 % 4] = [t]
            d = A(act(O[:, h0:h0 + 2, :].rearrange("p h t -> p (h t)"), M[:, :], ACT.Copy), t, *y_dead)
            MB.free[m] = [d]
            av_last[0] = t
            o_tok[h0] = o_tok[h0 + 1] = d

        o_tok = {}
        y_dead = []

        def evac_sig(dst, n, bcol):
            def ev(u, banks):
                i, a = low(banks[0])
                s, d = join_s(banks[0], i, a)
                b = tS.bufs[s]
                p = P(tt(b[:, :], b[:, :], R2[:, :], ALU.mult), d)
                yield
                yield
                a = A(act(dst[:, n, :], b[:, :], ACT.Sigmoid, bias=C("b_in", bcol)), p)
                tS.free[s] = [a]
                sg2[dst.name, n] = a
            return ev
        sg2 = {}

        for j in range(8):
            unit2(ins["w_in2"], 32 + j, ZA, evac_glu_b(j))
            unit2(ins["w_in2"], 24 + j, ZA, evac_glu_a(j))
            for w in range(3):
                unit2(ins["w_in2"], 8 * w + j, ZA, evac_qkv(j, w))
        FG = len(units)
        for n in range(16):
            unit2(ins["w_in2"], 40 + n, ZA, evac_sig(rr["SGS"], n, 40 + n))
            unit2(ins["w_in2"], 56 + n, ZA, evac_sig(rr["SGC"], n, 56 + n))
        for s in range(F0 + 2, FG + 14):
            at(post, s, lambda: conv_step(5))
        at(post, FG + 14, lambda: conv_step(1000))

        ln = {}
        SQ8 = None

        def ln_mean():
            ln["s"] = D(lambda e: e.tensor_reduce(Rn[0][:, :], CV[:, :, :].rearrange("p k t -> p t k"), AX.X, ALU.add),
                        *conv_tok.values())
            m, t = mean_of(Rn[0][:, :], ln["s"])
            ln["mu"] = D(ts(Rn[0][:, :], MB.bufs[m][:, 0:256], 1.0 / 1024, ALU.mult), t)
            MB.free[m] = [ln["mu"]]

        def ln_sub():
            for j in range(8):
                p = P(tt(CV[:, j, :], CV[:, j, :], Rn[0][:, :], ALU.subtract), ln["mu"])
                add_square(0, j == 0, CV[:, j, :], p)
            ln["c"] = p

        def ln_rstd():
            ln["r"] = rstd(0, Rn[0][:, :], 1024, ln["c"])

        def ln_mul():
            ln["x"] = D(tt(CV[:, :, :], CV[:, :, :], Rn[0][:, :].unsqueeze(1).broadcast_to([128, 8, T]), ALU.mult), ln["r"])

        def ln_silu(j0):
            for j in range(j0, j0 + 4):
                a = A(act(CV[:, j, :], CV[:, j, :], ACT.Silu, scale=C("gcl", j), bias=C("bcl", j)), ln["x"])
                split(ZB, ready_b, 8 + j, CV[:, j, :], None, a, av_last[0])

        def o_split(j0):
            for j in range(j0, j0 + 4):
                split(ZB, ready_b, j, O[:, j, :], None, o_tok[j], av_last[0], o_tok[7])
        at(pre, FG, lambda: acc_free[0].extend(sg.free[0]) or acc_free[1].extend(sg.free[1]))
        at(post, FG + 15, ln_mean)
        at(post, FG + 16, ln_sub)
        at(post, FG + 18, ln_rstd)
        at(post, FG + 19, ln_mul)
        at(post, FG + 21, lambda: ln_silu(0))
        at(post, FG + 22, lambda: ln_silu(4))
        at(post, FG + 10, lambda: o_split(0))
        at(post, FG + 11, lambda: o_split(4))

        H0 = len(units)

        def evac_merge(m):
            def ev(u, banks):
                s1, s2 = rr["SGS"], rr["SGC"]
                i, a = low(banks[0])
                s, d = join_s(banks[0], i, a)
                b = tS.bufs[s]
                p = P(tt(b[:, :], b[:, :], s1[:, m, :], ALU.mult), d, sg2["SGS", m])
                i, a = low(banks[1])
                r, d = join_s(banks[1], i, a)
                c = tS.bufs[r]
                yield
                p2 = P(tt(c[:, :], c[:, :], s2[:, m, :], ALU.mult), d, sg2["SGC", m])
                p = P(tt(b[:, :], b[:, :], c[:, :], ALU.add), p, p2)
                tS.free[r] = [p]
                yield
                tS.free[s] = [split(ZA, ready_a, m, b[:, :], None, p, mm_half[units[H0 - 1][1] - 1])]
            return ev

        for m in range(16):
            unit([(ins["w_sc"][m, 0], ZB, 0, list(range(8)), 0, True, True),
                  (ins["w_sc"][m, 1], ZB, 1, list(range(8)), 1, True, True)], evac_merge(m))
        W0 = len(units)
        y_tok = {}

        def evac_wo(m):
            def ev(u, banks):
                i, a = low(banks[0])
                d = join(banks[0], i, a, Y[:, m, :], *ready_b[0], *ready_b[7], *ready_b[15])
                y_tok[m] = d
                add_square(0, m == 0, Y[:, m, :], d)
                yield
            return ev
        for m in range(16):
            unit2(ins["w_o"], m, ZA, evac_wo(m))
        M0 = len(units)

        def post_mix():
            r = rstd(0, R1[:, :], 2048, ln["x"])
            last = mm_half[units[M0 - 1][1] - 1]
            for m in range(16):
                d = D(stt(Y[:, m, :], Y[:, m, :], C("gpost", m), R1[:, :], ALU.mult, ALU.mult), r, y_tok[m])
                p = P(tt(X[:, m, :], X[:, m, :], Y[:, m, :], ALU.add), d, x_tok[m])
                x_tok[m] = y_tok[m] = p
                split(ZA, ready_a, m, X[:, m, :], C("gpmlp", m), p, last)
        at(pre, M0, post_mix)

        def norm_mlp():
            for m in range(16):
                add_square(0, m == 0, X[:, m, :], x_tok[m])
            rtok["R3"] = rstd(0, R3[:, :], 2048, x_tok[15])
        at(post, M0, norm_mlp)

        def evac_up(c, j):
            def ev(u, banks):
                i, a = low(banks[0])
                s, d = join_s(banks[0], i, a)
                b = tS.bufs[s]
                p = P(tt(b[:, :], b[:, :], R3[:, :], ALU.mult), d, rtok["R3"])
                yield
                d = D(stt(b[:, :], b[:, :], 0.0, b[:, :], ALU.max, ALU.mult), p)
                yield
                before = [d_last[c - 1]] if c else [mm_half[units[W0 - 1][1] - 1]]
                tS.free[s] = [split(ZB, ready_b, j, b[:, :], None, d, *before)]
            return ev

        d_last = {}

        def evac_down(c, m):
            def ev(u, banks):
                i, a = low(banks[0])
                b = tA.bufs[i]
                if c:
                    a = P(tt(b[:, :], b[:, :], Y[:, m, :], ALU.add), a, y_tok[m])
                d = join(banks[0], i, a, Y[:, m, :], y_tok[m])
                y_tok[m] = d
                if c == 3:
                    add_square(0, m == 0, Y[:, m, :], d)
                yield
            return ev

        for c in range(4):
            for j in range(16):
                unit2(ins["w_up"], 16 * c + j, ZA, evac_up(c, j))
            s = len(units)
            for m in range(16):
                unit2(ins["w_down"], m, ZB, evac_down(c, m), kbase=2 * c)
            at(pre, len(units), lambda c=c, s=s: d_last.__setitem__(c, mm_half[units[s + 15][1] - 1]))

        def finish():
            r = rstd(0, R1[:, :], 2048)
            for m in range(16):
                d = D(stt(Y[:, m, :], Y[:, m, :], C("gpostmlp", m), R1[:, :], ALU.mult, ALU.mult), r, y_tok[m])
                e_ = P if m % 2 else D
                t = e_(tt(X[:, m, :], X[:, m, :], Y[:, m, :], ALU.add), d, x_tok[m])
                o = SP.dma(lambda e, m=m: e.dma_start(out[:, m, :], X[:, m, :]), s_out, m + 1, t)
            SP.wait(o)

        def prelude():
            start_x()
            sqx = rr["sqx"]
            t = P(tt(sqx[:, :, :], X[:, :, :], X[:, :, :], ALU.mult), *ldx)
            ini['sqx'] = acc_tok[0] = D(lambda e: e.tensor_reduce(acc[0][:, :], sqx[:, :, :].rearrange("p k t -> p t k"), AX.X, ALU.add), t)
            lam = col[:, COL0["lam"]:COL0["lam"] + 8]
            t = A(act(sp4[:, 0, :], lam, ACT.Abs), ld["col"])
            t = A(act(sp4[:, 0, :], sp4[:, 0, :], ACT.Exp, scale=-1.0), t)
            t = A(act(sp4[:, 0, :], sp4[:, 0, :], ACT.Ln, bias=1.0), t)
            t2 = D(ts(sp4[:, 1, :], lam, -1.0, ALU.mult, 0.0, ALU.max), ld["col"])
            t = D(tt(sp4[:, 1, :], sp4[:, 1, :], sp4[:, 0, :], ALU.add), t, t2)
            ini['sp'] = D(ts(sp4[:, 2, :], sp4[:, 1, :], 4.0, ALU.mult), t)

        prelude()
        N = len(units)
        nxt = 3
        for u in range(N + 1):
            ev = units[u - 1][2](u, banks) if u else iter(())
            next(ev, None)
            prep(nxt)
            next(ev, None)
            prep(nxt + 1)
            nxt += 2
            next(ev, None)
            for fn in pre.get(u, []):
                fn()
            if u < N:
                banks = products(u)
                for fn in post.get(u, []):
                    fn()
        finish()

        block = ctx.enter_context(nc.Block())

        @block.sync
        def _(e):
            SP.run(e)

        @block.scalar
        def _(e):
            A.run(e)

        @block.vector
        def _(e):
            D.run(e)

        @block.gpsimd
        def _(e):
            P.run(e)

        @block.tensor
        def _(e):
            PE.run(e)


def _gemm(w):
    K, N = w.shape
    return w.reshape(K // 1024, 8, 128, N // 128, 128).transpose(3, 0, 2, 1, 4).reshape(N // 128, K // 1024, 128, 1024)


def _constants(np):
    f = np.float32
    c = np.zeros((128, CEND + 768), f)
    i = np.arange(128)
    c[:, CI:CI + 128] = np.eye(128, dtype=f)
    c[:, CTRI:CTRI + 128] = (i[:, None] >= i[None, :]).astype(f)
    c[:, CONE:CONE + 128] = 1.0
    c[:, CIOTA:CIOTA + 128] = i[None, :]
    for g, w in enumerate((2, 4, 8, 16)):
        c[:, CRC + 16 * g:CRC + 16 * g + 16] = 1.0 / np.minimum(np.arange(1, 17), w).astype(f)
    before = (i[:, None] < i[None, :]).astype(f)
    mask = np.concatenate([before, np.ones((128, 128), f), before], axis=1)
    c[:, CEND:CEND + 384] = mask
    c[:, CEND + 384:CEND + 768] = np.where(mask > 0, f(0), f(-1.0e38))
    return c


def kernel(**inputs):
    import numpy as np
    import concourse.bacc as _bacc
    from concourse.bass_utils import run_bass_kernel_spmd as _run

    v = {k: np.asarray(x) for k, x in inputs.items()}

    def cols(a):
        return a.reshape(-1, 128).T

    named = {"g1": v["norm1_g"], "pool_b": v["pool_b"], "pool_scale": v["pool_scale"], "conv_w": v["conv_w"],
             "conv_b": v["conv_b"], "gab": v["gate_a_b"], "gxb": v["gate_x_b"], "lam": v["lru_lambda"],
             "g2": v["norm2_g"], "gf": v["norm_f_g"], "gpm": v["g_pre_mix_2"], "b_in": v["b_in_2"],
             "w_dw": v["w_dw_2"], "b_dw": v["b_dw_2"], "gcl": v["g_conv_ln_2"], "bcl": v["b_conv_ln_2"],
             "gpost": v["g_post_mix_2"], "gpmlp": v["g_pre_mlp_2"], "gpostmlp": v["g_post_mlp_2"]}
    packed = [cols(named[n]) for n, _ in COLS[:-1]] + [np.full((128, 1), 1e-6, np.float32)]
    keys = np.stack([v["peer_keys1"][0], v["peer_keys2"][0]], axis=1)
    arrays = {
        "xT": v["x"][0].reshape(256, 16, 128).transpose(2, 1, 0),
        "con": _constants(np),
        "cols": np.concatenate(packed, axis=1),
        "gaw": v["gate_a_w"][0].transpose(1, 0, 2),
        "gxw": v["gate_x_w"][0].transpose(1, 0, 2),
        "poolw": v["pool_w"][0].reshape(4, 2, 128, 256).transpose(2, 0, 1, 3),
        "keys": keys.reshape(16, 128, 128).transpose(2, 0, 1),
        "w_in": _gemm(v["w_in"][0]),
        "w_out": _gemm(v["w_out"][0]),
        "wq": _gemm(v["peer_wq"][0]),
        "pu": v["peer_u"][0].reshape(128, 128, 2, 8, 128).transpose(1, 2, 4, 3, 0).reshape(128, 2, 128, 1024),
        "pv": v["peer_v"][0].reshape(128, 16, 8, 16, 128).transpose(3, 1, 0, 2, 4).reshape(16, 16, 128, 1024),
        "w_in2": _gemm(v["w_in_2"][0]),
        "w_sc": np.stack([_gemm(v["w_sb_out_2"][0])[:, 0], _gemm(v["w_conv_out_2"][0])[:, 0]], axis=1),
        "w_o": _gemm(v["w_o_2"][0]),
        "w_up": _gemm(v["w_up_2"][0]),
        "w_down": _gemm(v["w_down_2"][0]),
    }
    nc = _bacc.Bacc("TRN2", target_bir_lowering=False, num_devices=1)
    given, aps = {}, {}
    for name, a in arrays.items():
        a = np.ascontiguousarray(a)
        given[f"in_{name}"] = a
        aps[name] = nc.dram_tensor(f"in_{name}", a.shape, mybir.dt.from_np(a.dtype), kind="ExternalInput").ap()
    out = nc.dram_tensor("out_0", (128, 16, 256), F32, kind="ExternalOutput").ap()
    build(nc, aps, out)
    r = _run(nc, [given], core_ids=[0])
    got = np.asarray(r.results[0]["out_0"])
    return np.ascontiguousarray(got.transpose(2, 1, 0).reshape(1, 256, 2048))
```

```python
from contextlib import ExitStack

import concourse.bass as bass
from concourse import mybir
from concourse.alu_op_type import AluOpType as ALU

F32 = mybir.dt.float32
F32R = mybir.dt.float32r
U32 = mybir.dt.uint32
ACT = mybir.ActivationFunctionType
AX = mybir.AxisListType

T = 256
NRAW = 3
NW = 5
HALF = 8 * 128
TAPS = 31

COLS = [("g1", 16), ("pool_b", 8), ("pool_scale", 8), ("conv_w", 32), ("conv_b", 8), ("gab", 8), ("gxb", 8),
        ("lam", 8), ("g2", 16), ("gf", 16), ("gpm", 16), ("b_in", 72), ("w_dw", 8 * TAPS), ("b_dw", 8),
        ("gcl", 8), ("bcl", 8), ("gpost", 16), ("gpmlp", 16), ("gpostmlp", 16), ("eps", 1)]
COL0 = {}
NCOL = 0
for _n, _c in COLS:
    COL0[_n] = NCOL
    NCOL += _c

CI, CTRI, CONE, CIOTA, CRC, CEND = 0, 128, 256, 384, 512, 576


class Engine:

    def __init__(self, sem):
        self.sem, self.n, self.ops, self.waited = sem, 0, [], {}

    def wait(self, *tokens):
        for sem, value in tokens:
            if self.waited.get(sem.name, 0) < value:
                self.waited[sem.name] = value
                self.ops.append(lambda e, sem=sem, value=value: e.wait_ge(sem, value))

    def __call__(self, fn, *tokens):
        self.wait(*tokens)
        self.n += 1
        sem = self.sem
        self.ops.append(lambda e: fn(e).then_inc(sem, 1))
        return (self.sem, self.n)

    def dma(self, fn, sem, count, *tokens):
        self.wait(*tokens)
        self.ops.append(lambda e: fn(e).then_inc(sem, 16))
        return (sem, 16 * count)

    def run(self, e):
        for op in self.ops:
            op(e)


class Ring:

    def __init__(self, bufs):
        self.bufs, self.free, self.at = bufs, [[] for _ in bufs], -1

    def next(self):
        self.at = (self.at + 1) % len(self.bufs)
        return self.at


def build(nc, ins, out):
    ctx = ExitStack()
    with ctx:
        def sb(name, shape, dt=F32):
            return ctx.enter_context(nc.sbuf_tensor(name, shape, dt))

        def sem(name):
            return ctx.enter_context(nc.semaphore(name))

        def region(nbytes, name, *layouts):
            out = {}
            for layout in layouts:
                with ExitStack() as c:
                    for n, shape, dt in layout:
                        out[n] = c.enter_context(nc.sbuf_tensor(n, shape, dt))
            sb(name, [128, nbytes // 4])
            return out

        raw = [sb(f"raw{i}", [128, HALF]) for i in range(NRAW)]
        hi = [sb(f"hi{i}", [128, 8, 128], F32R) for i in range(NW)]
        lo = [sb(f"lo{i}", [128, 8, 128], F32R) for i in range(NW)]
        ZA = sb("ZA", [128, 16, 512], F32R)
        X = sb("X", [128, 16, T])
        zb = region(32768, "zb_mem",
                    [("ZB", [128, 16, 512], F32R)],
                    [("zb_pad0", [128, 16, T], F32), ("S1", [128, 8, T], F32), ("W1", [128, 8, T], F32)],
                    [("stage0", [128, 8, 16, 16], F32), ("stage1", [128, 8, 16, 16], F32),
                     ("oneA0", [128, 8, 128], F32), ("oneA1", [128, 8, 128], F32),
                     ("IJG", [128, 3, T], F32), ("TS", [128, 2, 128], F32), ("TP", [128, 2, 128], U32),
                     ("sel", [128, 3, 2, 128], F32)],
                    [("qkv", [128, 4, 3, T], F32), ("VT", [128, 4, T], F32), ("zs0", [128, 2, 384], F32),
                     ("zs1", [128, 2, 384], F32), ("sp0", [128, 2, 384], F32), ("sp1", [128, 2, 384], F32),
                     ("mask", [128, 384], F32), ("neg", [128, 384], F32)])
        ry = region(16384, "y_mem",
                    [("Y", [128, 16, T], F32)],
                    [("poolw", [128, 4, 2, 256], F32), ("gaw", [128, 8, 128], F32), ("gxw", [128, 8, 128], F32)],
                    [("y_pad1", [128, 8, T], F32), ("upa", [128, 2, 272], F32), ("upb", [128, 2, 272], F32)],
                    [("y_pad0", [128, 8, T], F32), ("keys", [128, 16, 128], F32)],
                    [("O", [128, 8, T], F32), ("CV", [128, 8, T], F32)])
        rr = region(39 * 1024, "rr_mem",
                    [("XC", [128, 8, T], F32), ("rg", [128, 8, T], F32), ("ig", [128, 8, T], F32),
                     ("gl", [128, 8, T], F32), ("XL0", [128, 260], F32), ("XL1", [128, 260], F32),
                     ("UP0", [128, 2, 272], F32), ("UP1", [128, 2, 272], F32)],
                    [("rr_pad0", [128, 8, T], F32), ("sqx", [128, 16, T], F32)],
                    [("A1", [128, 16, T], F32), ("Gc", [128, T, 16], F32)],
                    [("eq1", [128, 8, 16, 16], F32), ("rr_pad5", [128, 8, T], F32), ("eq0", [128, 8, 16, 16], F32), ("Vk", [128, 2, 8, 2, 16], F32),
                     ("Ik", [128, 2, 8, 2, 16], U32), ("If", [128, 2, 8, 2, 16], F32),
                     ("mr0", [128, 256], F32), ("mr1", [128, 256], F32)],
                    [("rr_pad2", [128, 16, T], F32), ("rr_pad3", [128, 16, T], F32),
                     ("cd0", [128, 16, 16], F32), ("cd1", [128, 16, 16], F32), ("tpa", [128, 2, 128], U32),
                     ("tpf", [128, 2, 128], F32), ("sm", [128, 4, 16], F32)],
                    [("rr_pad4", [128, 16, T], F32), ("oneB0", [128, 8, 128], F32), ("oneB1", [128, 8, 128], F32)],
                    [("U1", [128, 16, T], F32), ("U2", [128, 16, T], F32)],
                    [("SGS", [128, 16, T], F32), ("SGC", [128, 16, T], F32),
                     ("UC0", [128, 288], F32), ("UC1", [128, 288], F32), ("UC2", [128, 288], F32),
                     ("UC3", [128, 288], F32), ("UC4", [128, 288], F32)])
        con = sb("con", [128, CEND])
        col = sb("col", [128, NCOL])
        UP = [rr["UP0"], rr["UP1"]]
        upa, upb = ry["upa"], ry["upb"]
        sp4 = sb("sp4", [128, 3, 8])
        gpp, warm = sb("gpp", [128, 16]), sb("warm", [128, 1])
        Rn = [sb(f"R{i}", [128, T]) for i in range(3)]
        acc = [sb(f"acc{i}", [128, T]) for i in range(2)]
        tA = Ring([sb(f"tA{i}", [128, T]) for i in range(3)])
        tS = Ring([sb(f"tS{i}", [128, T]) for i in range(4)])
        tQ = Ring([sb(f"tQ{i}", [128, T]) for i in range(2)])
        GB = Ring([ctx.enter_context(nc.psum_tensor(f"G{i}", [128, 512], F32)) for i in range(4)])
        MB = Ring([ctx.enter_context(nc.psum_tensor(f"M{i}", [128, 512], F32)) for i in range(4)])
        scr = nc.dram_tensor("g_scratch", [8, 128, T * 16], F32, kind="Internal").ap()
        ident, tri, ones, iota = (con[:, c:c + 128] for c in (CI, CTRI, CONE, CIOTA))
        iota16 = con[:, CIOTA:CIOTA + 16]
        ZB, Y = zb["ZB"], ry["Y"]

        def C(name, i=0):
            return col[:, COL0[name] + i:COL0[name] + i + 1]

        PE, A, D, P = (Engine(sem(n)) for n in ("s_pe", "s_act", "s_dve", "s_pool"))
        SP = Engine(sem("s_sp"))
        s_raw = [sem(f"s_raw{i}") for i in range(NRAW)]
        s_in = {n: sem(f"s_{n}") for n in ("con", "col", "mask", "poolw", "gaw", "gxw", "keys")}
        s_x = [sem(f"s_x{i}") for i in range(4)]
        s_st = [sem("s_st0"), sem("s_st1")]
        s_gc, s_out = sem("s_gc"), sem("s_out")

        def tt(o, a, b, op):
            return lambda e: e.tensor_tensor(o, a, b, op)

        def ts(o, a, s1, op0, s2=None, op1=None):
            if op1 is None:
                return lambda e: e.tensor_scalar(o, a, s1, None, op0)
            return lambda e: e.tensor_scalar(o, a, s1, s2, op0, op1)

        def stt(o, a, s, b, op0, op1):
            return lambda e: e.scalar_tensor_tensor(out=o, in0=a, scalar=s, in1=b, op0=op0, op1=op1)

        def act(o, i, f, **k):
            return lambda e: e.activation(o, i, f, **k)

        def mm(o, l, r, start, stop):
            return lambda e: e.matmul(o, l, r, start=start, stop=stop, skip_group_check=True)

        def many(*fns):
            def run(e):
                for f in fns:
                    last = f(e)
                return last
            return run

        ld = {}
        xcut = (0, 2, 6, 11, 16)
        ldx = []
        for i in range(4):
            ldx.append(A.dma(lambda e, i=i: e.dma_start(X[:, xcut[i]:xcut[i + 1], :], ins["xT"][:, xcut[i]:xcut[i + 1], :]),
                             s_x[i], 1))
            if i == 0:
                ld["col"] = A.dma(lambda e: e.dma_start(col[:, :], ins["cols"]), s_in["col"], 1)
        ld["con"] = A.dma(lambda e: e.dma_start(con[:, :], ins["con"][:, 0:CEND]), s_in["con"], 1)
        ld["gaw"] = A.dma(lambda e: e.dma_start(ry["gaw"][:, :, :], ins["gaw"]), s_in["gaw"], 1)
        ld["gxw"] = A.dma(lambda e: e.dma_start(ry["gxw"][:, :, :], ins["gxw"]), s_in["gxw"], 1)
        ld["poolw"] = A.dma(lambda e: e.dma_start(ry["poolw"][:, :, :, :], ins["poolw"]), s_in["poolw"], 1)

        halves = []
        units = []

        def unit(hs, evac):
            a = len(halves)
            halves.extend(hs)
            units.append((a, len(halves), evac))

        def unit2(w, m, Z, evac, order=((0, range(8)), (1, range(8))), kbase=0):
            hs = []
            for n, (kh, kks) in enumerate(order):
                hs.append((w[m, kbase + kh], Z, kh, list(kks), 0, n == 0, n == 1))
            unit(hs, evac)

        ready_a, ready_b = [[] for _ in range(16)], [[] for _ in range(16)]
        mm_half = {}
        w_tok = {}

        def prep(h):
            if h >= len(halves):
                return
            r, w = h % NRAW, h % NW
            src = halves[h][0]
            ld_tok = SP.dma(lambda e: e.dma_start(raw[r][:, :], src), s_raw[r], h // NRAW + 1,
                            *(w_tok[h - NRAW] if h >= NRAW else []))
            free = [mm_half[h - NW]] if h >= NW else []
            rw = raw[r][:, :].rearrange("p (k n) -> p k n", k=8)
            a = A(act(hi[w][:, :, :], rw, ACT.Copy), ld_tok, *free)
            c = pool_share(h // 2)
            toks = [a]
            if c < 8:
                toks.append(D(tt(lo[w][:, 0:8 - c, :], rw[:, 0:8 - c, :], hi[w][:, 0:8 - c, :].bitcast(F32), ALU.subtract), a))
            if c:
                toks.append(P(tt(lo[w][:, 8 - c:8, :], rw[:, 8 - c:8, :], hi[w][:, 8 - c:8, :].bitcast(F32), ALU.subtract), a))
            w_tok[h] = toks

        def pool_share(u):
            return 5 if 42 <= u < U0 + 4 else 4 if U0 + 4 <= u < U0 + 28 else 2

        def products(u):
            a, b, _ = units[u]
            banks = {}
            for h in range(a, b):
                _, Z, kh, kks, bk, start, stop = halves[h]
                if bk not in banks:
                    banks[bk] = GB.next()
                g = banks[bk]
                G = GB.bufs[g]
                PE.wait(*w_tok[h])
                if start:
                    PE.wait(*GB.free[g])
                ready = ready_a if Z is ZA else ready_b
                w = h % NW
                for n, kk in enumerate(kks):
                    k = 8 * kh + kk
                    PE.wait(*ready[k])
                    f = many(mm(G[:, 0:512], hi[w][:, kk, :], Z[:, k, :], start and n == 0, False),
                             mm(G[:, 0:256], lo[w][:, kk, :], Z[:, k, 0:256], False, stop and n == 7))
                    if n < 7:
                        PE.ops.append(f)
                    else:
                        mm_half[h] = PE(f)
                if h == a:
                    for fn in mid.get(u, []):
                        fn()
            return [(GB.bufs[banks[k]], banks[k], mm_half[b - 1]) for k in sorted(banks)]

        def low(bank, scale=None):
            G, g, tok = bank
            i = tA.next()
            k = {} if scale is None else {"scale": scale}
            return i, A(act(tA.bufs[i][:, :], G[:, 256:512], ACT.Copy, **k), tok, *tA.free[i])

        def join(bank, i, a, dst, *tokens):
            G, g, tok = bank
            d = D(tt(dst, G[:, 0:256], tA.bufs[i][:, :], ALU.add), a, *tokens)
            GB.free[g] = [d]
            tA.free[i] = [d]
            return d

        def join_s(bank, i, a):
            j = tS.next()
            return j, join(bank, i, a, tS.bufs[j][:, :], *tS.free[j])

        def split(Z, ready, k, src, scale, *tokens):
            if scale is None:
                a = A(act(Z[:, k, 0:256], src, ACT.Copy), *tokens)
                d = D(tt(Z[:, k, 256:512], src, Z[:, k, 0:256].bitcast(F32), ALU.subtract), a)
            else:
                a = A(act(Z[:, k, 0:256], src, ACT.Copy, scale=scale), *tokens)
                d = D(stt(Z[:, k, 256:512], src, scale, Z[:, k, 0:256].bitcast(F32), ALU.mult, ALU.subtract), a)
            ready[k] = [a, d]
            return d

        acc_free = [[], []]
        acc_tok = [None, None]

        def add_square(n, first, src, *tokens):
            if first:
                acc_tok[n] = A(act(acc[n][:, :], src, ACT.Square), *tokens, *acc_free[n])
                return acc_tok[n]
            q = tQ.next()
            t = A(act(tQ.bufs[q][:, :], src, ACT.Square), *tokens, *tQ.free[q])
            acc_tok[n] = P(tt(acc[n][:, :], acc[n][:, :], tQ.bufs[q][:, :], ALU.add), t, acc_tok[n])
            tQ.free[q] = [acc_tok[n]]
            return t

        def mean_of(src, *tokens):
            m = MB.next()
            t = PE(mm(MB.bufs[m][:, 0:256], ones, src, True, True), *tokens, *MB.free[m], ld["con"])
            return m, t

        def rstd(n, dst, count, *tokens):
            m, t = mean_of(acc[n][:, :], acc_tok[n])
            acc_free[n] = [t]
            a = A(act(dst, MB.bufs[m][:, 0:256], ACT.Sqrt, scale=1.0 / count, bias=C("eps")), t, *tokens)
            MB.free[m] = [a]
            return D(lambda e: e.reciprocal(dst, dst), a)

        pre, mid, post, hold = {}, {}, {}, {}

        def at(where, step, fn):
            where.setdefault(step, []).append(fn)

        R1, R2, R3 = Rn
        rtok = {}
        XC, rg, ig, gl, S1, W1 = (rr[n] if n in rr else zb[n] for n in ("XC", "rg", "ig", "gl", "S1", "W1"))
        XL = Ring([rr["XL0"], rr["XL1"]])
        UPr = Ring(UP)
        pad_tok = [P(lambda e, b=b: e.memset(b[:, 0:3], 0.0)) for b in (rr["XL0"], rr["XL1"])]
        upad = [P(lambda e, b=b: e.memset(b[:, :, 0:16], 0.0)) for b in UP]

        def start_x():
            for i in range(4):
                for k in range(xcut[i], xcut[i + 1]):
                    split(ZA, ready_a, k, X[:, k, :], C("g1", k), ldx[i], ld["col"])
                if i == 0:
                    prep(0)
                if i == 1:
                    prep(1)
                if i == 3:
                    prep(2)

        ini = {}

        def first_norm():
            rtok["R1"] = rstd(0, R1[:, :], 2048)
        at(post, 1, first_norm)
        hold[0] = 2

        sg_tok, xc_tok, gl_tok = {}, {}, {}

        def evac_lru_x(j):
            def ev(u, banks):
                i, a = low(banks[0])
                x = XL.next()
                b = XL.bufs[x]
                d = join(banks[0], i, a, b[:, 3:259], pad_tok[x], *XL.free[x])
                p = P(tt(b[:, 3:259], b[:, 3:259], R1[:, :], ALU.mult), d, rtok["R1"])
                yield
                c = D(ts(XC[:, j, :], b[:, 0:256], C("conv_w", j), ALU.mult, C("conv_b", j), ALU.add), p)
                for k in range(1, 4):
                    c = D(stt(XC[:, j, :], b[:, k:k + 256], C("conv_w", 8 * k + j), XC[:, j, :], ALU.mult, ALU.add), c)
                XL.free[x] = [c]
                xc_tok[j] = c

                def gates():
                    m = MB.next()
                    M = MB.bufs[m]
                    t = PE(many(mm(M[:, 0:256], ry["gaw"][:, j, :], XC[:, j, :], True, True),
                                mm(M[:, 256:512], ry["gxw"][:, j, :], XC[:, j, :], True, True)),
                           xc_tok[j], ld["gaw"], ld["gxw"], *MB.free[m])
                    a = A(act(rg[:, j, :], M[:, 0:256], ACT.Sigmoid, bias=C("gab", j)), t, ini['sqx'])
                    b = A(act(ig[:, j, :], M[:, 256:512], ACT.Sigmoid, bias=C("gxb", j)), t)
                    MB.free[m] = [b]
                    sg_tok[j] = b
                at(post, u + 1, gates)
            return ev

        def evac_gate(j):
            def ev(u, banks):
                i, a = low(banks[0])
                s, d = join_s(banks[0], i, a)
                b = tS.bufs[s]
                p = P(tt(b[:, :], b[:, :], R1[:, :], ALU.mult), d)
                yield
                a = A(act(b[:, :], b[:, :], ACT.Gelu_apprx_tanh), p)
                p = P(tt(b[:, :], b[:, :], XC[:, j, :], ALU.mult), a, lru[f"h{j}"])
                yield
                tS.free[s] = [split(ZB, ready_b, 8 + j, b[:, :], None, p, lru["h7"])]
            return ev

        def evac_pool(g, mi):
            def ev(u, banks):
                i, a = low(banks[0])
                if mi == 0:
                    UPr.next()
                x = UPr.at
                b = UPr.bufs[x]
                d = join(banks[0], i, a, b[:, mi, 16:272], *upad, *UPr.free[x])
                p = P(tt(b[:, mi, 16:272], b[:, mi, 16:272], R1[:, :], ALU.mult), d)
                up_tok.setdefault(g, []).append(p)
                yield
                if mi == 1:
                    pool_tail(g, x, b, up_tok[g], u)
            return ev

        up_tok = {}
        yw_free = [[], []]
        up_busy = [sg_tok]

        def pool_tail(g, x, b, toks, u):
            nonlocal up_busy
            src, t, w, n, bufs = b, toks, 1, 0, [upa, upb]
            while w < (2, 4, 8, 16)[g]:
                dst = bufs[n % 2]
                t = [D(tt(dst[:, :, 2 * w:272], src[:, :, 2 * w:272], src[:, :, w:272 - w], ALU.add), *t, *([sg_tok[7]] if up_busy == [sg_tok] else up_busy))]
                up_busy = []
                src, w, n = dst, 2 * w, n + 1
            dst = bufs[n % 2]
            rcg = con[:, CRC + 16 * g:CRC + 16 * g + 16].unsqueeze(1).broadcast_to([128, 2, 16])
            t1 = D(tt(dst[:, :, 16:32], src[:, :, 16:32], rcg, ALU.mult), *t, ld["con"])
            D(stt(dst[:, :, 32:272], src[:, :, 32:272], 1.0 / w, b[:, :, 32:272], ALU.mult, ALU.subtract), *t)
            t = [D(tt(dst[:, :, 16:32], dst[:, :, 16:32], b[:, :, 16:32], ALU.subtract), t1)]
            UPr.free[x] = t
            d_tok = t

            def dense():
                nonlocal up_busy
                m = MB.next()
                M = MB.bufs[m]
                fns = []
                for mi in range(2):
                    for ki in range(2):
                        fns.append(mm(M[:, 256 * mi:256 * mi + 256], ry["poolw"][:, g, ki, 128 * mi:128 * mi + 128],
                                      dst[:, ki, 16:272], ki == 0, ki == 1))
                t = PE(many(*fns), *d_tok, ld["poolw"], *MB.free[m])
                up_busy = [t]
                for mi in range(2):
                    k = 2 * g + mi
                    s = tS.next()
                    S = tS.bufs[s]
                    d = D(ts(S[:, :], M[:, 256 * mi:256 * mi + 256], C("pool_b", k), ALU.add, C("pool_scale", k), ALU.mult),
                          t, *tS.free[s])
                    MB.free[m] = [d]
                    tS.free[s] = [split(ZB, ready_b, k, S[:, :], None, d)]
            at(post, u + 1, dense)

        nU = 0
        for j in range(8):
            unit2(ins["w_in"], 8 + j, ZA, evac_lru_x(j))
        for g in (3, 2, 1, 0):
            for mi in range(2):
                unit2(ins["w_in"], 2 * g + mi, ZA, evac_pool(g, mi))
        for j in range(8):
            unit2(ins["w_in"], 16 + j, ZA, evac_gate(j))

        lru = {}

        def lru_decay(j0):
            for j in range(j0, j0 + 4):
                t = A(act(S1[:, j, :], rg[:, j, :], ACT.Tanh, scale=sp4[:, 2, j:j + 1]), sg_tok[j], ini['sp'])
                lru[f"a{j}"] = A(act(rg[:, j, :], rg[:, j, :], ACT.Exp, scale=sp4[:, 1, j:j + 1]), t)
        at(post, 9, lambda: lru_decay(0))
        at(post, 10, lambda: lru_decay(4))

        def lru_b(h):
            j = slice(2 * h, 2 * h + 2)
            s = S1[:, j, :]
            a = A(act(s, s, ACT.Sqrt), lru[f"a{2 * h + 1}"])
            d = D(stt(s, rg[:, j, :], 1.0, s, ALU.add, ALU.mult), a)
            p = P(tt(s, s, ig[:, j, :], ALU.mult), d)
            lru[f"b{h}"] = P(tt(s, s, XC[:, j, :], ALU.mult), p, xc_tok[2 * h + 1])
        at(post, 11, lambda: (lru_b(0), lru_b(1)))
        at(post, 12, lambda: (lru_b(2), lru_b(3)))

        def lru_scan(j):
            lru[f"h{j}"] = D(lambda e: e.tensor_tensor_scan(XC[:, j, :], rg[:, j, :], S1[:, j, :], 0.0, ALU.mult, ALU.add),
                             lru[f"a{j}"], lru[f"b{j // 2}"])
        for j in range(8):
            at(post, 12 + j // 2, lambda j=j: lru_scan(j))

        x_tok = {k: ldx[i] for i in range(4) for k in range(xcut[i], xcut[i + 1])}

        def evac_wout(m):
            def ev(u, banks):
                i, a = low(banks[0])
                s, d = join_s(banks[0], i, a)
                b = tS.bufs[s]
                p = P(tt(X[:, m, :], b[:, :], X[:, m, :], ALU.add), d)
                tS.free[s] = [p]
                x_tok[m] = p
                add_square(0, m == 0, X[:, m, :], p)
                yield
                yield
                split(ZA, ready_a, m, X[:, m, :], C("g2", m), p, mm_half[2 * 24 - 1])
            return ev

        order = ((0, (6, 7, 4, 5, 2, 3, 0, 1)), (1, range(8)))
        for m in range(16):
            unit2(ins["w_out"], m, ZB, evac_wout(m), order)

        def norm2():
            rtok["R2"] = rstd(0, R2[:, :], 2048)
        at(post, 41, norm2)
        hold[40] = 42

        ld_keys = {}

        def load_keys():
            ld_keys[0] = A.dma(lambda e: e.dma_start(ry["keys"][:, :, :], ins["keys"]), s_in["keys"], 1, up_busy[0], sg_tok[7])
        at(post, 30, load_keys)

        Vk, Ik, If, eqs = rr["Vk"], rr["Ik"], rr["If"], Ring([rr["eq0"], rr["eq1"]])
        TS, TP, sel, sm, IJG = zb["TS"], zb["TP"], zb["sel"], rr["sm"], zb["IJG"]
        mr = Ring([rr["mr0"], rr["mr1"]])
        cd = Ring([rr["cd0"], rr["cd1"]])
        QT = Ring([tS.bufs[0]])
        q_tok, q_buf, key_bank, key_tok = {}, {}, {}, {}
        NEG = -3.0e38
        zb_old = []

        def top16(jobs, width):
            rs = [mr.next() for _ in jobs]
            R = [mr.bufs[r][:, 0:width] for r in rs]
            d = [D(lambda e, v=v, src=src: e.max(v[:, 0:8], src), *toks) for src, v, i, toks in jobs]
            f = [D(lambda e, n=n, v=v, src=src: e.match_replace(R[n], v[:, 0:8], src, NEG), d[n], *mr.free[rs[n]])
                 for n, (src, v, i, toks) in enumerate(jobs)]
            for n, (src, v, i, toks) in enumerate(jobs):
                D(lambda e, i=i, v=v, src=src: e.max_index(i[:, 0:8], v[:, 0:8], src), d[n])
            g = [D(lambda e, n=n, v=v: e.max(v[:, 8:16], R[n]), f[n]) for n, (src, v, i, toks) in enumerate(jobs)]
            for n, (src, v, i, toks) in enumerate(jobs):
                last = D(lambda e, n=n, i=i, v=v: e.max_index(i[:, 8:16], v[:, 8:16], R[n]), g[n])
                mr.free[rs[n]] = [last]
            return last

        def evac_wq(h, half):
            def ev(u, banks):
                i, a = low(banks[0])
                s, d = join_s(banks[0], i, a)
                b = tS.bufs[s]
                p = P(tt(b[:, :], b[:, :], R2[:, :], ALU.mult), d, rtok["R2"])
                q_tok[h, half], q_buf[h, half] = p, s
                tS.free[s] = [p]

                def scores():
                    m = key_bank[h, half] = MB.next()
                    M = MB.bufs[m]
                    s = q_buf[h, half]
                    fns = [mm(M[:, 128 * t:128 * t + 128], tS.bufs[s][:, 128 * t:128 * t + 128],
                              ry["keys"][:, 2 * h + half, :], True, True) for t in range(2)]
                    key_tok[h, half] = PE(many(*fns), q_tok[h, half], ld_keys[0], *MB.free[m])
                    tS.free[s] = [key_tok[h, half]]
                at(post, u + 1, scores)

                def route():
                    m = key_bank[h, half]
                    M = MB.bufs[m]
                    rk[h, half] = top16([(M[:, 128 * t:128 * t + 128], Vk[:, t, h, half, :], Ik[:, t, h, half, :],
                                          [key_tok[h, half]]) for t in range(2)], 128)
                    MB.free[m] = [rk[h, half]]
                at(post, u + 2, route)
                if half == 1:
                    at(post, u + 3, lambda: cand(h))
                yield
            return ev

        rk, ck = {}, {}

        def cand(h):
            jobs = []
            for t in range(2):
                c = cd.next()
                b = cd.bufs[c]
                v1 = Vk[:, t, h, 0, :].unsqueeze(2).broadcast_to([128, 16, 16])
                v2 = Vk[:, t, h, 1, :].unsqueeze(1).broadcast_to([128, 16, 16])
                p = P(tt(b[:, :, :], v1, v2, ALU.add), rk[h, 0], rk[h, 1], *cd.free[c])
                jobs.append((b[:, :, :].rearrange("p a b -> p (a b)"), TS[:, t, 16 * h:16 * h + 16],
                             TP[:, t, 16 * h:16 * h + 16], [p]))
            ck[h] = top16(jobs, 256)
            cd.free[0] = cd.free[1] = [ck[h]]

        for h in range(8):
            for half in range(2):
                unit2(ins["wq"], 2 * h + half, ZA, evac_wq(h, half))
        U0 = len(units)

        dec = {}

        def decode_a(t):
            a = P(lambda e: e.tensor_copy(If[:, t, :, :, :], Ik[:, t, :, :, :]), rk[7, 1])
            d = D(ts(rr["tpa"][:, t, :], TP[:, t, :], 4, ALU.logical_shift_right), ck[7])
            dec["pa", t] = D(lambda e: e.tensor_copy(sel[:, 0, t, :], rr["tpa"][:, t, :]), d)
            d = D(ts(rr["tpa"][:, t, :], TP[:, t, :], 15, ALU.bitwise_and), dec["pa", t])
            dec["pb", t] = D(lambda e: e.tensor_copy(sel[:, 1, t, :], rr["tpa"][:, t, :]), d)
            dec["if", t] = a

        def decode_b(t, half):
            q = eqs.next()
            eq = eqs.bufs[q]
            e3 = eq[:, :, :, :].rearrange("p h k a -> p (h k) a")
            io = iota16.unsqueeze(1).broadcast_to([128, 128, 16])
            d = D(tt(e3, sel[:, half, t, :].unsqueeze(2).broadcast_to([128, 128, 16]), io, ALU.is_equal),
                  dec["pb", t], *eqs.free[q])

            def pick():
                rows = If[:, t, :, half, :].unsqueeze(2).broadcast_to([128, 8, 16, 16])
                dec["pick", t, half] = P(tt(eq[:, :, :, :], eq[:, :, :, :], rows, ALU.mult), d, dec["if", t])

            def total():
                dst = rr["tpf"][:, half, :]
                dec["sel", t, half] = D(lambda e: e.tensor_reduce(dst, e3, AX.X, ALU.add), dec["pick", t, half],
                                        *([dec["turned", 0, half]] if t else []))
                eqs.free[q] = [dec["sel", t, half]]

            def turn():
                m = MB.next()
                M = MB.bufs[m]
                t1 = PE(lambda e: e.transpose(M[:, 0:128], rr["tpf"][:, half, :], ident), dec["sel", t, half], *MB.free[m])
                a = A(act(IJG[:, half, 128 * t:128 * t + 128], M[:, 0:128], ACT.Copy), t1)
                MB.free[m] = [a]
                dec["turned", t, half] = t1
                dec["ijg", t, half] = a
            return pick, total, turn

        def softmax(t):
            s3 = TS[:, t, :].rearrange("p (h k) -> p h k", h=8)
            g = sel[:, 2, t, :]
            g3 = g.rearrange("p (h k) -> p h k", h=8)
            d = D(tt(g3, s3, s3[:, :, 0:1].broadcast_to([128, 8, 16]), ALU.subtract), ck[7])
            dec["e", t] = A(act(g, g, ACT.Exp), d)

            def norm():
                d = D(lambda e: e.tensor_reduce(sm[:, t, 0:8], g3, AX.X, ALU.add), dec["e", t])
                d = D(lambda e: e.reciprocal(sm[:, t, 0:8], sm[:, t, 0:8]), d)
                dec["g", t] = D(tt(g3, g3, sm[:, t, 0:8].unsqueeze(2).broadcast_to([128, 8, 16]), ALU.mult), d)

            def turn():
                m = MB.next()
                M = MB.bufs[m]
                t1 = PE(lambda e: e.transpose(M[:, 0:128], g, ident), dec["g", t], *MB.free[m])
                a = A(act(IJG[:, 2, 128 * t:128 * t + 128], M[:, 0:128], ACT.Copy), t1)
                MB.free[m] = [a]
                dec["ijg", t, 2] = a
            return norm, turn

        def steps_b(t, half, u):
            pick, total, turn = decode_b(t, half)
            at(post, u + 1, pick)
            at(post, u + 2, total)
            at(post, u + 3, turn)

        def steps_s(t, u):
            norm, turn = softmax(t)
            at(post, u + 1, norm)
            at(post, u + 2, turn)

        D0 = U0 + 4
        at(post, D0, lambda: (decode_a(0), decode_a(1)))
        for n, (t, half) in enumerate(((0, 0), (0, 1), (1, 0), (1, 1))):
            w = D0 + (0, 1, 3, 4)[n]
            at(post, w, lambda t=t, half=half, w=w: steps_b(t, half, w))
        at(post, D0 + 1, lambda: steps_s(0, D0 + 1))
        at(post, D0 + 2, lambda: steps_s(1, D0 + 2))

        stage = Ring([zb["stage0"], zb["stage1"]])
        oA, oB = Ring([zb["oneA0"], zb["oneA1"]]), Ring([rr["oneB0"], rr["oneB1"]])
        st_w = []
        st_count = [0, 0]

        def one_hot(c):
            need = [dec["ijg", c // 128, k] for k in range(3)]
            a, b = oA.next(), oB.next()
            OA, OB = oA.bufs[a], oB.bufs[b]
            io = iota.unsqueeze(1).broadcast_to([128, 8, 128])
            db = D(tt(OB[:, :, :], io, IJG[:, 1, c:c + 8].unsqueeze(2).broadcast_to([128, 8, 128]), ALU.is_equal),
                   *need, dec["sel", 1, 0], *oB.free[b])
            da = D(tt(OA[:, :, :], io, IJG[:, 0, c:c + 8].unsqueeze(2).broadcast_to([128, 8, 128]), ALU.is_equal),
                   *oA.free[a])
            gated = []
            for n in range(4):
                gated.append(A(act(OB[:, n, :], OB[:, n, :], ACT.Copy, scale=IJG[:, 2, c + n:c + n + 1]), db))
            p = P(tt(OB[:, 4:8, :], OB[:, 4:8, :], IJG[:, 2, c + 4:c + 8].unsqueeze(2).broadcast_to([128, 4, 128]),
                     ALU.mult), db)
            oh[c] = (a, b, da, gated + [p] * 4)

        oh = {}

        def spread(c):
            if c % 16 == 0:
                stage.next()
            s = stage.at
            S = stage.bufs[s]
            a, b, da, gated = oh[c]
            for v in range(2):
                m = MB.next()
                M = MB.bufs[m]
                for n in range(4):
                    k = 4 * v + n
                    t = PE(mm(M[:, 128 * n:128 * n + 128], oA.bufs[a][:, k, :], oB.bufs[b][:, k, :], True, True),
                           da, gated[k], *(MB.free[m] if n == 0 else []))
                w = c % 16 + 4 * v
                e = A(act(S[:, :, w:w + 4, :], M[:, :].rearrange("p (c k j) -> p k c j", c=4, k=8), ACT.Copy),
                      t, *stage.free[s])
                MB.free[m] = [e]
            oA.free[a], oB.free[b] = [t], [t]
            if c % 16 == 8:
                st_count[s] += 1
                dst = scr[:, :, 16 * (c - 8):16 * (c - 8) + 256].rearrange("k p n -> p k n")
                w = A.dma(lambda e: e.dma_start(dst, S[:, :, :, :].rearrange("p k c j -> p k (c j)")), s_st[s],
                          st_count[s], e)
                stage.free[s] = [w]
                st_w.append(w)

        G0 = U0 + 11
        for n in range(16):
            if n == 0:
                at(post, G0 - 1, lambda: (one_hot(0), one_hot(8)))
            at(mid, G0 + n, lambda n=n: spread(16 * n))
            at(post, G0 + n, lambda n=n: spread(16 * n + 8))
            if n < 15:
                at(post, G0 + n, lambda n=n: (one_hot(16 * n + 16), one_hot(16 * n + 24)))

        Gc = rr["Gc"]
        gc = {"n": 0, "free": []}

        def load_g(jc):
            gc["n"] += 1
            gc[jc] = SP_G.dma(lambda e: e.dma_start(Gc[:, :, :].rearrange("p c j -> p (c j)"), scr[jc]), s_gc, gc["n"],
                              *st_w[-2:], *gc["free"], *oB.free[0], *oB.free[1])
        SP_G = A
        A1 = rr["A1"]
        a_tok = {}

        def evac_u(jc, j):
            def ev(u, banks):
                i, a = low(banks[0])
                s, d = join_s(banks[0], i, a)
                b = tS.bufs[s]
                p = P(tt(b[:, :], b[:, :], R2[:, :], ALU.mult), d)
                yield
                if jc < 2:
                    dst = (Y if jc == 0 else A1)[:, j, :]
                    old = list(key_tok.values()) if jc == 0 else [*eqs.free[1]]
                    a_tok[jc, j] = A(act(dst, b[:, :], ACT.Gelu_apprx_tanh), p, *old)
                    tS.free[s] = [a_tok[jc, j]]
                else:
                    a = A(act(b[:, :], b[:, :], ACT.Gelu_apprx_tanh), p)
                    p = P(tt(b[:, :], b[:, :], Gc[:, :, j], ALU.mult), a, gc[jc])
                    gc["free"] = [p]
                    yield
                    tS.free[s] = [split(ZB, ready_b, j, b[:, :], None, p, v_last[jc - 1][j // 8])]
            return ev

        def gate_a(jc, j0):
            B = Y if jc == 0 else A1
            k = slice(j0, j0 + 4)
            p = P(tt(B[:, k, :], B[:, k, :], Gc[:, :, k].rearrange("p c j -> p j c"), ALU.mult),
                  *[a_tok[jc, j] for j in range(j0, j0 + 4)], gc[jc])
            for j in range(j0, j0 + 4):
                a_tok[jc, j] = p
            gc["free"] = [p]

        def split_a(jc):
            B = Y if jc == 0 else A1
            hi_tok = {}

            def lows(n):
                k = slice(2 * n, 2 * n + 2)
                d = D(tt(ZB[:, k, 256:512], B[:, k, :], ZB[:, k, 0:256].bitcast(F32), ALU.subtract), hi_tok[n])
                ready_b[2 * n] = ready_b[2 * n + 1] = [hi_tok[n], d]
            for n in range(8):
                k = slice(2 * n, 2 * n + 2)
                hi_tok[n] = A(act(ZB[:, k, 0:256], B[:, k, :], ACT.Copy), a_tok[jc, 2 * n], a_tok[jc, 2 * n + 1],
                              *([v_last[jc - 1][n // 4]] if jc else [st_w[-1], st_w[-2], PE_last[0]]))
                if n:
                    lows(n - 1)
            lows(7)

        v_last = {}
        PE_last = [None]

        def evac_v(jc, m):
            def ev(u, banks):
                i, a = low(banks[0])
                b = tA.bufs[i]
                p = P(tt(b[:, :], b[:, :], X[:, m, :], ALU.add), a)
                d = join(banks[0], i, p, X[:, m, :])
                x_tok[m] = d
                yield
                if jc == 7:
                    add_square(0, m == 0, X[:, m, :], d)
                    p = A(act(X[:, m, :], X[:, m, :], ACT.Copy, scale=C("gf", m)), d)
                    add_square(1, m == 0, X[:, m, :], p)
                    x_tok[m] = p
                    yield
                    split(ZA, ready_a, m, X[:, m, :], C("gpm", m), p, last_zA[0])
            return ev

        last_zA = [None]

        def chunk_u(jc):
            s = len(units)
            for j in range(16):
                unit2(ins["pu"], 16 * jc + j, ZA, evac_u(jc, j))
            if jc == 7:
                at(pre, len(units), lambda: last_zA.__setitem__(0, mm_half[units[s + 15][1] - 1]))
            return s

        def chunk_v(jc):
            s = len(units)
            for m in range(16):
                unit2(ins["pv"], m, ZB, evac_v(jc, m), kbase=2 * jc)
            at(pre, len(units), lambda: v_last.__setitem__(jc, [mm_half[units[s + 15][0]], mm_half[units[s + 15][0] + 1]]))
            if jc >= 1 and jc < 7:
                at(post, s + 1, lambda: load_g(jc + 1))
            return s

        chunk_u(0)
        u1 = chunk_u(1)
        at(post, U0 + 27, lambda: load_g(0))
        for n in range(4):
            at(post, U0 + 29 + n // 2, lambda n=n: gate_a(0, 4 * n))
        v0 = len(units)

        def before_v0():
            PE_last[0] = oA.free[oA.at][0]
            split_a(0)
        at(pre, v0, before_v0)
        chunk_v(0)
        at(post, v0, lambda: load_g(1))
        for n in range(4):
            at(post, v0 + 4 + 2 * n, lambda n=n: gate_a(1, 4 * n))
        at(pre, v0 + 16, lambda: split_a(1))
        chunk_v(1)
        for jc in range(2, 8):
            chunk_u(jc)
            chunk_v(jc)

        F0 = len(units)

        def norm_f():
            t = rstd(0, R3[:, :], 2048)
            rtok["RF"] = t
            m, t2 = mean_of(acc[1][:, :], acc_tok[1])
            acc_free[1] = [t2]
            j = tS.next()
            b = tS.bufs[j]
            p = P(tt(b[:, :], R3[:, :], R3[:, :], ALU.mult), t, *tS.free[j])
            d = D(tt(b[:, :], MB.bufs[m][:, 0:256], b[:, :], ALU.mult), p, t2)
            MB.free[m] = [d]
            a = A(act(b[:, :], b[:, :], ACT.Sqrt, scale=1.0 / 2048, bias=C("eps")), d)
            d = D(lambda e: e.reciprocal(b[:, :], b[:, :]), a)
            rtok["RC"] = P(tt(R2[:, :], b[:, :], R3[:, :], ALU.mult), d)
            tS.free[j] = [rtok["RC"]]
        at(post, F0 + 2, norm_f)
        hold[F0] = F0 + 3

        def scale_x(m):
            x_tok[m] = P(tt(X[:, m, :], X[:, m, :], R3[:, :], ALU.mult), x_tok[m], *ready_a[m])
        for m in range(16):
            at(post, F0 + 4 + m, lambda m=m: scale_x(m))

        qkv, VT, O, CV = zb["qkv"], zb["VT"], ry["O"], ry["CV"]
        zsr, spr = Ring([zb["zs0"], zb["zs1"]]), Ring([zb["sp0"], zb["sp1"]])
        UC = Ring([rr[f"UC{i}"] for i in range(5)])
        zb_dead = {}

        def open_f():
            last = mm_half[units[F0 - 1][1] - 1]
            zb_dead[0] = last
            zb_dead["mask"] = A.dma(lambda e: e.dma_start(zb["mask"][:, :], ins["con"][:, CEND:CEND + 384]),
                                    s_in["mask"], 1, last)
            zb_dead["mask"] = A.dma(lambda e: e.dma_start(zb["neg"][:, :], ins["con"][:, CEND + 384:CEND + 768]),
                                    s_in["mask"], 2, last)
            for i in range(5):
                ucpad.append(P(lambda e, i=i: e.memset(rr[f"UC{i}"][:, 0:30], 0.0), gc["free"][0]))
        ucpad = []
        at(pre, F0, open_f)

        sgl = {}
        conv_q = []
        conv_tok = {}

        def evac_glu_b(j):
            def ev(u, banks):
                i, a = low(banks[0])
                s, d = join_s(banks[0], i, a)
                b = tS.bufs[s]
                p = P(tt(b[:, :], b[:, :], R2[:, :], ALU.mult), d, rtok["RC"])
                yield
                yield
                q = sg.next()
                sgl[j] = (q, A(act(sg.bufs[q][:, :], b[:, :], ACT.Sigmoid, bias=C("b_in", 32 + j)), p, *sg.free[q]))
                tS.free[s] = [sgl[j][1]]
            return ev
        sg = Ring([acc[0], acc[1]])

        def evac_glu_a(j):
            def ev(u, banks):
                i, a = low(banks[0])
                s, d = join_s(banks[0], i, a)
                b = tS.bufs[s]
                p = P(tt(b[:, :], b[:, :], R2[:, :], ALU.mult), d, rtok["RC"])
                yield
                c = UC.next()
                q, st = sgl[j]
                d = D(stt(UC.bufs[c][:, 30:286], b[:, :], C("b_in", 24 + j), sg.bufs[q][:, :], ALU.add, ALU.mult), p, st,
                      ucpad[c], *UC.free[c])
                tS.free[s] = [d]
                sg.free[q] = [d]
                for k in range(TAPS):
                    conv_q.append((j, k, c, d))
            return ev

        def conv_step(n):
            for _ in range(min(n, len(conv_q))):
                j, k, c, d = conv_q.pop(0)
                b = UC.bufs[c]
                w = C("w_dw", 8 * k + j)
                if k == 0:
                    t = D(ts(CV[:, j, :], b[:, 0:256], w, ALU.mult, C("b_dw", j), ALU.add), d)
                else:
                    t = D(stt(CV[:, j, :], b[:, k:k + 256], w, CV[:, j, :], ALU.mult, ALU.add), conv_tok[j])
                conv_tok[j] = t
                if k == TAPS - 1:
                    UC.free[c] = [t]

        qkv_free = [[] for _ in range(4)]
        vt_free = [[] for _ in range(4)]
        qkv_tok = {}

        def evac_qkv(h, w):
            def ev(u, banks):
                i, a = low(banks[0])
                s, d = join_s(banks[0], i, a)
                b = tS.bufs[s]
                p = P(tt(b[:, :], b[:, :], R2[:, :], ALU.mult), d, rtok["RC"])
                yield
                yield
                a = A(act(qkv[:, h % 4, w, :], b[:, :], ACT.Identity, bias=C("b_in", 8 * w + h)), p,
                      zb_dead[0], *qkv_free[h % 4])
                tS.free[s] = [a]
                qkv_tok[h, w] = a
                if w == 2 and h % 2:
                    g = attention(h - 1)
                    for n in range(4):
                        at(post, u + 1 + n, lambda: next(g, None))
            return ev

        av_last = [None]

        def attention(h0):
            mV = MB.next()
            tv = PE(many(*[(lambda e, h=h, b=b: e.transpose(MB.bufs[mV][:, 256 * (h - h0) + 128 * b:256 * (h - h0) + 128 * b + 128],
                                                           qkv[:, h % 4, 2, 128 * b:128 * b + 128], ident))
                           for h in (h0, h0 + 1) for b in range(2)]), qkv_tok[h0 + 1, 2], *MB.free[mV])
            av = D(lambda e: e.tensor_copy(VT[:, h0 % 4:h0 % 4 + 2, :].rearrange("p h n -> p (h n)"), MB.bufs[mV][:, :]),
                   tv, *vt_free[h0 % 4])
            MB.free[mV] = [av]
            z = zsr.next()
            s = spr.next()
            ZS, SPb = zsr.bufs[z], spr.bufs[s]
            for h in (h0, h0 + 1):
                m = MB.next()
                M = MB.bufs[m]
                q, k = qkv[:, h % 4, 0, :], qkv[:, h % 4, 1, :]
                t = PE(many(mm(M[:, 0:256], k[:, 0:128], q, True, True),
                            mm(M[:, 256:384], k[:, 128:256], q[:, 128:256], True, True)),
                       qkv_tok[h, 1], *MB.free[m])
                zt = A(act(ZS[:, h - h0, :], M[:, 0:384], ACT.Copy, scale=128 ** -0.5), t, *zsr.free[z])
                MB.free[m] = [zt]
            qkv_free[h0 % 4] = qkv_free[h0 % 4 + 1] = [t, tv]
            yield
            a = A(act(SPb[:, :, :], ZS[:, :, :], ACT.Abs), zt, *spr.free[s])
            a = A(act(SPb[:, :, :], SPb[:, :, :], ACT.Exp, scale=-1.0), a)
            a = A(act(SPb[:, :, :], SPb[:, :, :], ACT.Ln, bias=1.0), a)
            d = D(stt(SPb[:, :, :], ZS[:, :, :], 0.0, SPb[:, :, :], ALU.max, ALU.add), a)
            p = P(tt(SPb[:, :, :], SPb[:, :, :], zb["mask"][:, :].unsqueeze(1).broadcast_to([128, 2, 384]), ALU.mult),
                  d, zb_dead["mask"])
            yield
            for h in (h0, h0 + 1):
                n = h - h0
                m = MB.next()
                M = MB.bufs[m]
                t = PE(many(mm(M[:, 0:256], tri, SPb[:, n, 0:256], True, False),
                            mm(M[:, 128:256], ones, SPb[:, n, 256:384], False, True),
                            mm(M[:, 256:384], tri, SPb[:, n, 256:384], True, True)), p, *MB.free[m])
                d = D(tt(ZS[:, n, :], ZS[:, n, :], M[:, 0:384], ALU.subtract), t)
                MB.free[m] = [d]
            spr.free[s] = [t]
            p = P(tt(ZS[:, :, :], ZS[:, :, :], zb["neg"][:, :].unsqueeze(1).broadcast_to([128, 2, 384]), ALU.add), d)
            a = A(act(ZS[:, :, :], ZS[:, :, :], ACT.Exp), p)
            yield
            m = MB.next()
            M = MB.bufs[m]
            fns = []
            for h in (h0, h0 + 1):
                n = h - h0
                fns += [mm(M[:, 256 * n:256 * n + 256], VT[:, h % 4, 0:128], ZS[:, n, 0:256], True, False),
                        mm(M[:, 256 * n + 128:256 * n + 256], VT[:, h % 4, 128:256], ZS[:, n, 256:384], False, True)]
            t = PE(many(*fns), a, av, *MB.free[m])
            zsr.free[z] = [t]
            vt_free[h0 % 4] = [t]
            d = A(act(O[:, h0:h0 + 2, :].rearrange("p h t -> p (h t)"), M[:, :], ACT.Copy), t, *y_dead)
            MB.free[m] = [d]
            av_last[0] = t
            o_tok[h0] = o_tok[h0 + 1] = d

        o_tok = {}
        y_dead = []

        def evac_sig(dst, n, bcol):
            def ev(u, banks):
                i, a = low(banks[0])
                s, d = join_s(banks[0], i, a)
                b = tS.bufs[s]
                p = P(tt(b[:, :], b[:, :], R2[:, :], ALU.mult), d)
                yield
                yield
                a = A(act(dst[:, n, :], b[:, :], ACT.Sigmoid, bias=C("b_in", bcol)), p)
                tS.free[s] = [a]
                sg2[dst.name, n] = a
            return ev
        sg2 = {}

        for j in range(8):
            unit2(ins["w_in2"], 32 + j, ZA, evac_glu_b(j))
            unit2(ins["w_in2"], 24 + j, ZA, evac_glu_a(j))
            for w in range(3):
                unit2(ins["w_in2"], 8 * w + j, ZA, evac_qkv(j, w))
        FG = len(units)
        for n in range(16):
            unit2(ins["w_in2"], 40 + n, ZA, evac_sig(rr["SGS"], n, 40 + n))
            unit2(ins["w_in2"], 56 + n, ZA, evac_sig(rr["SGC"], n, 56 + n))
        for s in range(F0 + 2, FG + 14):
            at(post, s, lambda: conv_step(5))
        at(post, FG + 14, lambda: conv_step(1000))

        ln = {}
        SQ8 = None

        def ln_sum():
            ln["s"] = D(lambda e: e.tensor_reduce(Rn[0][:, :], CV[:, :, :].rearrange("p k t -> p t k"), AX.X, ALU.add),
                        *conv_tok.values())

        def ln_mean():
            m, t = mean_of(Rn[0][:, :], ln["s"])
            ln["mu"] = D(ts(Rn[0][:, :], MB.bufs[m][:, 0:256], 1.0 / 1024, ALU.mult), t)
            MB.free[m] = [ln["mu"]]

        def ln_sub():
            for j in range(8):
                p = P(tt(CV[:, j, :], CV[:, j, :], Rn[0][:, :], ALU.subtract), ln["mu"])
                add_square(0, j == 0, CV[:, j, :], p)
            ln["c"] = p

        def ln_rstd():
            ln["r"] = rstd(0, Rn[0][:, :], 1024, ln["c"])

        def ln_mul():
            ln["x"] = D(tt(CV[:, :, :], CV[:, :, :], Rn[0][:, :].unsqueeze(1).broadcast_to([128, 8, T]), ALU.mult), ln["r"])

        def ln_silu(j0):
            for j in range(j0, j0 + 4):
                a = A(act(CV[:, j, :], CV[:, j, :], ACT.Silu, scale=C("gcl", j), bias=C("bcl", j)), ln["x"])
                split(ZB, ready_b, 8 + j, CV[:, j, :], None, a, av_last[0])

        def o_split(j0):
            for j in range(j0, j0 + 4):
                split(ZB, ready_b, j, O[:, j, :], None, o_tok[j], av_last[0], o_tok[7])
        at(pre, FG, lambda: acc_free[0].extend(sg.free[0]) or acc_free[1].extend(sg.free[1]))
        at(post, FG + 15, ln_sum)
        at(post, FG + 16, ln_mean)
        at(post, FG + 17, ln_sub)
        at(post, FG + 21, ln_rstd)
        at(post, FG + 22, ln_mul)
        at(post, FG + 24, lambda: ln_silu(0))
        at(post, FG + 25, lambda: ln_silu(4))
        at(post, FG + 10, lambda: o_split(0))
        at(post, FG + 11, lambda: o_split(4))

        H0 = len(units)

        merged = []

        def evac_merge(m):
            def ev(u, banks):
                s1, s2 = rr["SGS"], rr["SGC"]
                i, a = low(banks[0])
                s, d = join_s(banks[0], i, a)
                b = tS.bufs[s]
                p = P(tt(b[:, :], b[:, :], s1[:, m, :], ALU.mult), d, sg2["SGS", m])
                i, a = low(banks[1])
                r, d = join_s(banks[1], i, a)
                c = tS.bufs[r]
                yield
                p2 = P(tt(c[:, :], c[:, :], s2[:, m, :], ALU.mult), d, sg2["SGC", m])
                p = P(tt(b[:, :], b[:, :], c[:, :], ALU.add), p, p2)
                tS.free[r] = [p]
                merged[:] = [p]
                yield
                tS.free[s] = [split(ZA, ready_a, m, b[:, :], None, p, mm_half[units[H0 - 1][1] - 1])]
            return ev

        for m in range(16):
            unit([(ins["w_sc"][m, 0], ZB, 0, list(range(8)), 0, True, True),
                  (ins["w_sc"][m, 1], ZB, 1, list(range(8)), 1, True, True)], evac_merge(m))
        W0 = len(units)
        y_tok = {}

        def evac_wo(m):
            def ev(u, banks):
                i, a = low(banks[0])
                d = join(banks[0], i, a, Y[:, m, :], *ready_b[0], *ready_b[7], *ready_b[15])
                y_tok[m] = d
                add_square(0, m == 0, Y[:, m, :], d)
                yield
                u_tok[m] = [A(act(rr["U1"][:, m, :], X[:, m, :], ACT.Copy, scale=C("gpmlp", m)), x_tok[m], *merged),
                            A(act(rr["U2"][:, m, :], Y[:, m, :], ACT.Copy, scale=gpp[:, m:m + 1]), d, gpp_tok)]
                y_tok[m] = A(act(Y[:, m, :], Y[:, m, :], ACT.Copy, scale=C("gpost", m)), d)
            return ev
        u_tok = {}
        gpp_tok = D(tt(gpp[:, :], col[:, COL0["gpost"]:COL0["gpost"] + 16], col[:, COL0["gpmlp"]:COL0["gpmlp"] + 16],
                       ALU.mult), ld["col"])
        for m in range(16):
            unit2(ins["w_o"], m, ZA, evac_wo(m))
        M0 = len(units)

        def post_mix():
            r = rstd(0, R1[:, :], 2048, ln["x"])
            last = mm_half[units[M0 - 1][1] - 1]
            U1, U2 = rr["U1"], rr["U2"]
            hi_tok = {}

            def lows(n):
                k = slice(2 * n, 2 * n + 2)
                d = D(tt(ZA[:, k, 256:512], U2[:, k, :], ZA[:, k, 0:256].bitcast(F32), ALU.subtract), hi_tok[n])
                ready_a[2 * n] = ready_a[2 * n + 1] = [hi_tok[n], d]
            for n in range(8):
                k = slice(2 * n, 2 * n + 2)
                d = D(tt(U2[:, k, :], U2[:, k, :], R1[:, :].unsqueeze(1).broadcast_to([128, 2, T]), ALU.mult), r,
                      *u_tok[2 * n], *u_tok[2 * n + 1])
                t = (P if n % 2 else D)(tt(U2[:, k, :], U2[:, k, :], U1[:, k, :], ALU.add), d)
                hi_tok[n] = A(act(ZA[:, k, 0:256], U2[:, k, :], ACT.Copy), t, last)
                if n:
                    lows(n - 1)
            lows(7)
            rtok["R1"] = r
        at(pre, M0, post_mix)

        def warm_sqrt():
            A(act(warm[:, :], gpp[:, 0:1], ACT.Sqrt, scale=0.0), gpp_tok)
        at(post, M0 - 3, warm_sqrt)

        def norm_mlp_a():
            for n in range(4):
                k = slice(4 * n, 4 * n + 4)
                d = D(tt(Y[:, k, :], Y[:, k, :], R1[:, :].unsqueeze(1).broadcast_to([128, 4, T]), ALU.mult), rtok["R1"],
                      y_tok[4 * n + 3])
                p = P(tt(X[:, k, :], X[:, k, :], Y[:, k, :], ALU.add), d, *u_tok[4 * n + 3], x_tok[4 * n + 3])
                t = A(act(Y[:, k, :], X[:, k, :], ACT.Square), p)
                for m in range(4 * n, 4 * n + 4):
                    x_tok[m], y_tok[m] = p, t
            acc_tok[0] = D(lambda e: e.tensor_reduce(acc[0][:, :], Y[:, :, :].rearrange("p k t -> p t k"), AX.X, ALU.add),
                           t, *acc_free[0])
            for m in range(16):
                y_tok[m] = acc_tok[0]

        def norm_mlp_b():
            rtok["R3"] = rstd(0, R3[:, :], 2048, x_tok[15])
        at(post, M0, norm_mlp_a)
        at(post, M0 + 3, norm_mlp_b)
        hold[M0] = M0 + 4

        def evac_up(c, j):
            def ev(u, banks):
                i, a = low(banks[0])
                s, d = join_s(banks[0], i, a)
                b = tS.bufs[s]
                p = P(tt(b[:, :], b[:, :], R3[:, :], ALU.mult), d, rtok["R3"])
                yield
                d = D(stt(b[:, :], b[:, :], 0.0, b[:, :], ALU.max, ALU.mult), p)
                yield
                before = [d_last[c - 1]] if c else [mm_half[units[W0 - 1][1] - 1]]
                tS.free[s] = [split(ZB, ready_b, j, b[:, :], None, d, *before)]
            return ev

        d_last = {}

        def evac_down(c, m):
            def ev(u, banks):
                i, a = low(banks[0])
                b = tA.bufs[i]
                if c:
                    a = P(tt(b[:, :], b[:, :], Y[:, m, :], ALU.add), a, y_tok[m])
                d = join(banks[0], i, a, Y[:, m, :], y_tok[m])
                y_tok[m] = d
                yield
                if c == 3:
                    add_square(0, m == 0, Y[:, m, :], d)
                    y_tok[m] = A(act(Y[:, m, :], Y[:, m, :], ACT.Copy, scale=C("gpostmlp", m)), d)
            return ev

        for c in range(4):
            for j in range(16):
                unit2(ins["w_up"], 16 * c + j, ZA, evac_up(c, j))
            s = len(units)
            for m in range(16):
                unit2(ins["w_down"], m, ZB, evac_down(c, m), kbase=2 * c)
            at(pre, len(units), lambda c=c, s=s: d_last.__setitem__(c, mm_half[units[s + 15][1] - 1]))

        def finish():
            r = rstd(0, R1[:, :], 2048)
            for n in range(8):
                k = slice(2 * n, 2 * n + 2)
                d = D(tt(Y[:, k, :], Y[:, k, :], R1[:, :].unsqueeze(1).broadcast_to([128, 2, T]), ALU.mult), r,
                      y_tok[2 * n], y_tok[2 * n + 1])
                t = (P if n % 3 == 1 else D)(tt(X[:, k, :], X[:, k, :], Y[:, k, :], ALU.add), d, x_tok[2 * n + 1])
                o = SP.dma(lambda e, k=k: e.dma_start(out[:, k, :], X[:, k, :]), s_out, n + 1, t)
            SP.wait(o)

        def prelude():
            start_x()
            sqx = rr["sqx"]
            for i in range(4):
                k = slice(xcut[i], xcut[i + 1])
                t = P(tt(sqx[:, k, :], X[:, k, :], X[:, k, :], ALU.mult), ldx[i])
            ini['sqx'] = acc_tok[0] = D(lambda e: e.tensor_reduce(acc[0][:, :], sqx[:, :, :].rearrange("p k t -> p t k"),
                                                                  AX.X, ALU.add), t)
            lam = col[:, COL0["lam"]:COL0["lam"] + 8]
            t = A(act(sp4[:, 0, :], lam, ACT.Abs), ld["col"])
            t = A(act(sp4[:, 0, :], sp4[:, 0, :], ACT.Exp, scale=-1.0), t)
            t = A(act(sp4[:, 0, :], sp4[:, 0, :], ACT.Ln, bias=1.0), t)
            t2 = D(ts(sp4[:, 1, :], lam, -1.0, ALU.mult, 0.0, ALU.max), ld["col"])
            t = D(tt(sp4[:, 1, :], sp4[:, 1, :], sp4[:, 0, :], ALU.add), t, t2)
            t = D(ts(sp4[:, 2, :], sp4[:, 1, :], 4.0, ALU.mult), t)
            ini['sp'] = D(ts(sp4[:, 1, :], sp4[:, 1, :], -8.0, ALU.mult), t)

        prelude()
        N = len(units)
        nxt = 3
        waiting = []
        for u in range(N + 1):
            if u:
                waiting.append((u - 1, banks))
            evs = []
            while waiting and hold.get(waiting[0][0], 0) <= u:
                w, b = waiting.pop(0)
                evs.append(units[w][2](u, b))
            for ev in evs[:-1]:
                for _ in ev:
                    pass
            ev = evs[-1] if evs else iter(())
            next(ev, None)
            prep(nxt)
            next(ev, None)
            prep(nxt + 1)
            nxt += 2
            next(ev, None)
            for fn in pre.get(u, []):
                fn()
            if u < N:
                banks = products(u)
                for fn in post.get(u, []):
                    fn()
        finish()

        block = ctx.enter_context(nc.Block())

        @block.sync
        def _(e):
            SP.run(e)

        @block.scalar
        def _(e):
            A.run(e)

        @block.vector
        def _(e):
            D.run(e)

        @block.gpsimd
        def _(e):
            P.run(e)

        @block.tensor
        def _(e):
            PE.run(e)


def _gemm(w):
    K, N = w.shape
    return w.reshape(K // 1024, 8, 128, N // 128, 128).transpose(3, 0, 2, 1, 4).reshape(N // 128, K // 1024, 128, 1024)


def _constants(np):
    f = np.float32
    c = np.zeros((128, CEND + 768), f)
    i = np.arange(128)
    c[:, CI:CI + 128] = np.eye(128, dtype=f)
    c[:, CTRI:CTRI + 128] = (i[:, None] >= i[None, :]).astype(f)
    c[:, CONE:CONE + 128] = 1.0
    c[:, CIOTA:CIOTA + 128] = i[None, :]
    for g, w in enumerate((2, 4, 8, 16)):
        c[:, CRC + 16 * g:CRC + 16 * g + 16] = 1.0 / np.minimum(np.arange(1, 17), w).astype(f)
    before = (i[:, None] < i[None, :]).astype(f)
    mask = np.concatenate([before, np.ones((128, 128), f), before], axis=1)
    c[:, CEND:CEND + 384] = mask
    c[:, CEND + 384:CEND + 768] = np.where(mask > 0, f(0), f(-1.0e38))
    return c


def kernel(**inputs):
    import numpy as np
    import concourse.bacc as _bacc
    from concourse.bass_utils import run_bass_kernel_spmd as _run

    v = {k: np.asarray(x) for k, x in inputs.items()}

    def cols(a):
        return a.reshape(-1, 128).T

    named = {"g1": v["norm1_g"], "pool_b": v["pool_b"], "pool_scale": v["pool_scale"], "conv_w": v["conv_w"],
             "conv_b": v["conv_b"], "gab": v["gate_a_b"], "gxb": v["gate_x_b"], "lam": v["lru_lambda"],
             "g2": v["norm2_g"], "gf": v["norm_f_g"], "gpm": v["g_pre_mix_2"], "b_in": v["b_in_2"],
             "w_dw": v["w_dw_2"], "b_dw": v["b_dw_2"], "gcl": v["g_conv_ln_2"], "bcl": v["b_conv_ln_2"],
             "gpost": v["g_post_mix_2"], "gpmlp": v["g_pre_mlp_2"], "gpostmlp": v["g_post_mlp_2"]}
    packed = [cols(named[n]) for n, _ in COLS[:-1]] + [np.full((128, 1), 1e-6, np.float32)]
    keys = np.stack([v["peer_keys1"][0], v["peer_keys2"][0]], axis=1)
    arrays = {
        "xT": v["x"][0].reshape(256, 16, 128).transpose(2, 1, 0),
        "con": _constants(np),
        "cols": np.concatenate(packed, axis=1),
        "gaw": v["gate_a_w"][0].transpose(1, 0, 2),
        "gxw": v["gate_x_w"][0].transpose(1, 0, 2),
        "poolw": v["pool_w"][0].reshape(4, 2, 128, 256).transpose(2, 0, 1, 3),
        "keys": keys.reshape(16, 128, 128).transpose(2, 0, 1),
        "w_in": _gemm(v["w_in"][0]),
        "w_out": _gemm(v["w_out"][0]),
        "wq": _gemm(v["peer_wq"][0]),
        "pu": v["peer_u"][0].reshape(128, 128, 2, 8, 128).transpose(1, 2, 4, 3, 0).reshape(128, 2, 128, 1024),
        "pv": v["peer_v"][0].reshape(128, 16, 8, 16, 128).transpose(3, 1, 0, 2, 4).reshape(16, 16, 128, 1024),
        "w_in2": _gemm(v["w_in_2"][0]),
        "w_sc": np.stack([_gemm(v["w_sb_out_2"][0])[:, 0], _gemm(v["w_conv_out_2"][0])[:, 0]], axis=1),
        "w_o": _gemm(v["w_o_2"][0]),
        "w_up": _gemm(v["w_up_2"][0]),
        "w_down": _gemm(v["w_down_2"][0]),
    }
    nc = _bacc.Bacc("TRN2", target_bir_lowering=False, num_devices=1)
    given, aps = {}, {}
    for name, a in arrays.items():
        a = np.ascontiguousarray(a)
        given[f"in_{name}"] = a
        aps[name] = nc.dram_tensor(f"in_{name}", a.shape, mybir.dt.from_np(a.dtype), kind="ExternalInput").ap()
    out = nc.dram_tensor("out_0", (128, 16, 256), F32, kind="ExternalOutput").ap()
    build(nc, aps, out)
    r = _run(nc, [given], core_ids=[0])
    got = np.asarray(r.results[0]["out_0"])
    return np.ascontiguousarray(got.transpose(2, 1, 0).reshape(1, 256, 2048))
```

```python
from contextlib import ExitStack

import concourse.bass as bass
from concourse import mybir
from concourse.alu_op_type import AluOpType as ALU

F32 = mybir.dt.float32
F32R = mybir.dt.float32r
U32 = mybir.dt.uint32
ACT = mybir.ActivationFunctionType
AX = mybir.AxisListType

T = 256
NRAW = 3
NW = 5
HALF = 8 * 128
TAPS = 31

COLS = [("g1", 16), ("pool_b", 8), ("pool_scale", 8), ("conv_w", 32), ("conv_b", 8), ("gab", 8), ("gxb", 8),
        ("lam", 8), ("g2", 16), ("gf", 16), ("gpm", 16), ("b_in", 72), ("w_dw", 8 * TAPS), ("b_dw", 8),
        ("gcl", 8), ("bcl", 8), ("gpost", 16), ("gpmlp", 16), ("gpostmlp", 16), ("eps", 1), ("eps16", 1)]
COL0 = {}
NCOL = 0
for _n, _c in COLS:
    COL0[_n] = NCOL
    NCOL += _c

CI, CTRI, CONE, CIOTA, CRC, CEND = 0, 128, 256, 384, 512, 576


class Engine:

    def __init__(self, sem):
        self.sem, self.n, self.ops, self.waited = sem, 0, [], {}

    def wait(self, *tokens):
        for sem, value in tokens:
            if self.waited.get(sem.name, 0) < value:
                self.waited[sem.name] = value
                self.ops.append(lambda e, sem=sem, value=value: e.wait_ge(sem, value))

    def __call__(self, fn, *tokens):
        self.wait(*tokens)
        self.n += 1
        sem = self.sem
        self.ops.append(lambda e: fn(e).then_inc(sem, 1))
        return (self.sem, self.n)

    def dma(self, fn, sem, count, *tokens):
        self.wait(*tokens)
        self.ops.append(lambda e: fn(e).then_inc(sem, 16))
        return (sem, 16 * count)

    def run(self, e):
        for op in self.ops:
            op(e)


class Ring:

    def __init__(self, bufs):
        self.bufs, self.free, self.at = bufs, [[] for _ in bufs], -1

    def next(self):
        self.at = (self.at + 1) % len(self.bufs)
        return self.at


def build(nc, ins, out):
    ctx = ExitStack()
    with ctx:
        def sb(name, shape, dt=F32):
            return ctx.enter_context(nc.sbuf_tensor(name, shape, dt))

        def sem(name):
            return ctx.enter_context(nc.semaphore(name))

        def region(nbytes, name, *layouts):
            out = {}
            for layout in layouts:
                with ExitStack() as c:
                    for n, shape, dt in layout:
                        out[n] = c.enter_context(nc.sbuf_tensor(n, shape, dt))
            sb(name, [128, nbytes // 4])
            return out

        raw = [sb(f"raw{i}", [128, HALF]) for i in range(NRAW)]
        hi = [sb(f"hi{i}", [128, 8, 128], F32R) for i in range(NW)]
        lo = [sb(f"lo{i}", [128, 8, 128], F32R) for i in range(NW)]
        ZA = sb("ZA", [128, 16, 512], F32R)
        X = sb("X", [128, 16, T])
        zb = region(32768, "zb_mem",
                    [("ZB", [128, 16, 512], F32R)],
                    [("zb_pad0", [128, 16, T], F32), ("S1", [128, 8, T], F32), ("W1", [128, 8, T], F32)],
                    [("stage0", [128, 8, 16, 16], F32), ("stage1", [128, 8, 16, 16], F32),
                     ("oneA0", [128, 8, 128], F32), ("oneA1", [128, 8, 128], F32),
                     ("IJG", [128, 3, T], F32), ("TS", [128, 2, 128], F32), ("TP", [128, 2, 128], U32),
                     ("sel", [128, 3, 2, 128], F32)],
                    [("qkv", [128, 4, 3, T], F32), ("VT", [128, 4, T], F32), ("zs0", [128, 2, 384], F32),
                     ("zs1", [128, 2, 384], F32), ("sp0", [128, 2, 384], F32), ("sp1", [128, 2, 384], F32),
                     ("mask", [128, 384], F32), ("neg", [128, 384], F32)])
        ry = region(16384, "y_mem",
                    [("Y", [128, 16, T], F32)],
                    [("poolw", [128, 4, 2, 256], F32), ("gaw", [128, 8, 128], F32), ("gxw", [128, 8, 128], F32)],
                    [("y_pad1", [128, 8, T], F32), ("upa", [128, 2, 272], F32), ("upb", [128, 2, 272], F32)],
                    [("y_pad0", [128, 8, T], F32), ("keys", [128, 16, 128], F32)],
                    [("O", [128, 8, T], F32), ("CV", [128, 8, T], F32)])
        rr = region(39 * 1024, "rr_mem",
                    [("XC", [128, 8, T], F32), ("rg", [128, 8, T], F32), ("ig", [128, 8, T], F32),
                     ("gl", [128, 8, T], F32), ("XL0", [128, 260], F32), ("XL1", [128, 260], F32),
                     ("UP0", [128, 2, 272], F32), ("UP1", [128, 2, 272], F32)],
                    [("rr_pad0", [128, 8, T], F32), ("sqx", [128, 16, T], F32)],
                    [("A1", [128, 16, T], F32), ("Gc", [128, T, 16], F32)],
                    [("eq1_", [128, 8, 16, 16], F32), ("Vk", [128, 2, 8, 2, 16], F32),
                     ("Ik", [128, 2, 8, 2, 16], U32), ("If", [128, 2, 8, 2, 16], F32),
                     ("mr0", [128, 256], F32), ("mr1", [128, 256], F32)],
                    [("eq1", [128, 8, 16, 16], F32), ("rr_pad5", [128, 8, T], F32), ("eq0", [128, 8, 16, 16], F32)],
                    [("rr_pad2", [128, 16, T], F32), ("rr_pad3", [128, 16, T], F32),
                     ("cd0", [128, 2, 64], F32), ("cd1", [128, 2, 64], F32), ("dg", [128, 4, 256], F32),
                     ("tpf", [128, 2, 128], F32), ("sm", [128, 4, 16], F32)],
                    [("rr_pad4", [128, 24, T], F32), ("oneB0", [128, 8, 128], F32), ("oneB1", [128, 8, 128], F32)],
                    [("U1", [128, 16, T], F32), ("U2", [128, 16, T], F32)],
                    [("SGS", [128, 16, T], F32), ("SGC", [128, 16, T], F32),
                     ("UC0", [128, 288], F32), ("UC1", [128, 288], F32), ("UC2", [128, 288], F32),
                     ("UC3", [128, 288], F32), ("UC4", [128, 288], F32)])
        con = sb("con", [128, CEND])
        col = sb("col", [128, NCOL])
        UP = [rr["UP0"], rr["UP1"]]
        upa, upb = ry["upa"], ry["upb"]
        sp4 = sb("sp4", [128, 3, 8])
        gpp, warm = sb("gpp", [128, 16]), sb("warm", [128, 1])
        Rn = [sb(f"R{i}", [128, T]) for i in range(3)]
        acc = [sb(f"acc{i}", [128, T]) for i in range(2)]
        tA = Ring([sb(f"tA{i}", [128, T]) for i in range(3)])
        tS = Ring([sb(f"tS{i}", [128, T]) for i in range(4)])
        tQ = Ring([sb(f"tQ{i}", [128, T]) for i in range(2)])
        GB = Ring([ctx.enter_context(nc.psum_tensor(f"G{i}", [128, 512], F32)) for i in range(4)])
        MB = Ring([ctx.enter_context(nc.psum_tensor(f"M{i}", [128, 512], F32)) for i in range(4)])
        scr = nc.dram_tensor("g_scratch", [8, 128, T * 16], F32, kind="Internal").ap()
        ident, tri, ones, iota = (con[:, c:c + 128] for c in (CI, CTRI, CONE, CIOTA))
        iota16 = con[:, CIOTA:CIOTA + 16]
        ZB, Y = zb["ZB"], ry["Y"]

        def C(name, i=0):
            return col[:, COL0[name] + i:COL0[name] + i + 1]

        PE, A, D, P = (Engine(sem(n)) for n in ("s_pe", "s_act", "s_dve", "s_pool"))
        SP = Engine(sem("s_sp"))
        s_raw = [sem(f"s_raw{i}") for i in range(NRAW)]
        s_in = {n: sem(f"s_{n}") for n in ("con", "col", "mask", "poolw", "gaw", "gxw", "keys")}
        s_x = [sem(f"s_x{i}") for i in range(4)]
        s_st = [sem("s_st0"), sem("s_st1")]
        s_gc, s_out = sem("s_gc"), sem("s_out")
        s_gh = [sem("s_gh0"), sem("s_gh1")]

        def tt(o, a, b, op):
            return lambda e: e.tensor_tensor(o, a, b, op)

        def ts(o, a, s1, op0, s2=None, op1=None):
            if op1 is None:
                return lambda e: e.tensor_scalar(o, a, s1, None, op0)
            return lambda e: e.tensor_scalar(o, a, s1, s2, op0, op1)

        def stt(o, a, s, b, op0, op1):
            return lambda e: e.scalar_tensor_tensor(out=o, in0=a, scalar=s, in1=b, op0=op0, op1=op1)

        def act(o, i, f, **k):
            return lambda e: e.activation(o, i, f, **k)

        def mm(o, l, r, start, stop):
            return lambda e: e.matmul(o, l, r, start=start, stop=stop, skip_group_check=True)

        def many(*fns):
            def run(e):
                for f in fns:
                    last = f(e)
                return last
            return run

        A(act(warm[:, :], warm[:, :], ACT.Copy), D(lambda e: e.memset(warm[:, :], 0.0)))

        ld = {}
        xcut = (0, 1, 5, 10, 16)
        ldx = []
        for i in range(4):
            ldx.append(A.dma(lambda e, i=i: e.dma_start(X[:, xcut[i]:xcut[i + 1], :], ins["xT"][:, xcut[i]:xcut[i + 1], :]),
                             s_x[i], 1))
            if i == 0:
                ld["col"] = A.dma(lambda e: e.dma_start(col[:, :], ins["cols"]), s_in["col"], 1)
        ld["con"] = A.dma(lambda e: e.dma_start(con[:, :], ins["con"][:, 0:CEND]), s_in["con"], 1)

        def load_gates():
            ld["gaw"] = A.dma(lambda e: e.dma_start(ry["gaw"][:, :, :], ins["gaw"]), s_in["gaw"], 1)
            ld["gxw"] = A.dma(lambda e: e.dma_start(ry["gxw"][:, :, :], ins["gxw"]), s_in["gxw"], 1)

        def load_poolw():
            ld["poolw"] = A.dma(lambda e: e.dma_start(ry["poolw"][:, :, :, :], ins["poolw"]), s_in["poolw"], 1)

        halves = []
        units = []

        def unit(hs, evac):
            a = len(halves)
            halves.extend(hs)
            units.append((a, len(halves), evac))

        def unit2(w, m, Z, evac, order=((0, range(8)), (1, range(8))), kbase=0):
            hs = []
            for n, (kh, kks) in enumerate(order):
                hs.append((w[m, kbase + kh], Z, kh, list(kks), 0, n == 0, n == 1))
            unit(hs, evac)

        ready_a, ready_b = [[] for _ in range(16)], [[] for _ in range(16)]
        mm_half = {}
        w_tok = {}

        def prep(h):
            if h >= len(halves):
                return
            r, w = h % NRAW, h % NW
            src = halves[h][0]
            ld_tok = SP.dma(lambda e: e.dma_start(raw[r][:, :], src), s_raw[r], h // NRAW + 1,
                            *(w_tok[h - NRAW] if h >= NRAW else []))
            free = [mm_half[h - NW]] if h >= NW else []
            rw = raw[r][:, :].rearrange("p (k n) -> p k n", k=8)
            a = A(act(hi[w][:, :, :], rw, ACT.Copy), ld_tok, *free)
            c = 7 if h == 2 * M0 + 3 else pool_share(h // 2)
            toks = [a]
            if c < 8:
                toks.append(D(tt(lo[w][:, 0:8 - c, :], rw[:, 0:8 - c, :], hi[w][:, 0:8 - c, :].bitcast(F32), ALU.subtract), a))
            if c:
                toks.append(P(tt(lo[w][:, 8 - c:8, :], rw[:, 8 - c:8, :], hi[w][:, 8 - c:8, :].bitcast(F32), ALU.subtract), a))
            w_tok[h] = toks

        def pool_share(u):
            return 0 if u < 3 else 5 if 42 <= u < U0 + 4 else 2 if U0 + 6 <= u < U0 + 11 else 4 if U0 + 4 <= u < U0 + 28 else 2

        paired = {}

        def products(u):
            if u in PAIRS:
                return products_pair(u)
            if u in paired:
                return paired.pop(u)
            a, b, _ = units[u]
            banks = {}
            for h in range(a, b):
                _, Z, kh, kks, bk, start, stop = halves[h]
                if bk not in banks:
                    banks[bk] = GB.next()
                g = banks[bk]
                G = GB.bufs[g]
                PE.wait(*w_tok[h])
                if start:
                    PE.wait(*GB.free[g])
                ready = ready_a if Z is ZA else ready_b
                w = h % NW
                for n, kk in enumerate(kks):
                    k = 8 * kh + kk
                    PE.wait(*ready[k])
                    f = many(mm(G[:, 0:512], hi[w][:, kk, :], Z[:, k, :], start and n == 0, False),
                             mm(G[:, 0:256], lo[w][:, kk, :], Z[:, k, 0:256], False, stop and n == 7))
                    if n < 7:
                        PE.ops.append(f)
                    else:
                        mm_half[h] = PE(f)
                if h == a:
                    for fn in mid.get(u, []):
                        fn()
            return [(GB.bufs[banks[k]], banks[k], mm_half[b - 1]) for k in sorted(banks)]

        def products_pair(u):
            gs = [GB.next(), GB.next()]
            for g in gs:
                PE.wait(*GB.free[g])
            for half in range(2):
                hs = [units[u + i][0] + half for i in range(2)]
                for h in hs:
                    PE.wait(*w_tok[h])
                _, Z, kh, kks, _, _, _ = halves[hs[0]]
                ready = ready_a if Z is ZA else ready_b
                for n, kk in enumerate(kks):
                    k = 8 * kh + kk
                    PE.wait(*ready[k])
                    for g, h in zip(gs, hs):
                        G, w = GB.bufs[g], h % NW
                        first, last = half == 0 and n == 0, half == 1 and n == 7
                        f = many(mm(G[:, 0:512], hi[w][:, kk, :], Z[:, k, :], first, False),
                                 mm(G[:, 0:256], lo[w][:, kk, :], Z[:, k, 0:256], False, last))
                        if n < 7:
                            PE.ops.append(f)
                        else:
                            mm_half[h] = PE(f)
                if half == 0:
                    for fn in mid.get(u, []) + mid.get(u + 1, []):
                        fn()
            b = [(GB.bufs[g], g, mm_half[hs[i]]) for i, g in enumerate(gs)]
            paired[u + 1] = [b[1]]
            return [b[0]]

        nxt, ahead = [3], [0]

        def advance():
            prep(nxt[0])
            nxt[0] += 1

        def step():
            if ahead[0]:
                ahead[0] -= 1
            else:
                advance()

        def low(bank, scale=None):
            G, g, tok = bank
            i = tA.next()
            k = {} if scale is None else {"scale": scale}
            return i, A(act(tA.bufs[i][:, :], G[:, 256:512], ACT.Copy, **k), tok, *tA.free[i])

        def join(bank, i, a, dst, *tokens):
            G, g, tok = bank
            d = D(tt(dst, G[:, 0:256], tA.bufs[i][:, :], ALU.add), a, *tokens)
            GB.free[g] = [d]
            tA.free[i] = [d]
            return d

        def join_s(bank, i, a):
            j = tS.next()
            return j, join(bank, i, a, tS.bufs[j][:, :], *tS.free[j])

        def split(Z, ready, k, src, scale, *tokens):
            if scale is None:
                a = A(act(Z[:, k, 0:256], src, ACT.Copy), *tokens)
                d = D(tt(Z[:, k, 256:512], src, Z[:, k, 0:256].bitcast(F32), ALU.subtract), a)
            else:
                a = A(act(Z[:, k, 0:256], src, ACT.Copy, scale=scale), *tokens)
                d = D(stt(Z[:, k, 256:512], src, scale, Z[:, k, 0:256].bitcast(F32), ALU.mult, ALU.subtract), a)
            ready[k] = [a, d]
            return d

        acc_free = [[], []]
        acc_tok = [None, None]

        def add_square(n, first, src, *tokens):
            if first:
                acc_tok[n] = A(act(acc[n][:, :], src, ACT.Square), *tokens, *acc_free[n])
                return acc_tok[n]
            q = tQ.next()
            t = A(act(tQ.bufs[q][:, :], src, ACT.Square), *tokens, *tQ.free[q])
            acc_tok[n] = P(tt(acc[n][:, :], acc[n][:, :], tQ.bufs[q][:, :], ALU.add), t, acc_tok[n])
            tQ.free[q] = [acc_tok[n]]
            return t

        def mean_of(src, *tokens):
            m = MB.next()
            t = PE(mm(MB.bufs[m][:, 0:256], ones, src, True, True), *tokens, *MB.free[m], ld["con"])
            return m, t

        def rms(n, dst, count, *tokens, also=None):
            if also is None:
                m, t = mean_of(acc[n][:, :], acc_tok[n])
            else:
                q, tok = also
                m = MB.next()
                M = MB.bufs[m][:, 0:256]
                PE(mm(M, ones, acc[n][:, :], True, False), acc_tok[n], *MB.free[m], ld["con"])
                t = PE(mm(M, ones, tQ.bufs[q][:, :], False, True), tok)
                tQ.free[q] = [t]
            acc_free[n] = [t]
            a = A(act(dst, MB.bufs[m][:, 0:256], ACT.Sqrt, scale=1.0 / count, bias=C("eps")), t, *tokens)
            MB.free[m] = [a]
            return a

        def rstd(n, dst, count, *tokens, also=None):
            a = rms(n, dst, count, *tokens, also=also)
            return D(lambda e: e.reciprocal(dst, dst), a)

        early, pre, mid, post, hold = {}, {}, {}, {}, {}

        def at(where, step, fn):
            where.setdefault(step, []).append(fn)

        R1, R2, R3 = Rn
        rtok = {}
        XC, rg, ig, gl, S1, W1 = (rr[n] if n in rr else zb[n] for n in ("XC", "rg", "ig", "gl", "S1", "W1"))
        XL = Ring([rr["XL0"], rr["XL1"]])
        UPr = Ring(UP)
        pad_tok = [P(lambda e, b=b: e.memset(b[:, 0:3], 0.0)) for b in (rr["XL0"], rr["XL1"])]
        upad = [P(lambda e, b=b: e.memset(b[:, :, 0:16], 0.0)) for b in UP]

        def start_x():
            for i in range(4):
                for k in range(xcut[i], xcut[i + 1]):
                    split(ZA, ready_a, k, X[:, k, :], C("g1", k), ldx[i], ld["col"])
                k = slice(xcut[i], xcut[i + 1])
                sq_tok.append(P(tt(sqx[:, k, :], X[:, k, :], X[:, k, :], ALU.mult), ldx[i]))
                if i == 0:
                    prep(0)
                if i == 1:
                    prep(1)
                if i == 3:
                    prep(2)

        ini = {}
        sq_tok = []
        sqx = rr["sqx"]

        at(post, 0, load_gates)
        at(post, 3, load_poolw)

        def first_sum(n):
            q = tQ.next()
            src = sqx[:, 8 * n:8 * n + 8, :].rearrange("p k t -> p t k")
            ini[n] = q, D(lambda e: e.tensor_reduce(tQ.bufs[q][:, :], src, AX.X, ALU.add), sq_tok[2 + n])
        at(early, 0, lambda: first_sum(0))
        at(pre, 0, lambda: first_sum(1))

        def first_norm():
            q, t = ini[0]
            m = MB.next()
            M = MB.bufs[m][:, 0:256]
            t = PE(mm(M, ones, tQ.bufs[q][:, :], True, False), t, ld["con"])
            tQ.free[q] = [t]
            q, t = ini[1]
            ini["sqx"] = t
            t = PE(mm(M, ones, tQ.bufs[q][:, :], False, True), t)
            tQ.free[q] = [t]
            a = A(act(R1[:, :], M, ACT.Sqrt, scale=1.0 / 2048, bias=C("eps")), t)
            MB.free[m] = [a]
            rtok["R1"] = D(lambda e: e.reciprocal(R1[:, :], R1[:, :]), a)
        at(post, 1, first_norm)
        hold[0] = 2

        sg_tok, xc_tok, gl_tok = {}, {}, {}

        def evac_lru_x(j):
            def ev(u, banks):
                i, a = low(banks[0])
                x = XL.next()
                b = XL.bufs[x]
                d = join(banks[0], i, a, b[:, 3:259], pad_tok[x], *XL.free[x])
                p = P(tt(b[:, 3:259], b[:, 3:259], R1[:, :], ALU.mult), d, rtok["R1"])
                yield
                c = D(ts(XC[:, j, :], b[:, 0:256], C("conv_w", j), ALU.mult, C("conv_b", j), ALU.add), p)
                for k in range(1, 4):
                    c = D(stt(XC[:, j, :], b[:, k:k + 256], C("conv_w", 8 * k + j), XC[:, j, :], ALU.mult, ALU.add), c)
                XL.free[x] = [c]
                xc_tok[j] = c

                def gates():
                    m = MB.next()
                    M = MB.bufs[m]
                    t = PE(many(mm(M[:, 0:256], ry["gaw"][:, j, :], XC[:, j, :], True, True),
                                mm(M[:, 256:512], ry["gxw"][:, j, :], XC[:, j, :], True, True)),
                           xc_tok[j], ld["gaw"], ld["gxw"], *MB.free[m])
                    a = A(act(rg[:, j, :], M[:, 0:256], ACT.Sigmoid, bias=C("gab", j)), t, ini['sqx'])
                    b = A(act(ig[:, j, :], M[:, 256:512], ACT.Sigmoid, bias=C("gxb", j)), t)
                    MB.free[m] = [b]
                    sg_tok[j] = b
                at(post, u + 1, gates)
            return ev

        def evac_gate(j):
            def ev(u, banks):
                i, a = low(banks[0])
                s, d = join_s(banks[0], i, a)
                b = tS.bufs[s]
                p = P(tt(b[:, :], b[:, :], R1[:, :], ALU.mult), d)
                yield
                a = A(act(b[:, :], b[:, :], ACT.Gelu_apprx_tanh), p)
                p = P(tt(b[:, :], b[:, :], XC[:, j, :], ALU.mult), a, lru[f"h{j}"])
                yield
                tS.free[s] = [split(ZB, ready_b, 8 + j, b[:, :], None, p, lru["h7"])]
            return ev

        def evac_pool(g, mi):
            def ev(u, banks):
                i, a = low(banks[0])
                if mi == 0:
                    UPr.next()
                x = UPr.at
                b = UPr.bufs[x]
                d = join(banks[0], i, a, b[:, mi, 16:272], *upad, *UPr.free[x])
                p = P(tt(b[:, mi, 16:272], b[:, mi, 16:272], R1[:, :], ALU.mult), d)
                up_tok.setdefault(g, []).append(p)
                yield
                if mi == 1:
                    pool_tail(g, x, b, up_tok[g], u)
            return ev

        up_tok = {}
        yw_free = [[], []]
        up_busy = [sg_tok]

        def pool_tail(g, x, b, toks, u):
            nonlocal up_busy
            src, t, w, n, bufs = b, toks, 1, 0, [upa, upb]
            while w < (2, 4, 8, 16)[g]:
                dst = bufs[n % 2]
                t = [D(tt(dst[:, :, 2 * w:272], src[:, :, 2 * w:272], src[:, :, w:272 - w], ALU.add), *t, *([sg_tok[7]] if up_busy == [sg_tok] else up_busy))]
                up_busy = []
                src, w, n = dst, 2 * w, n + 1
            dst = bufs[n % 2]
            rcg = con[:, CRC + 16 * g:CRC + 16 * g + 16].unsqueeze(1).broadcast_to([128, 2, 16])
            t1 = D(tt(dst[:, :, 16:32], src[:, :, 16:32], rcg, ALU.mult), *t, ld["con"])
            D(stt(dst[:, :, 32:272], src[:, :, 32:272], 1.0 / w, b[:, :, 32:272], ALU.mult, ALU.subtract), *t)
            t = [D(tt(dst[:, :, 16:32], dst[:, :, 16:32], b[:, :, 16:32], ALU.subtract), t1)]
            UPr.free[x] = t
            d_tok = t

            def dense():
                nonlocal up_busy
                m = MB.next()
                M = MB.bufs[m]
                fns = []
                for mi in range(2):
                    for ki in range(2):
                        fns.append(mm(M[:, 256 * mi:256 * mi + 256], ry["poolw"][:, g, ki, 128 * mi:128 * mi + 128],
                                      dst[:, ki, 16:272], ki == 0, ki == 1))
                t = PE(many(*fns), *d_tok, ld["poolw"], *MB.free[m])
                up_busy = [t]
                for mi in range(2):
                    k = 2 * g + mi
                    s = tS.next()
                    S = tS.bufs[s]
                    d = D(ts(S[:, :], M[:, 256 * mi:256 * mi + 256], C("pool_b", k), ALU.add, C("pool_scale", k), ALU.mult),
                          t, *tS.free[s])
                    MB.free[m] = [d]
                    tS.free[s] = [split(ZB, ready_b, k, S[:, :], None, d)]
            at(post, u + 1, dense)

        nU = 0
        for j in range(8):
            unit2(ins["w_in"], 8 + j, ZA, evac_lru_x(j))
        for g in (3, 2, 1, 0):
            for mi in range(2):
                unit2(ins["w_in"], 2 * g + mi, ZA, evac_pool(g, mi))
        for j in range(8):
            unit2(ins["w_in"], 16 + j, ZA, evac_gate(j))

        lru = {}

        def lru_decay(j0):
            for j in range(j0, j0 + 4):
                t = A(act(S1[:, j, :], rg[:, j, :], ACT.Tanh, scale=sp4[:, 2, j:j + 1]), sg_tok[j], ini['sp'])
                lru[f"a{j}"] = A(act(rg[:, j, :], rg[:, j, :], ACT.Exp, scale=sp4[:, 1, j:j + 1]), t)
        at(post, 9, lambda: lru_decay(0))
        at(post, 10, lambda: lru_decay(4))

        def lru_b0(h):
            s = S1[:, 2 * h:2 * h + 2, :]
            lru[f"q{h}"] = A(act(s, s, ACT.Sqrt), lru[f"a{2 * h + 1}"])

        def lru_b1(h):
            j = slice(2 * h, 2 * h + 2)
            s = S1[:, j, :]
            d = D(stt(s, rg[:, j, :], 1.0, s, ALU.add, ALU.mult), lru[f"q{h}"])
            p = P(tt(s, s, ig[:, j, :], ALU.mult), d)
            lru[f"b{h}"] = P(tt(s, s, XC[:, j, :], ALU.mult), p, xc_tok[2 * h + 1])
        at(post, 11, lambda: [lru_b0(h) for h in range(4)])
        for h in range(4):
            at(post, 12 + h, lambda h=h: lru_b1(h))

        def lru_scan(j):
            lru[f"h{j}"] = D(lambda e: e.tensor_tensor_scan(XC[:, j, :], rg[:, j, :], S1[:, j, :], 0.0, ALU.mult, ALU.add),
                             lru[f"a{j}"], lru[f"b{j // 2}"])
        for j in range(8):
            at(post, 13 + j // 2, lambda j=j: lru_scan(j))

        x_tok = {k: ldx[i] for i in range(4) for k in range(xcut[i], xcut[i + 1])}

        def evac_wout(m):
            def ev(u, banks):
                i, a = low(banks[0])
                s, d = join_s(banks[0], i, a)
                b = tS.bufs[s]
                p = P(tt(X[:, m, :], b[:, :], X[:, m, :], ALU.add), d)
                tS.free[s] = [p]
                x_tok[m] = p
                add_square(0, m == 0, X[:, m, :], p)
                yield
                yield
                split(ZA, ready_a, m, X[:, m, :], C("g2", m), p, mm_half[2 * 24 - 1])
            return ev

        order = ((0, (6, 7, 4, 5, 2, 3, 0, 1)), (1, range(8)))
        for m in range(16):
            unit2(ins["w_out"], m, ZB, evac_wout(m), order)

        def norm2():
            rtok["R2"] = rstd(0, R2[:, :], 2048)
        at(post, 41, norm2)
        hold[40] = 42

        ld_keys = {}

        def load_keys():
            ld_keys[0] = A.dma(lambda e: e.dma_start(ry["keys"][:, :, :], ins["keys"]), s_in["keys"], 1, up_busy[0], sg_tok[7])
        at(post, 30, load_keys)

        Vk, Ik, If, eqs = rr["Vk"], rr["Ik"], rr["If"], Ring([rr["eq0"], rr["eq1"]])
        TS, TP, sel, sm, IJG = zb["TS"], zb["TP"], zb["sel"], rr["sm"], zb["IJG"]
        mr = Ring([rr["mr0"], rr["mr1"]])
        cd = Ring([rr["cd0"], rr["cd1"]])
        QT = Ring([tS.bufs[0]])
        q_tok, q_buf, key_bank, key_tok = {}, {}, {}, {}
        NEG = -3.0e38
        zb_old = []

        def top16(jobs, width):
            rs = [mr.next() for _ in jobs]
            R = [mr.bufs[r][:, 0:width] for r in rs]
            d = [D(lambda e, v=v, src=src: e.max(v[:, 0:8], src), *toks) for src, v, i, toks in jobs]
            f = [D(lambda e, n=n, v=v, src=src: e.match_replace(R[n], v[:, 0:8], src, NEG), d[n], *mr.free[rs[n]])
                 for n, (src, v, i, toks) in enumerate(jobs)]
            for n, (src, v, i, toks) in enumerate(jobs):
                D(lambda e, i=i, v=v, src=src: e.max_index(i[:, 0:8], v[:, 0:8], src), d[n])
            g = [D(lambda e, n=n, v=v: e.max(v[:, 8:16], R[n]), f[n]) for n, (src, v, i, toks) in enumerate(jobs)]
            for n, (src, v, i, toks) in enumerate(jobs):
                last = D(lambda e, n=n, i=i, v=v: e.max_index(i[:, 8:16], v[:, 8:16], R[n]), g[n])
                mr.free[rs[n]] = [last]
            return last

        def evac_wq(h, half):
            def ev(u, banks):
                i, a = low(banks[0])
                s, d = join_s(banks[0], i, a)
                b = tS.bufs[s]
                p = P(tt(b[:, :], b[:, :], R2[:, :], ALU.mult), d, rtok["R2"])
                q_tok[h, half], q_buf[h, half] = p, s
                tS.free[s] = [p]

                def scores():
                    m = key_bank[h, half] = MB.next()
                    M = MB.bufs[m]
                    s = q_buf[h, half]
                    fns = [mm(M[:, 128 * t:128 * t + 128], tS.bufs[s][:, 128 * t:128 * t + 128],
                              ry["keys"][:, 2 * h + half, :], True, True) for t in range(2)]
                    key_tok[h, half] = PE(many(*fns), q_tok[h, half], ld_keys[0], *MB.free[m])
                    tS.free[s] = [key_tok[h, half]]
                at(post, u + 1, scores)

                def route():
                    m = key_bank[h, half]
                    M = MB.bufs[m]
                    rk[h, half] = top16([(M[:, 128 * t:128 * t + 128], Vk[:, t, h, half, :], Ik[:, t, h, half, :],
                                          [key_tok[h, half]]) for t in range(2)], 128)
                    MB.free[m] = [rk[h, half]]
                at(post, u + 2, route)
                if half == 1:
                    at(mid, u + 3, lambda: cand_sum(h))
                    at(post, u + 4, lambda: cand(h))
                yield
            return ev

        cand_jobs = {}
        rk, ck = {}, {}

        BLOCKS = ((0, 1, 16, 0), (1, 3, 8, 16), (4, 4, 4, 40), (8, 8, 1, 56))

        def cand_sum(h):
            c = cd.next()
            b = cd.bufs[c]
            for a0, na, nb, at0 in BLOCKS:
                o = b[:, :, at0:at0 + na * nb].rearrange("p t (a b) -> p t a b", a=na)
                v1 = Vk[:, :, h, 0, a0:a0 + na].unsqueeze(3).broadcast_to([128, 2, na, nb])
                v2 = Vk[:, :, h, 1, 0:nb].unsqueeze(2).broadcast_to([128, 2, na, nb])
                p = P(tt(o, v1, v2, ALU.add), rk[h, 0], rk[h, 1], *cd.free[c])
            cand_jobs[h] = c, [(b[:, t, :], TS[:, t, 16 * h:16 * h + 16], TP[:, t, 16 * h:16 * h + 16], [p])
                               for t in range(2)]

        def cand(h):
            c, jobs = cand_jobs[h]
            ck[h] = top16(jobs, 64)
            cd.free[c] = [ck[h]]

        for h in range(8):
            for half in range(2):
                unit2(ins["wq"], 2 * h + half, ZA, evac_wq(h, half))
        U0 = len(units)

        dec = {}

        def decode_a():
            for t in range(2):
                dec["if", t] = P(lambda e, t=t: e.tensor_copy(If[:, t, :, :, :], Ik[:, t, :, :, :]), rk[7, 1])
            p, m8, m12, m1 = (rr["dg"][:, n, :] for n in range(4))
            a = sel[:, 0, :, :].rearrange("p t k -> p (t k)")
            b = sel[:, 1, :, :].rearrange("p t k -> p (t k)")
            c = D(lambda e: e.tensor_copy(p, TP[:, :, :].rearrange("p t k -> p (t k)")), ck[7])
            t8 = D(ts(m8, p, 24.0, ALU.is_ge), c)
            t12 = D(ts(m12, p, 44.0, ALU.is_ge), c)
            t1 = D(ts(m1, p, -56.0, ALU.add, 0.0, ALU.max), c)
            t8 = D(stt(m8, p, 32.0, m8, ALU.is_ge, ALU.add), t8)
            t12 = D(stt(m12, p, 48.0, m12, ALU.is_ge, ALU.add), t12)
            ta = D(stt(a, p, 16.0, m1, ALU.is_ge, ALU.add), t1)
            t8 = D(stt(m8, p, 40.0, m8, ALU.is_ge, ALU.add), t8)
            t12 = D(stt(m12, p, 52.0, m12, ALU.is_ge, ALU.add), t12)
            t12 = D(stt(m12, p, 56.0, m12, ALU.is_ge, ALU.add), t12)
            ta = D(tt(a, a, m8, ALU.add), ta, t8)
            tb = D(stt(b, m8, 8.0, p, ALU.mult, ALU.add), t8)
            ta = D(tt(a, a, m12, ALU.add), ta, t12)
            tb = D(stt(b, m12, 12.0, b, ALU.mult, ALU.add), tb)
            tb = D(stt(b, m1, 15.0, b, ALU.mult, ALU.add), tb)
            tb = D(stt(b, a, -16.0, b, ALU.mult, ALU.add), ta, tb)
            dec["pb", 0] = dec["pb", 1] = tb

        def decode_b(t, half):
            q = eqs.next()
            eq = eqs.bufs[q]
            e3 = eq[:, :, :, :].rearrange("p h k a -> p (h k) a")
            io = iota16.unsqueeze(1).broadcast_to([128, 128, 16])
            d = D(tt(e3, sel[:, half, t, :].unsqueeze(2).broadcast_to([128, 128, 16]), io, ALU.is_equal),
                  dec["pb", t], *eqs.free[q])

            def pick():
                for E, k in ((P, slice(0, 4)), (D, slice(4, 8))):
                    rows = If[:, t, k, half, :].unsqueeze(2).broadcast_to([128, 4, 16, 16])
                    dec["pick", t, half, E is D] = E(tt(eq[:, k, :, :], eq[:, k, :, :], rows, ALU.mult), d, dec["if", t])

            def total():
                dst = rr["tpf"][:, half, :]
                dec["sel", t, half] = D(lambda e: e.tensor_reduce(dst, e3, AX.X, ALU.add),
                                        dec["pick", t, half, False], dec["pick", t, half, True],
                                        *([dec["turned", 0, half]] if t else []))
                eqs.free[q] = [dec["sel", t, half]]

            def turn():
                m = MB.next()
                M = MB.bufs[m]
                t1 = PE(lambda e: e.transpose(M[:, 0:128], rr["tpf"][:, half, :], ident), dec["sel", t, half], *MB.free[m])
                a = A(act(IJG[:, half, 128 * t:128 * t + 128], M[:, 0:128], ACT.Copy), t1)
                MB.free[m] = [a]
                dec["turned", t, half] = t1
                dec["ijg", t, half] = a
            return pick, total, turn

        def softmax(t):
            s3 = TS[:, t, :].rearrange("p (h k) -> p h k", h=8)
            g = sel[:, 2, t, :]
            g3 = g.rearrange("p (h k) -> p h k", h=8)
            d = D(tt(g3, s3, s3[:, :, 0:1].broadcast_to([128, 8, 16]), ALU.subtract), ck[7])
            dec["e", t] = A(act(g, g, ACT.Exp), d)

            def norm():
                d = D(lambda e: e.tensor_reduce(sm[:, t, 0:8], g3, AX.X, ALU.add), dec["e", t])
                d = D(lambda e: e.reciprocal(sm[:, t, 0:8], sm[:, t, 0:8]), d)
                dec["g", t] = D(tt(g3, g3, sm[:, t, 0:8].unsqueeze(2).broadcast_to([128, 8, 16]), ALU.mult), d)

            def turn():
                m = MB.next()
                M = MB.bufs[m]
                t1 = PE(lambda e: e.transpose(M[:, 0:128], g, ident), dec["g", t], *MB.free[m])
                a = A(act(IJG[:, 2, 128 * t:128 * t + 128], M[:, 0:128], ACT.Copy), t1)
                MB.free[m] = [a]
                dec["ijg", t, 2] = a
            return norm, turn

        def steps_b(t, half, u):
            pick, total, turn = decode_b(t, half)
            at(post, u + 1, pick)
            at(post, u + 2, total)
            at(post, u + 3, turn)

        D0 = U0 + 5
        at(mid, D0, decode_a)
        for t, half, w in ((0, 0, D0), (0, 1, D0 + 2), (1, 0, D0 + 7), (1, 1, D0 + 9)):
            at(post, w, lambda t=t, half=half, w=w: steps_b(t, half, w))

        def steps_s():
            norm0, turn0 = softmax(0)
            norm1, turn1 = softmax(1)
            at(post, D0 + 2, norm0)
            at(post, D0 + 3, turn0)
            at(post, D0 + 5, norm1)
            at(post, D0 + 6, turn1)
        at(post, D0 + 1, steps_s)

        stage = Ring([zb["stage0"], zb["stage1"]])
        oA, oB = Ring([zb["oneA0"], zb["oneA1"]]), Ring([rr["oneB0"], rr["oneB1"]])
        st_w = []
        st_count = [0, 0]

        def one_hot(c):
            need = [dec["ijg", c // 128, k] for k in range(3)]
            a, b = oA.next(), oB.next()
            OA, OB = oA.bufs[a], oB.bufs[b]
            io = iota.unsqueeze(1).broadcast_to([128, 8, 128])
            db = D(tt(OB[:, :, :], io, IJG[:, 1, c:c + 8].unsqueeze(2).broadcast_to([128, 8, 128]), ALU.is_equal),
                   *need, *oB.free[b])
            da = D(tt(OA[:, :, :], io, IJG[:, 0, c:c + 8].unsqueeze(2).broadcast_to([128, 8, 128]), ALU.is_equal),
                   *oA.free[a])
            gated = []
            for n in range(4):
                gated.append(A(act(OB[:, n, :], OB[:, n, :], ACT.Copy, scale=IJG[:, 2, c + n:c + n + 1]), db))
            p = P(tt(OB[:, 4:8, :], OB[:, 4:8, :], IJG[:, 2, c + 4:c + 8].unsqueeze(2).broadcast_to([128, 4, 128]),
                     ALU.mult), db)
            oh[c] = (a, b, da, gated + [p] * 4)

        oh = {}

        def spread(c):
            if c % 16 == 0:
                stage.next()
            s = stage.at
            S = stage.bufs[s]
            a, b, da, gated = oh[c]
            for v in range(2):
                m = MB.next()
                M = MB.bufs[m]
                for n in range(4):
                    k = 4 * v + n
                    t = PE(mm(M[:, 128 * n:128 * n + 128], oA.bufs[a][:, k, :], oB.bufs[b][:, k, :], True, True),
                           da, gated[k], *(MB.free[m] if n == 0 else []))
                w = c % 16 + 4 * v
                e = A(act(S[:, :, w:w + 4, :], M[:, :].rearrange("p (c k j) -> p k c j", c=4, k=8), ACT.Copy),
                      t, *stage.free[s])
                MB.free[m] = [e]
            oA.free[a], oB.free[b] = [t], [t]
            if c % 16 == 8:
                st_count[s] += 1
                dst = scr[:, :, 16 * (c - 8):16 * (c - 8) + 256].rearrange("k p n -> p k n")
                w = A.dma(lambda e: e.dma_start(dst, S[:, :, :, :].rearrange("p k c j -> p k (c j)")), s_st[s],
                          st_count[s], e)
                stage.free[s] = [w]
                st_w.append(w)

        G0 = U0 + 12
        for n in range(16):
            if n == 0:
                at(post, G0 - 1, lambda: (one_hot(0), one_hot(8)))
            at(mid, G0 + n, lambda n=n: spread(16 * n))
            at(post, G0 + n, lambda n=n: spread(16 * n + 8))
            if n < 15:
                at(post, G0 + n, lambda n=n: (one_hot(16 * n + 16), one_hot(16 * n + 24)))

        Gc = rr["Gc"]
        gc = {"n": 0, "free": []}

        def load_g(jc, part=None):
            c0, c1 = (0, T) if part is None else (128 * part, 128 * part + 128)
            gc["n"] += 1
            need = {0: [st_w[7], dec["sel", 1, 0]], 1: [*st_w[-2:], *oB.free[0], *oB.free[1]]}.get(part, [])
            sem = s_gc if part is None else s_gh[part]
            gc[jc, part] = SP_G.dma(lambda e: e.dma_start(Gc[:, c0:c1, :].rearrange("p c j -> p (c j)"),
                                                          scr[jc][:, 16 * c0:16 * c1]), sem, gc["n"] if part is None else 1,
                                    *need, *gc["free"])
            if part is not None:
                gc["n"] = 0

        SP_G = A
        A1 = rr["A1"]
        a_tok = {}

        def evac_u(jc, j):
            def ev(u, banks):
                i, a = low(banks[0])
                s, d = join_s(banks[0], i, a)
                b = tS.bufs[s]
                p = P(tt(b[:, :], b[:, :], R2[:, :], ALU.mult), d)
                yield
                if jc < 2:
                    yield
                    dst = (Y if jc == 0 else A1)[:, j, :]
                    old = list(key_tok.values()) if jc == 0 else [*eqs.free[1]]
                    a_tok[jc, j] = A(act(dst, b[:, :], ACT.Gelu_apprx_tanh), p, *old)
                    tS.free[s] = [a_tok[jc, j]]
                else:
                    a = A(act(b[:, :], b[:, :], ACT.Gelu_apprx_tanh), p)
                    p = P(tt(b[:, :], b[:, :], Gc[:, :, j], ALU.mult), a, gc[jc, None])
                    gc["free"] = [p]
                    yield
                    tS.free[s] = [split(ZB, ready_b, j, b[:, :], None, p, v_last[jc - 1][j // 8])]
            return ev

        def gate_a(jc, j0, part=None):
            B = Y if jc == 0 else A1
            k = slice(j0, j0 + 4)
            c = slice(0, T) if part is None else slice(128 * part, 128 * part + 128)
            p = P(tt(B[:, k, c], B[:, k, c], Gc[:, c, k].rearrange("p c j -> p j c"), ALU.mult),
                  *[a_tok[jc, j] for j in range(j0, j0 + 4)], gc[jc, part])
            if part != 0:
                for j in range(j0, j0 + 4):
                    a_tok[jc, j] = p
                gc["free"] = [p]

        def split_a(jc):
            B = Y if jc == 0 else A1
            for part in range(2):
                for n in range(4 * part, 4 * part + 4):
                    k = slice(2 * n, 2 * n + 2)
                    h = A(act(ZB[:, k, 0:256], B[:, k, :], ACT.Copy), a_tok[jc, 2 * n], a_tok[jc, 2 * n + 1],
                          *([mm_half[v_units[jc - 1] + part]] if jc else [st_w[-1], st_w[-2], PE_last[0]]))
                    d = D(tt(ZB[:, k, 256:512], B[:, k, :], ZB[:, k, 0:256].bitcast(F32), ALU.subtract), h)
                    ready_b[2 * n] = ready_b[2 * n + 1] = [h, d]
                yield

        v_units = {}
        v_last = {}
        PE_last = [None]

        def evac_v(jc, m):
            def ev(u, banks):
                i, a = low(banks[0])
                b = tA.bufs[i]
                p = P(tt(b[:, :], b[:, :], X[:, m, :], ALU.add), a)
                d = join(banks[0], i, p, X[:, m, :])
                x_tok[m] = d
                yield
                if jc == 7:
                    add_square(0, m == 0, X[:, m, :], d)
                    p = A(act(X[:, m, :], X[:, m, :], ACT.Copy, scale=C("gf", m)), d)
                    add_square(1, m == 0, X[:, m, :], p)
                    x_tok[m] = p
                    yield
                    split(ZA, ready_a, m, X[:, m, :], C("gpm", m), p, last_zA[0])
            return ev

        last_zA = [None]

        def chunk_u(jc):
            s = len(units)
            for j in range(16):
                unit2(ins["pu"], 16 * jc + j, ZA, evac_u(jc, j))
            if jc == 7:
                at(pre, len(units), lambda: last_zA.__setitem__(0, mm_half[units[s + 15][1] - 1]))
            return s

        def chunk_v(jc):
            s = len(units)
            for m in range(16):
                unit2(ins["pv"], m, ZB, evac_v(jc, m), kbase=2 * jc)
            at(pre, len(units), lambda: v_last.__setitem__(jc, [mm_half[units[s + 15][0]], mm_half[units[s + 15][0] + 1]]))
            if jc >= 1 and jc < 7:
                at(post, s + 1, lambda: load_g(jc + 1))
            return s

        chunk_u(0)
        u1 = chunk_u(1)
        at(post, G0 + 9, lambda: load_g(0, 0))
        at(post, G0 + 16, lambda: load_g(0, 1))
        for n in range(4):
            at(post, G0 + 12 + n, lambda n=n: gate_a(0, 4 * n, 0))
            at(post, G0 + 18 + n // 2, lambda n=n: gate_a(0, 4 * n, 1))
        v0 = len(units)

        def before_v(jc):
            PE_last[0] = oA.free[oA.at][0]
            if jc:
                v_units[jc - 1] = units[v0 + 16 * jc - 1][0]
            g = split_a(jc)
            next(g)
            at(pre, v0 + 16 * jc, lambda: next(g))
        at(early, v0, lambda: before_v(0))
        chunk_v(0)
        at(post, v0, lambda: load_g(1))
        for n in range(4):
            at(post, v0 + 4 + 2 * n, lambda n=n: gate_a(1, 4 * n))
        at(early, v0 + 16, lambda: before_v(1))
        chunk_v(1)
        for jc in range(2, 8):
            chunk_u(jc)
            chunk_v(jc)

        F0 = len(units)

        def norm_f():
            t = rstd(0, R3[:, :], 2048)
            rtok["RF"] = t
            m, t2 = mean_of(acc[1][:, :], acc_tok[1])
            acc_free[1] = [t2]
            j = tS.next()
            b = tS.bufs[j]
            p = P(tt(b[:, :], R3[:, :], R3[:, :], ALU.mult), t, *tS.free[j])
            d = D(tt(b[:, :], MB.bufs[m][:, 0:256], b[:, :], ALU.mult), p, t2)
            MB.free[m] = [d]
            a = A(act(b[:, :], b[:, :], ACT.Sqrt, scale=1.0 / 2048, bias=C("eps")), d)
            d = D(lambda e: e.reciprocal(b[:, :], b[:, :]), a)
            rtok["RC"] = P(tt(R2[:, :], b[:, :], R3[:, :], ALU.mult), d)
            tS.free[j] = [rtok["RC"]]
        at(post, F0 + 2, norm_f)
        hold[F0] = F0 + 3

        def scale_x(m):
            x_tok[m] = P(tt(X[:, m, :], X[:, m, :], R3[:, :], ALU.mult), x_tok[m], *ready_a[m])
        for m in range(16):
            at(post, F0 + 4 + m, lambda m=m: scale_x(m))

        qkv, VT, O, CV = zb["qkv"], zb["VT"], ry["O"], ry["CV"]
        zsr, spr = Ring([zb["zs0"], zb["zs1"]]), Ring([zb["sp0"], zb["sp1"]])
        UC = Ring([rr[f"UC{i}"] for i in range(5)])
        zb_dead = {}

        def open_f():
            last = mm_half[units[F0 - 1][1] - 1]
            zb_dead[0] = last
            zb_dead["mask"] = A.dma(lambda e: e.dma_start(zb["mask"][:, :], ins["con"][:, CEND:CEND + 384]),
                                    s_in["mask"], 1, last)
            zb_dead["mask"] = A.dma(lambda e: e.dma_start(zb["neg"][:, :], ins["con"][:, CEND + 384:CEND + 768]),
                                    s_in["mask"], 2, last)
            for i in range(5):
                ucpad.append(P(lambda e, i=i: e.memset(rr[f"UC{i}"][:, 0:30], 0.0), gc["free"][0]))
        ucpad = []
        at(pre, F0, open_f)

        sgl = {}
        conv_q = []
        conv_tok = {}

        def evac_glu_b(j):
            def ev(u, banks):
                i, a = low(banks[0])
                s, d = join_s(banks[0], i, a)
                b = tS.bufs[s]
                p = P(tt(b[:, :], b[:, :], R2[:, :], ALU.mult), d, rtok["RC"])
                yield
                yield
                q = sg.next()
                sgl[j] = (q, A(act(sg.bufs[q][:, :], b[:, :], ACT.Sigmoid, bias=C("b_in", 32 + j)), p, *sg.free[q]))
                tS.free[s] = [sgl[j][1]]
            return ev
        sg = Ring([acc[0], acc[1]])

        def evac_glu_a(j):
            def ev(u, banks):
                i, a = low(banks[0])
                s, d = join_s(banks[0], i, a)
                b = tS.bufs[s]
                p = P(tt(b[:, :], b[:, :], R2[:, :], ALU.mult), d, rtok["RC"])
                yield
                c = UC.next()
                q, st = sgl[j]
                d = D(stt(UC.bufs[c][:, 30:286], b[:, :], C("b_in", 24 + j), sg.bufs[q][:, :], ALU.add, ALU.mult), p, st,
                      ucpad[c], *UC.free[c])
                tS.free[s] = [d]
                sg.free[q] = [d]
                for k in range(TAPS):
                    conv_q.append((j, k, c, d))
            return ev

        def conv_step(n):
            for _ in range(min(n, len(conv_q))):
                j, k, c, d = conv_q.pop(0)
                b = UC.bufs[c]
                w = C("w_dw", 8 * k + j)
                if k == 0:
                    t = D(ts(CV[:, j, :], b[:, 0:256], w, ALU.mult, C("b_dw", j), ALU.add), d)
                else:
                    t = D(stt(CV[:, j, :], b[:, k:k + 256], w, CV[:, j, :], ALU.mult, ALU.add), conv_tok[j])
                conv_tok[j] = t
                if k == TAPS - 1:
                    UC.free[c] = [t]

        qkv_free = [[] for _ in range(4)]
        vt_free = [[] for _ in range(4)]
        qkv_tok = {}

        def evac_qkv(h, w):
            def ev(u, banks):
                i, a = low(banks[0])
                s, d = join_s(banks[0], i, a)
                b = tS.bufs[s]
                p = P(tt(b[:, :], b[:, :], R2[:, :], ALU.mult), d, rtok["RC"])
                yield
                yield
                a = A(act(qkv[:, h % 4, w, :], b[:, :], ACT.Identity, bias=C("b_in", 8 * w + h)), p,
                      zb_dead[0], *qkv_free[h % 4])
                tS.free[s] = [a]
                qkv_tok[h, w] = a
                if w == 2 and h % 2:
                    g = attention(h - 1)
                    for n in range(4):
                        at(post, u + 1 + n, lambda: next(g, None))
            return ev

        av_last = [None]

        def attention(h0):
            mV = MB.next()
            tv = PE(many(*[(lambda e, h=h, b=b: e.transpose(MB.bufs[mV][:, 256 * (h - h0) + 128 * b:256 * (h - h0) + 128 * b + 128],
                                                           qkv[:, h % 4, 2, 128 * b:128 * b + 128], ident))
                           for h in (h0, h0 + 1) for b in range(2)]), qkv_tok[h0 + 1, 2], *MB.free[mV])
            av = D(lambda e: e.tensor_copy(VT[:, h0 % 4:h0 % 4 + 2, :].rearrange("p h n -> p (h n)"), MB.bufs[mV][:, :]),
                   tv, *vt_free[h0 % 4])
            MB.free[mV] = [av]
            z = zsr.next()
            s = spr.next()
            ZS, SPb = zsr.bufs[z], spr.bufs[s]
            for h in (h0, h0 + 1):
                m = MB.next()
                M = MB.bufs[m]
                q, k = qkv[:, h % 4, 0, :], qkv[:, h % 4, 1, :]
                t = PE(many(mm(M[:, 0:256], k[:, 0:128], q, True, True),
                            mm(M[:, 256:384], k[:, 128:256], q[:, 128:256], True, True)),
                       qkv_tok[h, 1], *MB.free[m])
                zt = A(act(ZS[:, h - h0, :], M[:, 0:384], ACT.Copy, scale=128 ** -0.5), t, *zsr.free[z])
                MB.free[m] = [zt]
            qkv_free[h0 % 4] = qkv_free[h0 % 4 + 1] = [t, tv]
            yield
            a = A(act(SPb[:, :, :], ZS[:, :, :], ACT.Abs), zt, *spr.free[s])
            a = A(act(SPb[:, :, :], SPb[:, :, :], ACT.Exp, scale=-1.0), a)
            a = A(act(SPb[:, :, :], SPb[:, :, :], ACT.Ln, bias=1.0), a)
            d = D(stt(SPb[:, :, :], ZS[:, :, :], 0.0, SPb[:, :, :], ALU.max, ALU.add), a)
            p = P(tt(SPb[:, :, :], SPb[:, :, :], zb["mask"][:, :].unsqueeze(1).broadcast_to([128, 2, 384]), ALU.mult),
                  d, zb_dead["mask"])
            yield
            for h in (h0, h0 + 1):
                n = h - h0
                m = MB.next()
                M = MB.bufs[m]
                t = PE(many(mm(M[:, 0:256], tri, SPb[:, n, 0:256], True, False),
                            mm(M[:, 128:256], ones, SPb[:, n, 256:384], False, True),
                            mm(M[:, 256:384], tri, SPb[:, n, 256:384], True, True)), p, *MB.free[m])
                d = D(tt(ZS[:, n, :], ZS[:, n, :], M[:, 0:384], ALU.subtract), t)
                MB.free[m] = [d]
            spr.free[s] = [t]
            p = P(tt(ZS[:, :, :], ZS[:, :, :], zb["neg"][:, :].unsqueeze(1).broadcast_to([128, 2, 384]), ALU.add), d)
            a = A(act(ZS[:, :, :], ZS[:, :, :], ACT.Exp), p)
            yield
            m = MB.next()
            M = MB.bufs[m]
            fns = []
            for h in (h0, h0 + 1):
                n = h - h0
                fns += [mm(M[:, 256 * n:256 * n + 256], VT[:, h % 4, 0:128], ZS[:, n, 0:256], True, False),
                        mm(M[:, 256 * n + 128:256 * n + 256], VT[:, h % 4, 128:256], ZS[:, n, 256:384], False, True)]
            t = PE(many(*fns), a, av, *MB.free[m])
            zsr.free[z] = [t]
            vt_free[h0 % 4] = [t]
            d = A(act(O[:, h0:h0 + 2, :].rearrange("p h t -> p (h t)"), M[:, :], ACT.Copy), t, *y_dead)
            MB.free[m] = [d]
            av_last[0] = t
            o_tok[h0] = o_tok[h0 + 1] = d

        o_tok = {}
        y_dead = []

        def evac_sig(dst, n, bcol):
            def ev(u, banks):
                i, a = low(banks[0])
                s, d = join_s(banks[0], i, a)
                b = tS.bufs[s]
                p = P(tt(b[:, :], b[:, :], R2[:, :], ALU.mult), d)
                yield
                yield
                a = A(act(dst[:, n, :], b[:, :], ACT.Sigmoid, bias=C("b_in", bcol)), p)
                tS.free[s] = [a]
                sg2[dst.name, n] = a
            return ev
        sg2 = {}

        for j in range(8):
            unit2(ins["w_in2"], 32 + j, ZA, evac_glu_b(j))
            unit2(ins["w_in2"], 24 + j, ZA, evac_glu_a(j))
            for w in range(3):
                unit2(ins["w_in2"], 8 * w + j, ZA, evac_qkv(j, w))
        FG = len(units)
        for n in range(16):
            unit2(ins["w_in2"], 40 + n, ZA, evac_sig(rr["SGS"], n, 40 + n))
            unit2(ins["w_in2"], 56 + n, ZA, evac_sig(rr["SGC"], n, 56 + n))
        for s in range(F0 + 2, FG + 14):
            at(post, s, lambda: conv_step(5))
        at(post, FG + 14, lambda: conv_step(1000))

        ln = {}
        SQ8 = None

        def ln_sum():
            ln["s"] = D(lambda e: e.tensor_reduce(Rn[0][:, :], CV[:, :, :].rearrange("p k t -> p t k"), AX.X, ALU.add),
                        *conv_tok.values())

        def ln_mean():
            m, t = mean_of(Rn[0][:, :], ln["s"])
            ln["mu"] = D(ts(Rn[0][:, :], MB.bufs[m][:, 0:256], 1.0 / 1024, ALU.mult), t)
            MB.free[m] = [ln["mu"]]

        def ln_sub():
            ln["c"] = D(tt(CV[:, :, :], CV[:, :, :], Rn[0][:, :].unsqueeze(1).broadcast_to([128, 8, T]), ALU.subtract),
                        ln["mu"])

        def ln_square():
            ln["q"] = A(act(O[:, :, :], CV[:, :, :], ACT.Square), ln["c"], *[t for k in range(8) for t in ready_b[k]])

        def ln_sum2():
            acc_tok[0] = D(lambda e: e.tensor_reduce(acc[0][:, :], O[:, :, :].rearrange("p k t -> p t k"), AX.X, ALU.add),
                           ln["q"], *acc_free[0])

        def ln_rstd():
            ln["r"] = rstd(0, Rn[0][:, :], 1024, ln["c"])

        def ln_mul():
            ln["x"] = D(tt(CV[:, :, :], CV[:, :, :], Rn[0][:, :].unsqueeze(1).broadcast_to([128, 8, T]), ALU.mult), ln["r"])

        def ln_silu(j0):
            for j in range(j0, j0 + 4):
                a = A(act(CV[:, j, :], CV[:, j, :], ACT.Silu, scale=C("gcl", j), bias=C("bcl", j)), ln["x"])
                split(ZB, ready_b, 8 + j, CV[:, j, :], None, a, av_last[0])

        def o_split(j0):
            for j in range(j0, j0 + 4):
                split(ZB, ready_b, j, O[:, j, :], None, o_tok[j], av_last[0], o_tok[7])
        at(pre, FG, lambda: acc_free[0].extend(sg.free[0]) or acc_free[1].extend(sg.free[1]))
        at(post, FG + 15, ln_sum)
        at(post, FG + 16, ln_mean)
        at(post, FG + 17, ln_sub)
        at(post, FG + 18, ln_square)
        at(post, FG + 19, ln_sum2)
        at(post, FG + 20, ln_rstd)
        at(post, FG + 21, ln_mul)
        at(post, FG + 23, lambda: ln_silu(0))
        at(post, FG + 24, lambda: ln_silu(4))
        at(post, FG + 10, lambda: o_split(0))
        at(post, FG + 11, lambda: o_split(4))

        H0 = len(units)

        merged = []

        def evac_merge(m):
            def ev(u, banks):
                s1, s2 = rr["SGS"], rr["SGC"]
                i, a = low(banks[0])
                s, d = join_s(banks[0], i, a)
                b = tS.bufs[s]
                p = P(tt(b[:, :], b[:, :], s1[:, m, :], ALU.mult), d, sg2["SGS", m])
                i, a = low(banks[1])
                r, d = join_s(banks[1], i, a)
                c = tS.bufs[r]
                yield
                p2 = P(tt(c[:, :], c[:, :], s2[:, m, :], ALU.mult), d, sg2["SGC", m])
                p = P(tt(b[:, :], b[:, :], c[:, :], ALU.add), p, p2)
                tS.free[r] = [p]
                merged[:] = [p]
                yield
                tS.free[s] = [split(ZA, ready_a, m, b[:, :], None, p, mm_half[units[H0 - 1][1] - 1])]
            return ev

        for m in range(16):
            unit([(ins["w_sc"][m, 0], ZB, 0, list(range(8)), 0, True, True),
                  (ins["w_sc"][m, 1], ZB, 1, list(range(8)), 1, True, True)], evac_merge(m))
        W0 = len(units)
        y_tok = {}

        def evac_wo(m):
            def ev(u, banks):
                if m == 15:
                    advance()
                    ahead[0] += 1
                i, a = low(banks[0])
                d = join(banks[0], i, a, Y[:, m, :], *ready_b[0], *ready_b[7], *ready_b[15])
                y_tok[m] = d
                if m == 15:
                    q = tQ.next()
                    a = A(act(tQ.bufs[q][:, :], Y[:, m, :], ACT.Square), d, *tQ.free[q])
                    u2 = A(act(rr["U2"][:, m, :], Y[:, m, :], ACT.Copy, scale=gpp[:, m:m + 1]), d, gpp_tok)
                    u_tok[m].append(u2)
                    rtok["q"] = rms(0, R2[:, :], 2048, ln["x"], also=(q, a))
                    post_mix()
                else:
                    add_square(0, m == 0, Y[:, m, :], d)
                yield
                if m != 15:
                    u2 = A(act(rr["U2"][:, m, :], Y[:, m, :], ACT.Copy, scale=gpp[:, m:m + 1]), d, gpp_tok)
                if m != 15:
                    make_u1(m)
                    u_tok[m].append(u2)
                if m == 14:
                    make_u1(15)
                y_tok[m] = A(act(Y[:, m, :], Y[:, m, :], ACT.Copy, scale=C("gpost", m)), d)
            return ev
        u_tok = {}

        def make_u1(m):
            u_tok[m] = [A(act(rr["U1"][:, m, :], X[:, m, :], ACT.Copy, scale=C("gpmlp", m)), x_tok[m], *merged)]

        gpp_tok = D(tt(gpp[:, :], col[:, COL0["gpost"]:COL0["gpost"] + 16], col[:, COL0["gpmlp"]:COL0["gpmlp"] + 16],
                       ALU.mult), ld["col"])
        for m in range(16):
            unit2(ins["w_o"], m, ZA, evac_wo(m))
        M0 = len(units)

        def post_mix():
            last = mm_half[units[M0 - 1][1] - 1]
            U1, U2 = rr["U1"], rr["U2"]
            q = rtok["q"]

            def lows(k, h):
                d = D(tt(ZA[:, k, 256:512], U2[:, k, :], ZA[:, k, 0:256].bitcast(F32), ALU.subtract), h)
                for i in range(k.start, k.stop):
                    ready_a[i] = [h, d]
            before = None
            for n, (a, b) in enumerate(((0, 1), (1, 2), (2, 4), (4, 6), (6, 8), (8, 10), (10, 12), (12, 14), (14, 16))):
                k = slice(a, b)
                E = P if n in (2, 4, 6, 8) else D
                d = E(tt(U1[:, k, :], U1[:, k, :], R2[:, :].unsqueeze(1).broadcast_to([128, b - a, T]), ALU.mult), q,
                      *[t for i in range(a, b) for t in u_tok[i]])
                t = E(tt(U2[:, k, :], U2[:, k, :], U1[:, k, :], ALU.add), d)
                h = A(act(ZA[:, k, 0:256], U2[:, k, :], ACT.Copy), t, last)
                if before:
                    lows(*before)
                before = (k, h)
                if n == 6:
                    advance()
                    ahead[0] += 1
            lows(*before)

        def warm_sqrt():
            A(act(warm[:, :], gpp[:, 0:1], ACT.Sqrt, scale=0.0), gpp_tok)
        at(post, M0 - 3, warm_sqrt)
        at(post, M0 + 125, warm_sqrt)

        def residual_scale():
            rtok["R1"] = D(lambda e: e.reciprocal(R1[:, :], R2[:, :]), rtok["q"])

        def residual(ns):
            for n in ns:
                k = slice(4 * n, 4 * n + 4)
                d = D(tt(Y[:, k, :], Y[:, k, :], R1[:, :].unsqueeze(1).broadcast_to([128, 4, T]), ALU.mult), rtok["R1"],
                      y_tok[4 * n + 3])
                p = (D if n == 3 else P)(tt(X[:, k, :], X[:, k, :], Y[:, k, :], ALU.add), d, *u_tok[4 * n + 3],
                                         x_tok[4 * n + 3])
                for m in range(4 * n, 4 * n + 4):
                    x_tok[m] = p

        def residual_squares():
            for n in range(4):
                k = slice(4 * n, 4 * n + 4)
                y_tok[0] = A(act(Y[:, k, :], X[:, k, :], ACT.Square), x_tok[4 * n])

        def residual_sum():
            acc_tok[0] = D(lambda e: e.tensor_reduce(acc[0][:, :], Y[:, :, :].rearrange("p k t -> p t k"), AX.X, ALU.add),
                           y_tok[0], *acc_free[0])
            for m in range(16):
                y_tok[m] = acc_tok[0]

        def residual_norm():
            m, t = mean_of(acc[0][:, :], acc_tok[0])
            acc_free[0] = [t]
            v2 = D(ts(R3[:, :], MB.bufs[m][:, 0:256], 1.0 / 2048, ALU.mult, C("eps"), ALU.add), t)
            MB.free[m] = [v2]
            d = D(tt(R2[:, :], R2[:, :], R2[:, :], ALU.mult), rtok["R1"])
            d = D(tt(R3[:, :], R3[:, :], R2[:, :], ALU.mult), v2, d)
            rtok["R3"] = D(stt(R3[:, :], R3[:, :], C("eps16"), R3[:, :], ALU.mult, ALU.mult), d)
        at(post, M0 + 2, residual_scale)
        for n in range(4):
            at(post, M0 + 3 + n, lambda n=n: residual([n]))
        at(post, M0 + 8, residual_squares)
        at(post, M0 + 9, residual_sum)
        at(post, M0 + 10, residual_norm)

        def evac_up(c, j):
            def ev(u, banks):
                i, a = low(banks[0])
                s, d = join_s(banks[0], i, a)
                b = tS.bufs[s]
                yield
                d = D(stt(b[:, :], b[:, :], 0.0, b[:, :], ALU.max, ALU.mult), d)
                yield
                before = [d_last[c - 1]] if c else [mm_half[units[W0 - 1][1] - 1]]
                tS.free[s] = [split(ZB, ready_b, j, b[:, :], None, d, *before)]
            return ev

        d_last = {}

        def evac_down(c, m):
            def ev(u, banks):
                i, a = low(banks[0])
                b = tA.bufs[i]
                if c:
                    a = P(tt(b[:, :], b[:, :], Y[:, m, :], ALU.add), a, y_tok[m])
                d = join(banks[0], i, a, Y[:, m, :], y_tok[m])
                y_tok[m] = d
                yield
                if c == 3:
                    if m == 0:
                        acc_tok[0] = P(lambda e: e.tensor_copy(acc[0][:, :], R3[:, :]), rtok["R3"], *acc_free[0])
                    if m == 15:
                        q = tQ.next()
                        a = A(act(tQ.bufs[q][:, :], Y[:, m, :], ACT.Square), d, *tQ.free[q])
                    else:
                        add_square(0, False, Y[:, m, :], d)
                    y_tok[m] = A(act(Y[:, m, :], Y[:, m, :], ACT.Copy, scale=C("gpostmlp", m)), d)
                    if m == 15:
                        rtok["R1"] = rstd(0, R1[:, :], 2048, also=(q, a))
            return ev

        for c in range(4):
            for j in range(16):
                unit2(ins["w_up"], 16 * c + j, ZA, evac_up(c, j))
            s = len(units)
            for m in range(16):
                unit2(ins["w_down"], m, ZB, evac_down(c, m), kbase=2 * c)
            at(pre, len(units), lambda c=c, s=s: d_last.__setitem__(c, mm_half[units[s + 15][1] - 1]))

        def finish():
            r = rtok["R1"]
            for n in range(8):
                k = slice(2 * n, 2 * n + 2)
                E1, E2 = (P if n in (1, 4) else D), (P if n in (1, 4, 6) else D)
                d = E1(tt(Y[:, k, :], Y[:, k, :], R1[:, :].unsqueeze(1).broadcast_to([128, 2, T]), ALU.mult), r,
                       y_tok[2 * n], y_tok[2 * n + 1])
                t = E2(tt(X[:, k, :], X[:, k, :], Y[:, k, :], ALU.add), d, x_tok[2 * n + 1])
                o = SP.dma(lambda e, k=k: e.dma_start(out[:, k, :], X[:, k, :]), s_out, n + 1, t)
            SP.wait(o)

        def prelude():
            start_x()
            ini['sq'] = sq_tok[-1]

        def softplus():
            lam = col[:, COL0["lam"]:COL0["lam"] + 8]
            t = A(act(sp4[:, 0, :], lam, ACT.Abs), ld["col"])
            t = A(act(sp4[:, 0, :], sp4[:, 0, :], ACT.Exp, scale=-1.0), t)
            t = A(act(sp4[:, 0, :], sp4[:, 0, :], ACT.Ln, bias=1.0), t)
            t2 = D(ts(sp4[:, 1, :], lam, -1.0, ALU.mult, 0.0, ALU.max), ld["col"])
            t = D(tt(sp4[:, 1, :], sp4[:, 1, :], sp4[:, 0, :], ALU.add), t, t2)
            t = D(ts(sp4[:, 2, :], sp4[:, 1, :], 4.0, ALU.mult), t)
            ini['sp'] = D(ts(sp4[:, 1, :], sp4[:, 1, :], -8.0, ALU.mult), t)

        PAIRS = (v0, M0)
        prelude()
        at(post, 5, softplus)
        N = len(units)
        waiting = []
        for u in range(N + 1):
            for fn in early.get(u, []):
                fn()
            if u:
                waiting.append((u - 1, banks))
            evs = []
            while waiting and hold.get(waiting[0][0], 0) <= u:
                w, b = waiting.pop(0)
                evs.append(units[w][2](u, b))
            if len(evs) > 1:
                step()
            for n, ev in enumerate(evs[:-1]):
                for _ in ev:
                    pass
                if n == 0:
                    step()
            ev = evs[-1] if evs else iter(())
            next(ev, None)
            if len(evs) <= 1:
                step()
                next(ev, None)
                step()
            else:
                next(ev, None)
            next(ev, None)
            for fn in pre.get(u, []):
                fn()
            if u < N:
                banks = products(u)
                for fn in post.get(u, []):
                    fn()
        finish()

        block = ctx.enter_context(nc.Block())

        @block.sync
        def _(e):
            SP.run(e)

        @block.scalar
        def _(e):
            A.run(e)

        @block.vector
        def _(e):
            D.run(e)

        @block.gpsimd
        def _(e):
            P.run(e)

        @block.tensor
        def _(e):
            PE.run(e)


def _gemm(w):
    K, N = w.shape
    return w.reshape(K // 1024, 8, 128, N // 128, 128).transpose(3, 0, 2, 1, 4).reshape(N // 128, K // 1024, 128, 1024)


def _constants(np):
    f = np.float32
    c = np.zeros((128, CEND + 768), f)
    i = np.arange(128)
    c[:, CI:CI + 128] = np.eye(128, dtype=f)
    c[:, CTRI:CTRI + 128] = (i[:, None] >= i[None, :]).astype(f)
    c[:, CONE:CONE + 128] = 1.0
    c[:, CIOTA:CIOTA + 128] = i[None, :]
    for g, w in enumerate((2, 4, 8, 16)):
        c[:, CRC + 16 * g:CRC + 16 * g + 16] = 1.0 / np.minimum(np.arange(1, 17), w).astype(f)
    before = (i[:, None] < i[None, :]).astype(f)
    mask = np.concatenate([before, np.ones((128, 128), f), before], axis=1)
    c[:, CEND:CEND + 384] = mask
    c[:, CEND + 384:CEND + 768] = np.where(mask > 0, f(0), f(-1.0e38))
    return c


def kernel(**inputs):
    import numpy as np
    import concourse.bacc as _bacc
    from concourse.bass_utils import run_bass_kernel_spmd as _run

    v = {k: np.asarray(x) for k, x in inputs.items()}

    def cols(a):
        return a.reshape(-1, 128).T

    named = {"g1": v["norm1_g"], "pool_b": v["pool_b"], "pool_scale": v["pool_scale"], "conv_w": v["conv_w"],
             "conv_b": v["conv_b"], "gab": v["gate_a_b"], "gxb": v["gate_x_b"], "lam": v["lru_lambda"],
             "g2": v["norm2_g"], "gf": v["norm_f_g"], "gpm": v["g_pre_mix_2"], "b_in": v["b_in_2"],
             "w_dw": v["w_dw_2"], "b_dw": v["b_dw_2"], "gcl": v["g_conv_ln_2"], "bcl": v["b_conv_ln_2"],
             "gpost": v["g_post_mix_2"], "gpmlp": v["g_pre_mlp_2"], "gpostmlp": v["g_post_mlp_2"]}
    packed = [cols(named[n]) for n, _ in COLS[:-2]] + [np.full((128, 1), 1e-6, np.float32), np.full((128, 1), 16e-6, np.float32)]
    keys = np.stack([v["peer_keys1"][0], v["peer_keys2"][0]], axis=1)
    arrays = {
        "xT": v["x"][0].reshape(256, 16, 128).transpose(2, 1, 0),
        "con": _constants(np),
        "cols": np.concatenate(packed, axis=1),
        "gaw": v["gate_a_w"][0].transpose(1, 0, 2),
        "gxw": v["gate_x_w"][0].transpose(1, 0, 2),
        "poolw": v["pool_w"][0].reshape(4, 2, 128, 256).transpose(2, 0, 1, 3),
        "keys": keys.reshape(16, 128, 128).transpose(2, 0, 1),
        "w_in": _gemm(v["w_in"][0]),
        "w_out": _gemm(v["w_out"][0]),
        "wq": _gemm(v["peer_wq"][0]),
        "pu": v["peer_u"][0].reshape(128, 128, 2, 8, 128).transpose(1, 2, 4, 3, 0).reshape(128, 2, 128, 1024),
        "pv": v["peer_v"][0].reshape(128, 16, 8, 16, 128).transpose(3, 1, 0, 2, 4).reshape(16, 16, 128, 1024),
        "w_in2": _gemm(v["w_in_2"][0]),
        "w_sc": np.stack([_gemm(v["w_sb_out_2"][0])[:, 0], _gemm(v["w_conv_out_2"][0])[:, 0]], axis=1),
        "w_o": _gemm(v["w_o_2"][0]),
        "w_up": _gemm(v["w_up_2"][0]),
        "w_down": _gemm(v["w_down_2"][0]),
    }
    nc = _bacc.Bacc("TRN2", target_bir_lowering=False, num_devices=1)
    given, aps = {}, {}
    for name, a in arrays.items():
        a = np.ascontiguousarray(a)
        given[f"in_{name}"] = a
        aps[name] = nc.dram_tensor(f"in_{name}", a.shape, mybir.dt.from_np(a.dtype), kind="ExternalInput").ap()
    out = nc.dram_tensor("out_0", (128, 16, 256), F32, kind="ExternalOutput").ap()
    build(nc, aps, out)
    r = _run(nc, [given], core_ids=[0])
    got = np.asarray(r.results[0]["out_0"])
    return np.ascontiguousarray(got.transpose(2, 1, 0).reshape(1, 256, 2048))
```
